# Optimizing a Trainium2 kernel written in Bass

```python
import jax, jax.numpy as jnp
from jax import lax
import numpy as np

D_MODEL = 1024
BATCH = 1
SEQ = 512
DEPTH = 2

GRID_W = 64
CTX_LEN = 256
EPS = 1e-6
ROPE_BASE = 10000.0
CHUNK = 64

GLA_HEADS = 4
GLA_DK = D_MODEL // 16
GLA_DV = D_MODEL // 8
GLA_RANK = 16
GLA_TAU = 16.0

MLSTM_HEADS = 4
MLSTM_DH = D_MODEL // 8

MIX_WIDTH = GLA_HEADS * GLA_DV + MLSTM_HEADS * MLSTM_DH
EVEN_SIZES = (GLA_HEADS * GLA_DK, GLA_HEADS * GLA_DK, GLA_HEADS * GLA_DV, GLA_HEADS * GLA_DV, 2 * GLA_RANK,
              MLSTM_HEADS * MLSTM_DH, MLSTM_HEADS * MLSTM_DH, MLSTM_HEADS * MLSTM_DH, MLSTM_HEADS * MLSTM_DH,
              4 * MLSTM_HEADS)
EVEN_IN = sum(EVEN_SIZES)

NA_HEADS = 16
NA_DH = D_MODEL // NA_HEADS
NA_WIN_H = 8
NA_WIN_W = 16

D_FF = ((8 * D_MODEL // 3 + 255) // 256) * 256
FFN_CONV = 3

kernel_name = 'hybrid_gla_mlstm_natten_convffn_dit'

def rms_norm(x, w):
    xf = x.astype(jnp.float32)
    y = xf * lax.rsqrt(jnp.mean(xf * xf, axis=-1, keepdims=True) + EPS)
    return (y * w.astype(jnp.float32)).astype(x.dtype)

def head_rms_norm(h, w):
    return h * lax.rsqrt(jnp.mean(h * h, axis=-1, keepdims=True) + EPS) * w.astype(jnp.float32)

def axial_rope(n_tokens, head_dim):
    pos = jnp.arange(n_tokens, dtype=jnp.int32)
    row = (pos // GRID_W).astype(jnp.float32)
    col = (pos % GRID_W).astype(jnp.float32)
    n_freq = head_dim // 4
    inv_freq = ROPE_BASE ** (-jnp.arange(n_freq, dtype=jnp.float32) / n_freq)
    ang = jnp.concatenate([row[:, None] * inv_freq, col[:, None] * inv_freq], axis=-1)
    return jnp.cos(ang), jnp.sin(ang)

def apply_rope(x, cos, sin):
    half = x.shape[-1] // 2
    x1, x2 = x[..., :half], x[..., half:]
    c = cos[None, :, None, :]
    s = sin[None, :, None, :]
    return jnp.concatenate([x1 * c - x2 * s, x1 * s + x2 * c], axis=-1)

def gla_chunked(q, k, v, log_a, state0):
    B, H, T, dk = q.shape
    dv = v.shape[-1]
    nc = T // CHUNK
    q = q.reshape(B, H, nc, CHUNK, dk)
    k = k.reshape(B, H, nc, CHUNK, dk)
    v = v.reshape(B, H, nc, CHUNK, dv)
    b = jnp.cumsum(log_a.reshape(B, H, nc, CHUNK, dk), axis=3)
    g = b[:, :, :, -1]
    q_dec = q * jnp.exp(b)
    k_dec = k * jnp.exp(-b)
    k_end = k * jnp.exp(g[:, :, :, None, :] - b)
    causal = jnp.tril(jnp.ones((CHUNK, CHUNK), dtype=bool))
    scores = jnp.where(causal, jnp.einsum('bhnid,bhnjd->bhnij', q_dec, k_dec), 0.0)
    o_intra = jnp.einsum('bhnij,bhnjv->bhniv', scores, v)
    kv = jnp.einsum('bhnjd,bhnjv->bhndv', k_end, v)

    def step(s, inp):
        g_n, kv_n = inp
        return jnp.exp(g_n)[..., None] * s + kv_n, s

    s_final, s_start = lax.scan(step, state0, (jnp.moveaxis(g, 2, 0), jnp.moveaxis(kv, 2, 0)))
    o_inter = jnp.einsum('bhnid,nbhdv->bhniv', q_dec, s_start)
    return (o_intra + o_inter).reshape(B, H, T, dv), s_final

def mlstm_chunked(q, k, v, log_i, log_f, state0):
    B, H, T, dh = q.shape
    nc = T // CHUNK
    q = q.reshape(B, H, nc, CHUNK, dh)
    k = k.reshape(B, H, nc, CHUNK, dh)
    v = v.reshape(B, H, nc, CHUNK, dh)
    log_i = log_i.reshape(B, H, nc, CHUNK)
    b = jnp.cumsum(log_f.reshape(B, H, nc, CHUNK), axis=-1)
    g = b[..., -1]
    causal = jnp.tril(jnp.ones((CHUNK, CHUNK), dtype=bool))
    log_d = jnp.where(causal, b[..., :, None] - b[..., None, :] + log_i[..., None, :], -jnp.inf)
    log_w_end = g[..., None] - b + log_i
    m_loc = jnp.max(log_w_end, axis=-1)
    w_end = jnp.exp(log_w_end - m_loc[..., None])
    c_loc = jnp.einsum('bhns,bhnsd,bhnse->bhnde', w_end, k, v)
    n_loc = jnp.einsum('bhns,bhnsd->bhnd', w_end, k)

    def step(carry, inp):
        c_st, n_st, m_st = carry
        g_n, m_loc_n, c_loc_n, n_loc_n = inp
        m_new = jnp.maximum(g_n + m_st, m_loc_n)
        a = jnp.exp(g_n + m_st - m_new)
        w = jnp.exp(m_loc_n - m_new)
        c_new = a[..., None, None] * c_st + w[..., None, None] * c_loc_n
        n_new = a[..., None] * n_st + w[..., None] * n_loc_n
        return (c_new, n_new, m_new), (c_st, n_st, m_st)

    mv = lambda t: jnp.moveaxis(t, 2, 0)
    final, (c_s, n_s, m_s) = lax.scan(step, state0, (mv(g), mv(m_loc), mv(c_loc), mv(n_loc)))
    log_inter = b + jnp.moveaxis(m_s, 0, 2)[..., None]
    m_t = jnp.maximum(log_inter, jnp.max(log_d, axis=-1))
    d_w = jnp.exp(log_d - m_t[..., None])
    inter_w = jnp.exp(log_inter - m_t)
    s = jnp.einsum('bhntd,bhnsd->bhnts', q, k) * d_w
    numer = jnp.einsum('bhnts,bhnse->bhnte', s, v) + inter_w[..., None] * jnp.einsum('bhntd,nbhde->bhnte', q, c_s)
    denom = jnp.sum(s, axis=-1) + inter_w * jnp.einsum('bhntd,nbhd->bhnt', q, n_s)
    h = numer / jnp.maximum(jnp.abs(denom), jnp.exp(-m_t))[..., None]
    return h.reshape(B, H, T, dh), final

def even_project(u, w_in, a_up, a_bias, ml_gate_bias, rope_gla, rope_ml):
    B, T, _ = u.shape
    z = (u @ w_in).astype(jnp.float32)
    splits = np.cumsum(EVEN_SIZES)[:-1].tolist()
    gq, gk, gv, gg, ga, mq, mk, mv, mo, mg = jnp.split(z, splits, axis=-1)
    gq = gq.reshape(B, T, GLA_HEADS, GLA_DK)
    gk = gk.reshape(B, T, GLA_HEADS, GLA_DK)
    mq = mq.reshape(B, T, MLSTM_HEADS, MLSTM_DH)
    mk = mk.reshape(B, T, MLSTM_HEADS, MLSTM_DH)
    if rope_gla is not None:
        gq, gk = apply_rope(gq, *rope_gla), apply_rope(gk, *rope_gla)
        mq, mk = apply_rope(mq, *rope_ml), apply_rope(mk, *rope_ml)
    bhtd = lambda t: t.transpose(0, 2, 1, 3)
    a_pre = jnp.einsum('btzr,zre->zbte', ga.reshape(B, T, 2, GLA_RANK), a_up) + a_bias[:, None, None, :]
    log_a = (jax.nn.log_sigmoid(a_pre) / GLA_TAU).reshape(2, B, T, GLA_HEADS, GLA_DK).transpose(0, 1, 3, 2, 4)
    mg = (mg.reshape(B, T, 2, 2, MLSTM_HEADS) + ml_gate_bias).transpose(2, 3, 0, 4, 1)
    return dict(
        gq=bhtd(gq) * GLA_DK ** -0.5, gk=bhtd(gk), gv=bhtd(gv.reshape(B, T, GLA_HEADS, GLA_DV)), la=log_a, gg=gg,
        mq=bhtd(mq), mk=bhtd(mk) * MLSTM_DH ** -0.5, mv=bhtd(mv.reshape(B, T, MLSTM_HEADS, MLSTM_DH)),
        li=mg[:, 0], lf=jax.nn.log_sigmoid(mg[:, 1]), mo=mo)

def flip_t(t):
    return jnp.flip(t, axis=2)

def gla_bidir(p, init):
    o_f, s_f = gla_chunked(p['gq'], p['gk'], p['gv'], p['la'][0], init[0])
    o_b, s_b = gla_chunked(flip_t(p['gq']), flip_t(p['gk']), flip_t(p['gv']), flip_t(p['la'][1]), init[1])
    return o_f + flip_t(o_b), (s_f, s_b)

def mlstm_bidir(p, init):
    h_f, s_f = mlstm_chunked(p['mq'], p['mk'], p['mv'], p['li'][0], p['lf'][0], init[0])
    h_b, s_b = mlstm_chunked(flip_t(p['mq']), flip_t(p['mk']), flip_t(p['mv']),
                             flip_t(p['li'][1]), flip_t(p['lf'][1]), init[1])
    return h_f + flip_t(h_b), (s_f, s_b)

def even_output(gla_o, ml_h, p, gla_norm_w, ml_norm_w, w_out, dtype):
    B, _, T, _ = gla_o.shape
    go = head_rms_norm(gla_o.transpose(0, 2, 1, 3), gla_norm_w) * jax.nn.silu(p['gg']).reshape(B, T, GLA_HEADS, GLA_DV)
    mo = head_rms_norm(ml_h.transpose(0, 2, 1, 3), ml_norm_w) * jax.nn.sigmoid(p['mo']).reshape(B, T, MLSTM_HEADS, MLSTM_DH)
    y = jnp.concatenate([go.reshape(B, T, -1), mo.reshape(B, T, -1)], axis=-1).astype(dtype)
    return y @ w_out

def even_mixer(u_lat, u_ctx, w_in, w_out, a_up, a_bias, gla_norm_w, ml_gate_bias, ml_norm_w, rope_gla, rope_ml, need_ctx):
    B = u_lat.shape[0]
    p_ctx = even_project(u_ctx, w_in, a_up, a_bias, ml_gate_bias, None, None)
    p_lat = even_project(u_lat, w_in, a_up, a_bias, ml_gate_bias, rope_gla, rope_ml)
    gla0 = jnp.zeros((B, GLA_HEADS, GLA_DK, GLA_DV), jnp.float32)
    ml0 = (jnp.zeros((B, MLSTM_HEADS, MLSTM_DH, MLSTM_DH), jnp.float32),
           jnp.zeros((B, MLSTM_HEADS, MLSTM_DH), jnp.float32),
           jnp.zeros((B, MLSTM_HEADS), jnp.float32))
    gla_c, gla_states = gla_bidir(p_ctx, (gla0, gla0))
    ml_c, ml_states = mlstm_bidir(p_ctx, (ml0, ml0))
    gla_l, _ = gla_bidir(p_lat, gla_states)
    ml_l, _ = mlstm_bidir(p_lat, ml_states)
    y_lat = even_output(gla_l, ml_l, p_lat, gla_norm_w, ml_norm_w, w_out, u_lat.dtype)
    y_ctx = even_output(gla_c, ml_c, p_ctx, gla_norm_w, ml_norm_w, w_out, u_ctx.dtype) if need_ctx else None
    return y_lat, y_ctx

def neighbourhood_tables(rows):
    kh = min(NA_WIN_H, rows)
    kw = NA_WIN_W
    r = np.arange(rows)
    col = np.arange(GRID_W)
    key_r = np.clip(r - kh // 2, 0, rows - kh)[:, None] + np.arange(kh)[None, :]
    key_c = np.clip(col - kw // 2, 0, GRID_W - kw)[:, None] + np.arange(kw)[None, :]
    kr = key_r[:, None, :, None]
    kc = key_c[None, :, None, :]
    idx = kr * GRID_W + kc
    off = ((kr - r[:, None, None, None] + NA_WIN_H - 1) * (2 * NA_WIN_W - 1)
           + (kc - col[None, :, None, None] + NA_WIN_W - 1))
    n_keys = kh * kw
    return (jnp.asarray(idx.reshape(rows, GRID_W, n_keys), jnp.int32),
            jnp.asarray(off.reshape(rows, GRID_W, n_keys), jnp.int32))

def na_mixer(u_lat, u_ctx, w_qkv, w_out, rpb, need_ctx):
    B, T, D = u_lat.shape
    n_ctx = u_ctx.shape[1]
    rows = T // GRID_W
    scale = NA_DH ** -0.5
    heads = lambda z, n, parts: z.reshape(B, n, parts, NA_HEADS, NA_DH).transpose(2, 0, 3, 1, 4)
    q, k, v = heads(u_lat @ w_qkv, T, 3)
    if need_ctx:
        qc, kc, vc = heads(u_ctx @ w_qkv, n_ctx, 3)
    else:
        kc, vc = heads(u_ctx @ w_qkv[:, D:], n_ctx, 2)
    nbr_idx, bias_idx = neighbourhood_tables(rows)
    n_keys = nbr_idx.shape[-1]
    bias = rpb.reshape(NA_HEADS, -1)[:, bias_idx].astype(jnp.float32).transpose(1, 0, 2, 3)
    q_rows = (q * scale).reshape(B, NA_HEADS, rows, GRID_W, NA_DH).transpose(2, 0, 1, 3, 4)

    def row_block(args):
        q_r, idx_r, bias_r = args
        k_n = k[:, :, idx_r]
        v_n = v[:, :, idx_r]
        s = jnp.concatenate([jnp.einsum('bhqd,bhqkd->bhqk', q_r, k_n).astype(jnp.float32) + bias_r,
                             jnp.einsum('bhqd,bhcd->bhqc', q_r, kc).astype(jnp.float32)], axis=-1)
        p = jax.nn.softmax(s, axis=-1).astype(v.dtype)
        return (jnp.einsum('bhqk,bhqkd->bhqd', p[..., :n_keys], v_n)
                + jnp.einsum('bhqc,bhcd->bhqd', p[..., n_keys:], vc))

    o = lax.map(row_block, (q_rows, nbr_idx, bias))
    y_lat = o.transpose(1, 0, 3, 2, 4).reshape(B, T, D) @ w_out
    y_ctx = None
    if need_ctx:
        s_c = jnp.einsum('bhqd,bhkd->bhqk', qc * scale, kc).astype(jnp.float32)
        oc = jnp.einsum('bhqk,bhkd->bhqd', jax.nn.softmax(s_c, axis=-1).astype(vc.dtype), vc)
        y_ctx = oc.transpose(0, 2, 1, 3).reshape(B, n_ctx, D) @ w_out
    return y_lat, y_ctx

def conv_ffn(u, w_up, conv_w, conv_b, w_down):
    a, g = jnp.split(u @ w_up, 2, axis=-1)
    pad = FFN_CONV // 2
    a = lax.conv_general_dilated(a, conv_w[:, None, :].astype(a.dtype), (1,), [(pad, pad)],
                                 dimension_numbers=('NWC', 'WIO', 'NWC'), feature_group_count=D_FF) + conv_b
    return (jax.nn.gelu(a) * g) @ w_down

def setup_inputs(seed: int = 0) -> dict:
    key = jax.random.key(seed)
    ks = jax.random.split(key, 24)
    n_even = (DEPTH + 1) // 2
    n_odd = DEPTH // 2
    D = D_MODEL
    nrm = lambda k, shape, s: jax.random.normal(k, shape, jnp.float32) * s
    in_gate_b = nrm(ks[12], (n_even, 2, 1, MLSTM_HEADS), 0.1)
    fg_gate_b = jnp.linspace(3.0, 6.0, MLSTM_HEADS, dtype=jnp.float32)[None, None, None, :] + nrm(ks[13], (n_even, 2, 1, MLSTM_HEADS), 0.1)
    return {
        'x': nrm(ks[0], (BATCH, SEQ, D), 1.0),
        'c': nrm(ks[1], (BATCH, D), 1.0),
        'ctx': nrm(ks[2], (BATCH, CTX_LEN, D), 1.0),
        'c_ctx': nrm(ks[3], (D,), 1.0),
        'mod_w': nrm(ks[4], (DEPTH, D, 6 * D), 0.5 * D ** -0.5),
        'mod_b': nrm(ks[5], (DEPTH, 6 * D), 0.02),
        'norm_mix_w': 1.0 + nrm(ks[6], (DEPTH, D), 0.02),
        'norm_ffn_w': 1.0 + nrm(ks[7], (DEPTH, D), 0.02),
        'ev_w_in': nrm(ks[8], (n_even, D, EVEN_IN), D ** -0.5),
        'ev_w_out': nrm(ks[9], (n_even, MIX_WIDTH, D), MIX_WIDTH ** -0.5),
        'gla_a_up': nrm(ks[10], (n_even, 2, GLA_RANK, GLA_HEADS * GLA_DK), GLA_RANK ** -0.5),
        'gla_a_bias': nrm(ks[11], (n_even, 2, GLA_HEADS * GLA_DK), 0.1),
        'gla_norm_w': 1.0 + nrm(ks[14], (n_even, GLA_DV), 0.02),
        'ml_gate_bias': jnp.concatenate([in_gate_b, fg_gate_b], axis=2),
        'ml_norm_w': 1.0 + nrm(ks[15], (n_even, MLSTM_DH), 0.02),
        'na_w_qkv': nrm(ks[16], (n_odd, D, 3 * D), D ** -0.5),
        'na_w_out': nrm(ks[17], (n_odd, D, D), D ** -0.5),
        'na_rpb': nrm(ks[18], (n_odd, NA_HEADS, 2 * NA_WIN_H - 1, 2 * NA_WIN_W - 1), 0.05),
        'ffn_w_up': nrm(ks[19], (DEPTH, D, 2 * D_FF), D ** -0.5),
        'ffn_conv_w': nrm(ks[20], (DEPTH, FFN_CONV, D_FF), FFN_CONV ** -0.5),
        'ffn_conv_b': nrm(ks[21], (DEPTH, D_FF), 0.02),
        'ffn_w_down': nrm(ks[22], (DEPTH, D_FF, D), D_FF ** -0.5),
        'final_norm_w': 1.0 + nrm(ks[23], (D,), 0.02),
    }

def reference(x, c, ctx, c_ctx, mod_w, mod_b, norm_mix_w, norm_ffn_w, ev_w_in, ev_w_out, gla_a_up, gla_a_bias,
              gla_norm_w, ml_gate_bias, ml_norm_w, na_w_qkv, na_w_out, na_rpb, ffn_w_up, ffn_conv_w, ffn_conv_b,
              ffn_w_down, final_norm_w):
    T = x.shape[1]
    rope_gla = axial_rope(T, GLA_DK)
    rope_ml = axial_rope(T, MLSTM_DH)
    h, hc = x, ctx
    for layer in range(DEPTH):
        need_ctx = layer < DEPTH - 1
        j = layer // 2
        m_lat = (jax.nn.silu(c) @ mod_w[layer] + mod_b[layer])[:, None, :]
        m_ctx = (jax.nn.silu(c_ctx) @ mod_w[layer] + mod_b[layer])[None, None, :]
        sh1, sc1, g1, sh2, sc2, g2 = jnp.split(m_lat, 6, axis=-1)
        csh1, csc1, cg1, csh2, csc2, cg2 = jnp.split(m_ctx, 6, axis=-1)
        u = rms_norm(h, norm_mix_w[layer]) * (1.0 + sc1) + sh1
        uc = rms_norm(hc, norm_mix_w[layer]) * (1.0 + csc1) + csh1
        if layer % 2 == 0:
            y, yc = even_mixer(u, uc, ev_w_in[j], ev_w_out[j], gla_a_up[j], gla_a_bias[j], gla_norm_w[j],
                               ml_gate_bias[j], ml_norm_w[j], rope_gla, rope_ml, need_ctx)
        else:
            y, yc = na_mixer(u, uc, na_w_qkv[j], na_w_out[j], na_rpb[j], need_ctx)
        h = h + g1 * y.astype(h.dtype)
        u = rms_norm(h, norm_ffn_w[layer]) * (1.0 + sc2) + sh2
        h = h + g2 * conv_ffn(u, ffn_w_up[layer], ffn_conv_w[layer], ffn_conv_b[layer], ffn_w_down[layer])
        if need_ctx:
            hc = hc + cg1 * yc.astype(hc.dtype)
            uc = rms_norm(hc, norm_ffn_w[layer]) * (1.0 + csc2) + csh2
            hc = hc + cg2 * conv_ffn(uc, ffn_w_up[layer], ffn_conv_w[layer], ffn_conv_b[layer], ffn_w_down[layer])
    return rms_norm(h, final_norm_w)


_drawn_inputs = setup_inputs


def setup_inputs(seed=0):
    import zlib

    import numpy as np

    out = dict(_drawn_inputs(seed))
    spreads = {}
    factors = {'norm_mix_w': 6.264,
     'norm_ffn_w': 6.066,
     'gla_a_bias': 8.0,
     'gla_norm_w': 8.0,
     'ml_norm_w': 63.519,
     'na_rpb': 64.0,
     'ffn_conv_b': 8.0,
     'final_norm_w': 8.293}
    for name, (base, spread) in spreads.items():
        noise = np.random.default_rng([zlib.crc32(name.encode()), seed]).standard_normal(out[name].shape)
        drawn = base * np.exp(spread * noise) if base else spread * noise
        out[name] = __import__('jax').numpy.asarray(drawn.astype(out[name].dtype))
    for name, factor in factors.items():
        out[name] = (out[name] * factor).astype(out[name].dtype)
    return out
```

```python
from contextlib import ExitStack, contextmanager

import numpy as np

import concourse.bass as bass
from concourse import mybir

ALU = mybir.AluOpType
ACT = mybir.ActivationFunctionType
AX_X = mybir.AxisListType.X
F32 = mybir.dt.float32
F32R = mybir.dt.float32r

P = 128
D = 1024
KT = D // P
N_CTX, N_LAT = 256, 512
N_TOK = N_CTX + N_LAT
CTX, LAT = slice(0, N_CTX), slice(N_CTX, N_TOK)
TILES = N_TOK // P
GRID_W, GRID_H = 64, N_LAT // 64
EPS = 1e-6

GLA_CHUNK = 64
GLA_DK, ML_DH = 64, 128
HEADS = 4
GLA_PAIRS = HEADS // 2
GLA_TAU = 16.0

NA_HEADS, NA_DH = 16, 64
NA_WIN_W = 16
NA_TILES = N_LAT // P

D_FF = ((8 * D // 3 + 255) // 256) * 256
FT = D_FF // P
M_GROUP = 4

BLOCK = 1024
RAW_SLOTS, SPLIT_SLOTS = 4, 2
N_IN, N_V, N_OUT, N_UP, N_DOWN, N_QK = 21, 8, 8, 2 * FT, FT, 16
S_IN = 0
S_V = S_IN + N_IN
S_OUT0 = S_V + N_V
S_UP0 = S_OUT0 + N_OUT
S_DOWN0 = S_UP0 + N_UP
S_QK = S_DOWN0 + N_DOWN
S_V1 = S_QK + N_QK
S_OUT1 = S_V1 + N_V
S_UP1 = S_OUT1 + N_OUT
S_DOWN1 = S_UP1 + N_UP
S_END = S_DOWN1 + N_DOWN
MOD_PARTS = 6
MOD_TILES = 2 * MOD_PARTS * KT
MOD_FIRST = 2 * KT
assert MOD_FIRST % 4 == 0 and (MOD_TILES - MOD_FIRST) % 4 == 0
NEG = -1e30

V_NMIX, V_NFFN, V_NFIN = 0, 16, 32
V_MODB = 40
V_GLAN, V_MLN = V_MODB + MOD_TILES, V_MODB + MOD_TILES + 1
V_ABIAS = V_MLN + 1
V_CONV = V_ABIAS + 4
V_GATEB = V_CONV + 2 * FT * 4
V_C = V_GATEB + 2
V_N = V_C + 2 * KT


def raw_index(s):
    return s + MOD_FIRST if s < S_OUT0 else s + MOD_TILES


def q_scale(n):
    return GLA_DK ** -0.5 if n in (1, 2) else ML_DH ** -0.5 if n >= 9 else 1.0


def mod_raw_index(m):
    return m if m < MOD_FIRST else m + S_OUT0


class Signal:

    def __init__(self, sem):
        self.sem, self.base, self.k, self.per, self.i = sem, 0, 0, 0, 0

    def count(self):
        return self.base + self.k + self.per * self.i if self.per else self.base + self.k


class Own:

    def __init__(self, eng):
        self.eng, self.newest = eng, None

    def one(self, signal):
        signal.k += 1
        self.newest = signal
        return signal.sem, 1

    def last(self):
        return self.newest.sem, self.newest.count()

    @contextmanager
    def loop(self, trips, per):
        self.eng.wait_ge(*self.last())
        with self.eng.Fori(0, trips) as i:
            for s, n in per.items():
                s.base, s.k, s.per, s.i = s.base + s.k, 0, n, i
            yield i
            self.eng.wait_ge(*self.last())
        for s, n in per.items():
            assert s.k == n, (s.sem, s.k, n)
            s.base, s.k, s.per, s.i = s.base + n * trips, 0, 0, 0


def build(nc, xT, vecs, consts_d, rope_d, reset_d, a_up_d, na_bias_d, weights, outT):
    ctx = ExitStack()
    with ctx:
        SB0 = 16512
        T = N_TOK * 4
        place = [SB0]

        def at(name, shape, off, dt=F32):
            assert off % 32 == 0
            return nc.alloc_sbuf_tensor_at(name, shape, dt, offset=off)

        def take(name, shape, dt=F32):
            n = 4
            for x in shape[1:]:
                n *= x
            t = at(name, shape, place[0], dt)
            place[0] += (n + 31) // 32 * 32
            return t

        h_off = place[0]
        h = take("h", [P, KT, N_TOK])
        gates = at("gates", [P, KT, N_TOK], h_off)
        u_off = place[0]
        u = take("u", [P, KT, 2, N_TOK], F32R)
        raw = take("raw", [P, RAW_SLOTS, BLOCK])
        wsp = take("wsp", [P, SPLIT_SLOTS, 2, BLOCK], F32R)
        ident = take("ident", [P, P])
        ones = take("ones", [P, P])
        vec = take("vec", [P, V_N])
        modm = take("modm", [P, MOD_TILES, 2])
        amod = take("amod", [P, 4, KT, 2])
        cvec = take("cvec", [P, KT, 2])
        epsc = take("epsc", [P, 1])
        mdec = take("mdec", [P, HEADS])
        mstart = take("mstart", [64, TILES])
        pend = take("pend", [64, TILES])
        ar = place[0]
        AR_END = 229344

        sq = at("sq", [P, 2, N_TOK], ar)
        nt = at("nt", [P, 2, N_TOK], ar + 2 * T)
        rstd = at("rstd", [P, N_TOK], ar + 4 * T)
        fout = at("fout", [P, KT, N_LAT], ar + 5 * T)
        gqk = at("gqk", [P, 4, N_TOK], ar)
        gv = at("gv", [P, TILES, 512], ar + 4 * T)
        mqk = at("mqk", [P, 8, N_TOK], ar + 8 * T)
        mv = at("mv", [P, TILES, 512], ar + 16 * T)
        o0 = ar + 20 * T
        small = at("small", [P, N_TOK], o0)
        tmp = at("tmp", [P, N_TOK], o0 + T)
        reset = at("reset", [P, 2, N_TOK + 1], o0 + 2 * T)
        o1 = o0 + 2 * T + 6176
        cmask = at("cmask", [P, 4, P], o1)
        sel = at("sel", [P, 2, 64], o1 + 2048)
        aup = at("aup", [P, 2, 256], o1 + 2560)
        wend = at("wend", [P, TILES, 64], o1 + 4608)
        gdec = at("gdec", [P, 4, N_TOK // GLA_CHUNK], o1 + 6144)
        o2 = o1 + 6336
        rope = at("rope", [P, 4, N_LAT], o2)
        xs = at("xs", [P, N_LAT], o2 + 8192)
        cum = at("cum", [P, 4, N_TOK], o2 + 10240)
        assert o2 + 10240 + 4 * T <= AR_END
        qd = at("qd", [P, 4, N_TOK], u_off)
        kd = at("kd", [P, 4, N_TOK], u_off + 4 * T)
        gla_o = at("gla_o", [P, HEADS, N_TOK], u_off + 12 * T)
        gsc = at("gsc", [P, 2, 2, GLA_PAIRS, P], o2)
        gktok = at("gktok", [P, 2, 2 * P], o2 + 4096)
        gT = at("gT", [P, 2, GLA_PAIRS, 2, P], o2 + 6144)
        gS = at("gS", [P, 2, GLA_PAIRS, 2, P], o2 + 10240)
        rA = at("rA", [64, N_TOK], u_off + 8 * T)
        rB = at("rB", [64, N_TOK], u_off + 9 * T)
        rP = at("rP", [64, N_TOK], u_off + 10 * T)
        rI = at("rI", [64, N_TOK], u_off + 11 * T)
        mktok = at("mktok", [P, TILES, 512], u_off)
        ml_o = at("ml_o", [P, HEADS, N_TOK], ar)
        mD = at("mD", [P, HEADS, P], o2)
        msc = at("msc", [P, HEADS, P], o2 + 2048)
        mqs = at("mqs", [P, HEADS, P], o2 + 4096)
        mks = at("mks", [P, HEADS, P], o2 + 6144)
        megs = at("megs", [P, HEADS, P], o2 + 8192)
        mden = at("mden", [P, HEADS, P], o2 + 10240)
        mC = at("mC", [P, 2, HEADS, 2 * P], o2 + 12288)
        assert o2 + 12288 + 8192 <= AR_END
        gsq = at("gsq", [P, 2, N_TOK], ar + 4 * T)
        grt = at("grt", [P, 2, N_TOK], ar + 6 * T)
        gy = at("gy", [P, 2, N_TOK], ar + 8 * T)
        PADW = N_TOK + 4
        CW = N_TOK + 2
        L0C = N_CTX + 2
        hid = at("hid", [P, FT, N_TOK], ar)
        f0 = ar + FT * T
        apad = at("apad", [P, 2, PADW], f0)
        conv = at("conv", [P, 2, CW], f0 + 6176)
        gel = at("gel", [P, 2, CW], f0 + 12352)
        hsp = at("hsp", [P, 2, 2, N_TOK], f0 + 18528, F32R)
        assert f0 + 18528 + 4 * T <= AR_END
        naq = at("naq", [P, KT, N_LAT], ar)
        nak = at("nak", [P, KT, N_TOK], ar + 16384)
        nav = at("nav", [P, TILES, D], ar + 16384 + 8 * T)
        n0 = ar + 16384 + 16 * T
        nab = at("nab", [P, 2, NA_TILES, 256], n0)
        nas = at("nas", [P, 2, 512], n0 + 8192)
        nap = at("nap", [P, 2, 4, P], n0 + 12288)
        nay = at("nay", [P, 2, N_LAT], n0 + 16384)
        nast = at("nast", [P, 2, 4], n0 + 20480)
        assert n0 + 20512 <= AR_END

        ps = ctx.enter_context(nc.psum_tensor("ps", [P, 8, 512], F32))

        def sem(name):
            return Signal(ctx.enter_context(nc.semaphore(name)))

        vec_loaded, x_loaded, const_loaded, x_again, out_stored = map(
            sem, ("vec_loaded", "x_loaded", "const_loaded", "x_again", "out_stored"))
        raw_loaded = [sem(f"raw_loaded{i}") for i in range(RAW_SLOTS)]
        bias_loaded = [sem(f"bias_loaded{i}") for i in range(2)]
        hi_ready, lo_ready, block_used = map(sem, ("hi_ready", "lo_ready", "block_used"))
        mod_done, mod_taken, mod_scaled = map(sem, ("mod_done", "mod_taken", "mod_scaled"))
        act_own, dve_own, pool_own = map(sem, ("act_own", "dve_own", "pool_own"))
        ones_ready, c_ready = map(sem, ("ones_ready", "c_ready"))

        class Norm:
            def __init__(self, n):
                self.cx_bank = 5 if n == 1 else 7
                self.sq_ready = sem(f"norm{n}_sq_ready")
                self.sq_summed = sem(f"norm{n}_sq_summed")
                self.root_ready = sem(f"norm{n}_root_ready")
                self.t_ready = sem(f"norm{n}_t_ready")
                self.hi_ready = sem(f"norm{n}_hi_ready")
                self.lo_ready = sem(f"norm{n}_lo_ready")
        norm = [Norm(n) for n in range(5)]
        (in_act_took, in_dve_took, xs_used, apre_done, apre_taken, apre_log, cum_ready, v_act, v_dve,
         rows_done, rows_taken, row_abs, row_ln, row_lf, row_args, row_exp, wend_turned, wend_ready,
         dec_exp, dec_ready, state_zero) = map(sem, (
             "in_act_took", "in_dve_took", "xs_used", "apre_done", "apre_taken", "apre_log", "cum_ready", "v_act",
             "v_dve", "rows_done", "rows_taken", "row_abs", "row_ln", "row_lf", "row_args", "row_exp",
             "wend_turned", "wend_ready", "dec_exp", "dec_ready", "state_zero"))
        ga_done, gsc_ready, gktok_ready, gkv_done, gS_ready, gT_ready, gi_done, go_taken = map(sem, (
            "ga_done", "gsc_ready", "gktok_ready", "gkv_done", "gS_ready", "gT_ready", "gi_done", "go_taken"))
        ktok_turned, ktok_ready, mC_zero = map(sem, ("ktok_turned", "ktok_ready", "mC_zero"))
        ml_lw, ml_sc, ml_iw, lw_ready, mD_ready, mqs_ready, iw_taken, msc_ready, mks_ready = map(sem, (
            "ml_lw", "ml_sc", "ml_iw", "lw_ready", "mD_ready", "mqs_ready", "iw_taken", "msc_ready", "mks_ready"))
        eg_done, megs_ready, mkv_done, mC_ready, mh_done, mden_ready, mh_taken = map(sem, (
            "eg_done", "megs_ready", "mkv_done", "mC_ready", "mh_done", "mden_ready", "mh_taken"))
        g_sq, g_sum, g_root, g_y, g_hi, g_lo = map(sem, ("g_sq", "g_sum", "g_root", "g_y", "g_hi", "g_lo"))

        class Ffn:
            def __init__(self, n):
                self.pad_zero = sem(f"ffn{n}_pad_zero")
                self.a_taken = sem(f"ffn{n}_a_taken")
                self.c_ready = sem(f"ffn{n}_c_ready")
                self.conv_done = sem(f"ffn{n}_conv_done")
                self.gel_ready = sem(f"ffn{n}_gel_ready")
                self.g_taken = sem(f"ffn{n}_g_taken")
                self.hh_ready = sem(f"ffn{n}_hh_ready")
                self.hl_ready = sem(f"ffn{n}_hl_ready")
                self.hid_used = sem(f"ffn{n}_hid_used")
                self.h_updated = sem(f"ffn{n}_h_updated")
                self.out_updated = sem(f"ffn{n}_out_updated")
        ffn = [Ffn(n) for n in range(2)]
        (qk_taken, nav_act, nav_dve, s_done, s_ctx, s_lat, neg_max, p_exp, p_ready, p_turned, pt_ready,
         o_done, y_taken, y_hi, y_lo, bias_used) = map(sem, (
             "qk_taken", "nav_act", "nav_dve", "s_done", "s_ctx", "s_lat", "neg_max", "p_exp", "p_ready",
             "p_turned", "pt_ready", "o_done", "y_taken", "y_hi", "y_lo", "bias_used"))

        ORDER = [list(range(TILES)), [1, 0, 5, 4, 3, 2]]
        UNITS = [(n, z, ORDER[z][n]) for n in range(TILES) for z in range(2)]
        seen, FRESH = set(), []
        for _, _, i in UNITS:
            FRESH.append(i not in seen)
            seen.add(i)

        def tile(i):
            return slice(P * i, P * i + P)

        def halves(t):
            return ((CTX, 1), (LAT, 0))

        def blocks(eng_loop, per, count, body, first=4):
            for n in range(min(first, count)):
                body(n, 0)
            turns = (count - first) // 4
            if turns > 0:
                with eng_loop(turns, per) as i:
                    for n in range(first, first + 4):
                        body(n, i)
                for n in range(first + 4 * turns, count):
                    body(n, 0)

        def s_count(s, i):
            return s + 4 * i + 1

        def at_(t, col, off):
            if isinstance(off, int):
                return lambda n: t[:, col + off + n:col + off + n + 1]
            return lambda n: t[:, bass.ds(off + (col + n), 1)]

        def hid_at(k, i, toks, step=8):
            if isinstance(i, int):
                return hid[:, k + step * i, toks]
            return hid[:, bass.ds(i * step + k, 1), toks].rearrange("p a n -> p (a n)")

        def cx_bank(n):
            return ps[:, 2 if n % 2 == 0 else 7, 0:N_CTX]

        block = ctx.enter_context(nc.Block())

        @block.sync
        def _(sp):
            sp.dma_start(vec[:, :], vecs).then_inc(vec_loaded.sem, 16)
            sp.dma_start(h[:, :, :], xT).then_inc(x_loaded.sem, 16)

            def source(r, i):
                if isinstance(i, int):
                    return weights[r + 4 * i]
                return weights[bass.ds(i * 4 + r, 1), :, :].rearrange("a p n -> (a p) n")

            def load(r, i, used, least):
                if used is not None:
                    sp.wait_ge(used.sem, least + 4 * i)
                sp.dma_start(raw[:, r % 4, :], source(r, i)).then_inc(raw_loaded[r % 4].sem, 16)

            def run(a, b, used, least):
                turns = (b - a) // 4
                if turns > 1:
                    with sp.Fori(0, turns) as i:
                        for n in range(4):
                            load(a + n, i, used, least + n)
                    a, least = a + 4 * turns, least + 4 * turns
                for n in range(b - a):
                    load(a + n, 0, used, least + n)

            for r in range(RAW_SLOTS):
                load(r, 0, None, 0)
            sp.dma_start(ident[:, :], consts_d[:, 0:P]).then_inc(const_loaded.sem, 16)
            sp.dma_start(rope[:, :, :], rope_d).then_inc(const_loaded.sem, 16)
            sp.dma_start(sel[:, :, :], consts_d[:, P:2 * P].rearrange("p (a b) -> p a b", a=2)).then_inc(const_loaded.sem, 16)
            sp.dma_start(cmask[:, :, :], consts_d[:, 2 * P:6 * P].rearrange("p (a b) -> p a b", a=4)).then_inc(const_loaded.sem, 16)
            sp.dma_start(reset[:, :, :], reset_d).then_inc(const_loaded.sem, 16)
            sp.dma_start(aup[:, :, :], a_up_d).then_inc(const_loaded.sem, 16)
            m0, ms = MOD_FIRST, MOD_FIRST + S_OUT0
            run(RAW_SLOTS, m0, mod_done, 1)
            run(m0, m0 + 4, mod_done, m0 - 3)
            run(m0 + 4, ms, lo_ready, 1)
            run(ms, ms + 4, lo_ready, S_OUT0 - 3)
            run(ms + 4, MOD_TILES + S_OUT0, mod_done, m0 + 1)
            run(MOD_TILES + S_OUT0, MOD_TILES + S_OUT0 + 4, mod_done, MOD_TILES - 3)
            run(MOD_TILES + S_OUT0 + 4, MOD_TILES + S_END, lo_ready, S_OUT0 + 1)
            for k in range(KT):
                sp.wait_ge(norm[4].t_ready.sem, k + 1)
                sp.dma_start(outT[:, k, :], fout[:, k, :]).then_inc(out_stored.sem, 16)
            sp.wait_ge(out_stored.sem, 16 * KT)

        @block.gpsimd
        def _(pool):
            own = Own(pool)
            pool.memset(ones[:, :], 1.0).then_inc(*own.one(ones_ready))
            pool.memset(epsc[:, :], EPS).then_inc(*own.one(ones_ready))

            def low(s, i):
                pool.wait_ge(*own.last())
                pool.wait_ge(hi_ready.sem, s_count(s, i))
                pool.tensor_tensor(wsp[:, s % 2, 1, :], raw[:, s % 4, :], wsp[:, s % 2, 0, :].bitcast(F32),
                                   ALU.subtract).then_inc(*own.one(lo_ready))

            blocks(own.loop, {lo_ready: 4}, S_OUT0, low)
            blocks(own.loop, {lo_ready: 4}, S_END - S_OUT0, lambda n, i: low(S_OUT0 + n, i))

        @block.scalar
        def _(act):
            own = Own(act)

            def high(s, i=0):
                if isinstance(i, int):
                    if s + 4 * i >= S_END:
                        return
                act.wait_ge(*own.last())
                act.wait_ge(raw_loaded[s % 4].sem, 16 * (raw_index(s) // 4 + 1 + i))
                if s >= 2:
                    act.wait_ge(block_used.sem, s_count(s, i) - 2)
                act.activation(wsp[:, s % 2, 0, :], raw[:, s % 4, :], ACT.Copy).then_inc(*own.one(hi_ready))

            act.wait_ge(vec_loaded.sem, 16)
            act.activation(cvec[:, :, :], vec[:, V_C:V_C + 2 * KT].rearrange("p (k r) -> p k r", r=2),
                           ACT.Silu).then_inc(*own.one(c_ready))

            def normalise(q, idx, A, B, updated, last_tok, permute=False):
                for k in range(KT):
                    act.wait_ge(*own.last())
                    if updated is not None:
                        act.wait_ge(updated.sem, k + 1 if updated is not x_loaded else 16)
                    if k >= 2:
                        act.wait_ge(q.sq_summed.sem, k - 1)
                    act.activation(sq[:, k % 2, last_tok], h[:, k, last_tok], ACT.Square)\
                       .then_inc(*own.one(q.sq_ready))
                act.wait_ge(ones_ready.sem, 2)
                act.wait_ge(q.sq_summed.sem, KT)
                for t, bank, w in ((LAT, 6, N_LAT), (CTX, q.cx_bank, N_CTX)):
                    if t == CTX and last_tok == LAT:
                        continue
                    act.wait_ge(*own.last())
                    act.activation(rstd[:, t], ps[:, bank, 0:w], ACT.Sqrt, bias=epsc[:, 0:1], scale=1.0 / D)\
                       .then_inc(*own.one(q.root_ready))
                if A is None:
                    return
                act.wait_ge(mod_scaled.sem, idx + 1)
                for k in range(KT):
                    act.wait_ge(q.t_ready.sem, k + 1)
                    for t, r in halves(None):
                        if t == CTX and last_tok == LAT:
                            continue
                        act.wait_ge(*own.last())
                        act.activation(nt[:, k % 2, t], nt[:, k % 2, t], ACT.Identity,
                                       bias=B(k, r), scale=A[:, k, r:r + 1]).then_inc(*own.one(act_own))
                    act.wait_ge(*own.last())
                    if not permute:
                        act.activation(u[:, k, 0, last_tok], nt[:, k % 2, last_tok], ACT.Copy)\
                           .then_inc(*own.one(q.hi_ready))
                    else:
                        act.activation(u[:, k, 0, CTX], nt[:, k % 2, CTX], ACT.Copy).then_inc(*own.one(act_own))
                        act.wait_ge(*own.last())
                        act.activation(u[:, k, 0, LAT].rearrange("p (g r c) -> p r g c", g=8, c=8),
                                       nt[:, k % 2, LAT].rearrange("p (r g c) -> p r g c", g=8, c=8), ACT.Copy)\
                           .then_inc(*own.one(q.hi_ready))

            def shift(layer, part):
                return lambda k, r: modm[:, (layer * MOD_PARTS + part) * KT + k, r:r + 1]

            high(0)
            high(1)
            normalise(norm[0], 0, amod[:, 0], shift(0, 0), x_loaded, slice(0, N_TOK))

            def log_sigmoid_parts(src_abs, rows, out_signal):
                act.wait_ge(*own.last())
                act.activation(tmp[0:rows, :], src_abs, ACT.Abs).then_inc(*own.one(act_own))
                act.wait_ge(*own.last())
                act.activation(tmp[0:rows, :], tmp[0:rows, :], ACT.Exp, scale=-1.0).then_inc(*own.one(act_own))
                act.wait_ge(*own.last())
                act.activation(tmp[0:rows, :], tmp[0:rows, :], ACT.Ln, bias=1.0).then_inc(*own.one(out_signal))

            def decay_logs(zp):
                b = 3 + 2 * (zp % 2)
                act.wait_ge(apre_done.sem, zp + 1)
                for t, bank, w in ((LAT, b, N_LAT), (CTX, b + 1, N_CTX)):
                    act.wait_ge(*own.last())
                    act.activation(cum[:, zp, t], ps[:, bank, 0:w], ACT.Identity,
                                   bias=vec[:, V_ABIAS + zp:V_ABIAS + zp + 1]).then_inc(*own.one(apre_taken))
                if zp:
                    act.wait_ge(cum_ready.sem, zp)
                log_sigmoid_parts(cum[:, zp, :], P, apre_log)

            act.wait_ge(const_loaded.sem, 16 * 6)
            for n in range(N_IN):
                act.wait_ge(block_used.sem, n + 1)
                high(n + 2)
                lat, cx = ps[:, n % 2, :], cx_bank(n)
                act.wait_ge(*own.last())
                if n == 0:
                    act.activation(small[:, CTX], cx, ACT.Copy).then_inc(*own.one(act_own))
                    act.activation(small[:, LAT], lat, ACT.Copy).then_inc(*own.one(in_act_took))
                elif n <= 12:
                    dst = gqk[:, n - 1, :] if n <= 4 else mqk[:, n - 5, :]
                    half = GLA_DK // 2 if n <= 4 else ML_DH // 2
                    act.activation(dst[:, CTX], cx, ACT.Copy, scale=q_scale(n)).then_inc(*own.one(act_own))
                    if n >= 2:
                        act.wait_ge(xs_used.sem, n - 1)
                    for a in range(0, P, half):
                        b = a ^ half
                        last = a + half == P
                        act.activation(xs[a:a + half, :], ps[b:b + half, n % 2, :], ACT.Copy)\
                           .then_inc(*own.one(in_act_took if last else act_own))
                else:
                    f = n - 13
                    func = ACT.Silu if f < 4 else ACT.Sigmoid
                    act.activation(gates[:, f, CTX], cx, func).then_inc(*own.one(act_own))
                    act.activation(gates[:, f, LAT], lat, func).then_inc(*own.one(in_act_took))
                if n in (2, 10):
                    decay_logs(0 if n == 2 else 2)
                    decay_logs(1 if n == 2 else 3)
            for cg, dst in enumerate((gv, mv)):
                for b in range(4):
                    act.wait_ge(block_used.sem, S_V + 4 * cg + b + 1)
                    if S_V + 4 * cg + b + 2 < S_OUT0:
                        high(S_V + 4 * cg + b + 2)
                for i in range(0, TILES, 2):
                    act.wait_ge(*own.last())
                    act.activation(dst[:, i, :], ps[:, i, :], ACT.Copy).then_inc(*own.one(v_act))

            for zp in range(4):
                act.wait_ge(cum_ready.sem, 4)
                act.wait_ge(*own.last())
                act.activation(qd[:, zp, :], cum[:, zp, :], ACT.Exp, scale=1.0 / GLA_TAU).then_inc(*own.one(act_own))
                act.activation(kd[:, zp, :], cum[:, zp, :], ACT.Exp, scale=-1.0 / GLA_TAU).then_inc(*own.one(act_own))
                end = GLA_CHUNK - 1 if zp < 2 else 0
                act.activation(gdec[:, zp, :], cum[:, zp, end::GLA_CHUNK], ACT.Exp, scale=1.0 / GLA_TAU)\
                   .then_inc(*own.one(dec_exp))

            act.wait_ge(rows_done.sem, 2)
            for row, b, col in ((rA, 3, 0), (rB, 5, 1)):
                for t, bank, w in ((LAT, b, N_LAT), (CTX, b + 1, N_CTX)):
                    act.wait_ge(*own.last())
                    act.activation(row[:, t], ps[0:64, bank, 0:w], ACT.Identity,
                                   bias=vec[0:64, V_GATEB + col:V_GATEB + col + 1]).then_inc(*own.one(rows_taken))
            act.wait_ge(cum_ready.sem, 4)
            log_sigmoid_parts(rB[:, :], 64, row_ln)

            def row_exps():
                act.wait_ge(row_args.sem, 1)
                act.wait_ge(*own.last())
                act.activation(rI[:, :], rI[:, :], ACT.Exp).then_inc(*own.one(row_exp))
                act.activation(tmp[0:64, :], tmp[0:64, :], ACT.Exp).then_inc(*own.one(row_exp))
                act.activation(rB[:, :], rB[:, :], ACT.Exp, scale=-1.0).then_inc(*own.one(row_exp))

            for un, (n, z, i) in enumerate(UNITS):
                act.wait_ge(ga_done.sem, un + 1)
                act.wait_ge(*own.last())
                if un >= 2:
                    act.wait_ge(gkv_done.sem, un - 1)
                act.activation(gktok[:, un % 2, :], ps[:, 2, 0:2 * P], ACT.Copy).then_inc(*own.one(gktok_ready))
                if un == 0:
                    act.wait_ge(state_zero.sem, 1)
                for c in range(2):
                    place_c = 2 * i + (c if z == 0 else 1 - c)
                    if c == 1:
                        before = 2 * i + (0 if z == 0 else 1)
                    else:
                        j = ORDER[z][n - 1] if n else i
                        before = 2 * j + (1 if z == 0 else 0)
                    if un >= 1:
                        act.wait_ge(gi_done.sem, 2 * (un - 1) + c + 1)
                        act.wait_ge(gT_ready.sem, 2 * (un - 1) + c + 1)
                    if c == 1:
                        act.wait_ge(gT_ready.sem, 2 * un + 1)
                    act.wait_ge(*own.last())
                    for p in range(GLA_PAIRS):
                        zp = 2 * z + p
                        act.activation(gS[:, c, p, :, :], gT[:, z, p, :, :], ACT.Copy,
                                       scale=gdec[:, zp, before:before + 1])\
                           .then_inc(*own.one(gS_ready if p else act_own))
                if un == 3:
                    row_exps()

            act.wait_ge(wend_turned.sem, 1)
            act.wait_ge(*own.last())
            act.activation(wend[:, :, :], ps[:, 5, 0:TILES * 64].rearrange("p (i r) -> p i r", r=64), ACT.Copy)\
               .then_inc(*own.one(wend_ready))
            for i in range(TILES):
                act.wait_ge(ktok_turned.sem, i + 1)
                act.wait_ge(*own.last())
                act.activation(mktok[:, i, :], ps[:, i % 2, :], ACT.Copy).then_inc(*own.one(ktok_ready))
            for un, (n, z, i) in enumerate(UNITS):
                act.wait_ge(*own.last())
                if un >= 1:
                    act.wait_ge(mkv_done.sem, un)
                for hd in range(HEADS):
                    r = 32 * z + hd
                    act.activation(mks[:, hd, :], mktok[:, i, tile(hd)], ACT.Copy, scale=wend[:, i, r:r + 1])\
                       .then_inc(*own.one(mks_ready if hd == HEADS - 1 else act_own))
                act.wait_ge(lw_ready.sem, un + 1)
                act.activation(mD[:, :, :], mD[:, :, :], ACT.Exp).then_inc(*own.one(mD_ready))
                act.wait_ge(eg_done.sem, un + 1)
                if un >= 1:
                    act.wait_ge(mden_ready.sem, un)
                act.activation(megs[:, :, :], ps[:, 2, :].rearrange("p (a b) -> p a b", a=HEADS), ACT.Copy)\
                   .then_inc(*own.one(megs_ready))

            high(S_OUT0)
            high(S_OUT0 + 1)
            for f in range(KT + 1):
                if f < KT:
                    if f == 0:
                        act.wait_ge(go_taken.sem, len(UNITS))
                        act.wait_ge(mh_taken.sem, len(UNITS))
                    act.wait_ge(*own.last())
                    if f >= 2:
                        act.wait_ge(g_sum.sem, f - 1)
                    o = gla_o[:, f, :] if f < 4 else ml_o[:, f - 4, :]
                    act.activation(gsq[:, f % 2, :], o, ACT.Square).then_inc(*own.one(g_sq))
                if f >= 1:
                    e = f - 1
                    act.wait_ge(g_sum.sem, e + 1)
                    if e >= 2:
                        act.wait_ge(g_y.sem, e - 1)
                    for t, bank, w in ((LAT, 2 * (e % 2), N_LAT), (CTX, 2 * (e % 2) + 1, N_CTX)):
                        act.wait_ge(*own.last())
                        act.activation(grt[:, e % 2, t], ps[:, bank, 0:w], ACT.Sqrt, bias=epsc[:, 0:1], scale=1.0 / P)\
                           .then_inc(*own.one(g_root))
                    act.wait_ge(g_y.sem, e + 1)
                    act.wait_ge(*own.last())
                    act.activation(u[:, e, 0, :], gy[:, e % 2, :], ACT.Copy).then_inc(*own.one(g_hi))
            act.dma_start(h[:, :, :], xT).then_inc(x_again.sem, 16)
            for m in range(N_OUT):
                act.wait_ge(block_used.sem, S_OUT0 + m + 1)
                high(S_OUT0 + m + 2)

            def feed_forward(q, layer, s_up, s_down, toks):
                lo, w = (0, CW) if layer == 0 else (L0C, N_LAT)
                cv = V_CONV + layer * FT * 4

                def up(n, i):
                    j, par = n // 2, (n // 2) % 2
                    act.wait_ge(block_used.sem, s_count(s_up + n, i))
                    high(s_up + n + 2, i)
                    act.wait_ge(*own.last())
                    if n % 2 == 0:
                        if n == 0:
                            act.wait_ge(q.pad_zero.sem, 1)
                        if j >= 2:
                            act.wait_ge(q.conv_done.sem, j - 1 + 2 * i)
                            act.wait_ge(q.gel_ready.sem, j - 1 + 2 * i)
                        if layer == 0:
                            act.activation(apad[:, par, 1:1 + N_CTX], cx_bank(0), ACT.Copy)\
                               .then_inc(*own.one(act_own))
                        act.activation(apad[:, par, L0C + 1:L0C + 1 + N_LAT], ps[:, 0, :], ACT.Copy)\
                           .then_inc(*own.one(q.a_taken))
                        act.wait_ge(*own.last())
                        c = at_(vec, cv + 4 * j, 8 * i)
                        act.activation(conv[:, par, lo:lo + w], apad[:, par, lo + 1:lo + 1 + w], ACT.Identity,
                                       bias=c(3), scale=c(1)).then_inc(*own.one(q.c_ready))
                    else:
                        act.wait_ge(q.conv_done.sem, j + 1 + 2 * i)
                        if j >= 2:
                            act.wait_ge(q.g_taken.sem, j - 1 + 2 * i)
                        act.activation(gel[:, par, lo:lo + w], conv[:, par, lo:lo + w], ACT.Gelu_apprx_tanh)\
                           .then_inc(*own.one(q.gel_ready))

                blocks(own.loop, {hi_ready: 4, q.a_taken: 2, q.c_ready: 2, q.gel_ready: 2,
                                  **({act_own: 2} if layer == 0 else {})}, N_UP, up)

                def hidden_high(k, kx, i=0):
                    act.wait_ge(*own.last())
                    if k < 2:
                        act.wait_ge(q.g_taken.sem, FT)
                    if k >= 2 and k % 2 == 0:
                        act.wait_ge(q.hid_used.sem, k // 2 + 4 * i)
                    elif k >= 2:
                        act.wait_ge(block_used.sem, s_down + k // 2 + 4 * i)
                    act.activation(hsp[:, k % 2, 0, toks], hid_at(kx, i, toks), ACT.Copy)\
                       .then_inc(*own.one(q.hh_ready))

                hidden_high(0, 0)
                hidden_high(1, 1)

                def down(b, i):
                    g0 = b // (FT // 2) * (FT // 2)
                    for kk in range(2):
                        k = 2 * b + kk + 2
                        if k < 2 * FT:
                            hidden_high(k, k - (FT if k >= FT else 0), i)
                    act.wait_ge(block_used.sem, s_count(s_down + b, i))
                    high(s_down + b + 2, i)

                half = FT // 2
                for g0 in (0, half):
                    down(g0, 0)
                    with own.loop(2, {q.hh_ready: 8, hi_ready: 4}) as i:
                        for b in range(g0 + 1, g0 + 5):
                            down(b, i)
                    for b in range(g0 + 9, g0 + half):
                        down(b, 0)

            normalise(norm[1], 1, amod[:, 1], shift(0, 3), ffn[0].out_updated, slice(0, N_TOK))
            feed_forward(ffn[0], 0, S_UP0, S_DOWN0, slice(0, N_TOK))
            normalise(norm[2], 2, amod[:, 2], shift(1, 0), ffn[0].h_updated, slice(0, N_TOK), permute=True)

            def qk(n, i, first):
                act.wait_ge(block_used.sem, s_count(S_QK + n, i))
                high(S_QK + n + 2, i)
                act.wait_ge(*own.last())
                lat, cx = ps[:, n % 2, :], cx_bank(n)
                if n < KT:
                    act.activation(naq[:, n, :], lat, ACT.Copy, scale=NA_DH ** -0.5).then_inc(*own.one(qk_taken))
                else:
                    act.activation(nak[:, n - KT, CTX], cx, ACT.Copy).then_inc(*own.one(act_own))
                    act.activation(nak[:, n - KT, LAT], lat, ACT.Copy).then_inc(*own.one(qk_taken))

            for n in range(N_QK):
                qk(n, 0, 0)
            for cg in range(2):
                for b in range(4):
                    act.wait_ge(block_used.sem, S_V1 + 4 * cg + b + 1)
                    high(S_V1 + 4 * cg + b + 2)
                for i in range(0, TILES, 2):
                    act.wait_ge(*own.last())
                    act.activation(nav[:, i, 512 * cg:512 * cg + 512], ps[:, i, :], ACT.Copy).then_inc(*own.one(nav_act))

            def load_bias(hd):
                act.dma_start(nab[:, hd % 2, :, :], na_bias_d[hd]).then_inc(bias_loaded[hd % 2].sem, 16)

            for hd in range(2):
                load_bias(hd)
            N_NA = NA_HEADS * NA_TILES
            for un in range(N_NA + 2):
                if un < N_NA:
                    act.wait_ge(*own.last())
                    act.wait_ge(s_done.sem, un + 1)
                    if un >= 2:
                        act.wait_ge(p_turned.sem, un - 1)
                    act.activation(nas[:, un % 2, 256:512], ps[:, 6 + un % 2, 0:256], ACT.Copy).then_inc(*own.one(s_ctx))
                    act.wait_ge(neg_max.sem, un + 1)
                    act.wait_ge(*own.last())
                    act.activation(nas[:, un % 2, :], nas[:, un % 2, :], ACT.Exp, bias=nast[:, un % 2, 0:1],
                                   accum_out=nast[:, un % 2, 1:2]).then_inc(*own.one(p_exp))
                    if un % NA_TILES == NA_TILES - 1 and un // NA_TILES + 2 < NA_HEADS:
                        hd = un // NA_TILES
                        act.wait_ge(bias_used.sem, hd + 1)
                        load_bias(hd + 2)
                if 1 <= un <= N_NA:
                    e = un - 1
                    act.wait_ge(p_turned.sem, e + 1)
                    act.wait_ge(*own.last())
                    if e >= 2:
                        act.wait_ge(o_done.sem, e - 1)
                    act.activation(nap[:, e % 2, :, :], ps[:, 2 + e % 2, :].rearrange("p (a b) -> p a b", a=4), ACT.Copy)\
                       .then_inc(*own.one(pt_ready))
                if un >= 2 and (un - 2) % 8 == 7:
                    m = (un - 2) // 8
                    act.wait_ge(y_taken.sem, m + 1)
                    act.wait_ge(*own.last())
                    act.activation(u[:, m, 0, LAT], nay[:, m % 2, :], ACT.Copy).then_inc(*own.one(y_hi))
            for m in range(N_OUT):
                act.wait_ge(block_used.sem, S_OUT1 + m + 1)
                high(S_OUT1 + m + 2)
            normalise(norm[3], 3, amod[:, 3], shift(1, 3), ffn[1].out_updated, LAT)
            feed_forward(ffn[1], 1, S_UP1, S_DOWN1, LAT)
            normalise(norm[4], 4, None, None, ffn[1].h_updated, LAT)

        @block.vector
        def _(dve):
            own = Own(dve)

            def take_mod(q):
                dve.wait_ge(mod_done.sem, 16 * (q + 1))
                if q:
                    dve.wait_ge(*own.last())
                bias = vec[:, V_MODB + 16 * q:V_MODB + 16 * q + 16].unsqueeze(2).to_broadcast([P, 16, 2])
                dve.tensor_tensor(modm[:, 16 * q:16 * q + 16, :], ps[:, 7, 0:32].rearrange("p (a b) -> p a b", b=2),
                                  bias, ALU.add).then_inc(*own.one(mod_taken))
                idx = {0: 0, 2: 1, 3: 2, 5: 3}.get(q)
                if idx is not None:
                    layer, ff = idx // 2, idx % 2
                    sc = (layer * MOD_PARTS + 1 + 3 * ff) * KT
                    w0 = (V_NFFN if ff else V_NMIX) + layer * KT
                    w = vec[:, w0:w0 + KT].unsqueeze(2).to_broadcast([P, KT, 2])
                    dve.wait_ge(*own.last())
                    dve.scalar_tensor_tensor(out=amod[:, idx, :, :], in0=modm[:, sc:sc + KT, :], scalar=1.0, in1=w,
                                             op0=ALU.add, op1=ALU.mult).then_inc(*own.one(mod_scaled))

            def normalise(q, last_tok, permute=False, final=False):
                roots = 2 if last_tok != LAT else 1
                dve.wait_ge(q.root_ready.sem, roots)
                if own.newest:
                    dve.wait_ge(*own.last())
                dve.reciprocal(rstd[:, last_tok], rstd[:, last_tok]).then_inc(*own.one(dve_own))
                for k in range(KT + 1):
                    if k < KT:
                        dve.wait_ge(*own.last())
                        if final:
                            dve.scalar_tensor_tensor(out=fout[:, k, :], in0=h[:, k, LAT],
                                                     scalar=vec[:, V_NFIN + k:V_NFIN + k + 1], in1=rstd[:, LAT],
                                                     op0=ALU.mult, op1=ALU.mult).then_inc(*own.one(q.t_ready))
                            continue
                        dve.tensor_tensor(nt[:, k % 2, last_tok], h[:, k, last_tok], rstd[:, last_tok], ALU.mult)\
                           .then_inc(*own.one(q.t_ready))
                    if k >= 1 and not final:
                        e = k - 1
                        dve.wait_ge(q.hi_ready.sem, e + 1)
                        dve.wait_ge(*own.last())
                        if not permute:
                            dve.tensor_tensor(u[:, e, 1, last_tok], nt[:, e % 2, last_tok],
                                              u[:, e, 0, last_tok].bitcast(F32), ALU.subtract)\
                               .then_inc(*own.one(q.lo_ready))
                        else:
                            dve.tensor_tensor(u[:, e, 1, CTX], nt[:, e % 2, CTX],
                                              u[:, e, 0, CTX].bitcast(F32), ALU.subtract).then_inc(*own.one(dve_own))
                            dve.wait_ge(*own.last())
                            grid = lambda t: t.rearrange("p (g r c) -> p r g c", g=8, c=8)
                            dve.tensor_tensor(grid(u[:, e, 1, LAT]),
                                              nt[:, e % 2, LAT].rearrange("p (r g c) -> p r g c", g=8, c=8),
                                              grid(u[:, e, 0, LAT].bitcast(F32)), ALU.subtract)\
                               .then_inc(*own.one(q.lo_ready))

            dve.wait_ge(vec_loaded.sem, 16)
            take_mod(0)
            dve.wait_ge(x_loaded.sem, 16)
            normalise(norm[0], slice(0, N_TOK))

            def running_sum(zp):
                dve.wait_ge(apre_log.sem, zp + 1)
                dve.wait_ge(*own.last())
                dve.scalar_tensor_tensor(out=tmp[:, :], in0=cum[:, zp, :], scalar=0.0, in1=tmp[:, :],
                                         op0=ALU.min, op1=ALU.subtract).then_inc(*own.one(dve_own))
                dve.wait_ge(*own.last())
                if zp < 2:
                    dve.tensor_tensor_scan(cum[:, zp, :], reset[:, 0, 0:N_TOK], tmp[:, :], 0.0, ALU.mult, ALU.add)\
                       .then_inc(*own.one(cum_ready))
                else:
                    dve.tensor_tensor_scan(cum[:, zp, ::-1], reset[:, 0, N_TOK:0:-1], tmp[:, ::-1], 0.0,
                                           ALU.mult, ALU.add).then_inc(*own.one(cum_ready))

            dve.wait_ge(const_loaded.sem, 16 * 6)
            for n in range(1, 13):
                dve.wait_ge(block_used.sem, n + 1)
                dve.wait_ge(*own.last())
                dst = (gqk[:, n - 1, :] if n <= 4 else mqk[:, n - 5, :])[:, LAT]
                cos, sin = (0, 1) if n <= 4 else (2, 3)
                dve.wait_ge(in_act_took.sem, n + 1)
                dve.scalar_tensor_tensor(out=dst, in0=ps[:, n % 2, :], scalar=q_scale(n), in1=rope[:, cos, :],
                                         op0=ALU.mult, op1=ALU.mult).then_inc(*own.one(in_dve_took))
                dve.wait_ge(*own.last())
                dve.scalar_tensor_tensor(out=xs[:, :], in0=xs[:, :], scalar=q_scale(n), in1=rope[:, sin, :],
                                         op0=ALU.mult, op1=ALU.mult).then_inc(*own.one(dve_own))
                dve.wait_ge(*own.last())
                dve.tensor_tensor(dst, dst, xs[:, :], ALU.add).then_inc(*own.one(xs_used))
                if n in (2, 10):
                    running_sum(0 if n == 2 else 2)
                    running_sum(1 if n == 2 else 3)
            for cg, dst in enumerate((gv, mv)):
                dve.wait_ge(block_used.sem, S_V + 4 * cg + 4)
                for i in range(1, TILES, 2):
                    dve.wait_ge(*own.last())
                    dve.tensor_copy(dst[:, i, :], ps[:, i, :]).then_inc(*own.one(v_dve))

            for zp in range(4):
                dve.wait_ge(dec_exp.sem, zp + 1)
                dve.wait_ge(*own.last())
                dve.tensor_tensor(qd[:, zp, :], qd[:, zp, :], gqk[:, zp % 2, :], ALU.mult).then_inc(*own.one(dve_own))
                dve.tensor_tensor(kd[:, zp, :], kd[:, zp, :], gqk[:, 2 + zp % 2, :], ALU.mult)\
                   .then_inc(*own.one(dec_ready))
            dve.wait_ge(*own.last())
            dve.memset(gT[:, :, :, :, :], 0.0).then_inc(*own.one(state_zero))

            def mlstm_rows():
                def step(sig=dve_own):
                    dve.wait_ge(*own.last())
                    return own.one(sig)
                dve.wait_ge(row_ln.sem, 1)
                n = step()
                dve.scalar_tensor_tensor(out=rI[:, :], in0=rB[:, :], scalar=0.0, in1=tmp[0:64, :],
                                         op0=ALU.min, op1=ALU.subtract).then_inc(*n)
                n = step()
                dve.tensor_tensor_scan(rB[0:32, :], reset[0:32, 1, 0:N_TOK], rI[0:32, :], 0.0, ALU.mult, ALU.add)\
                   .then_inc(*n)
                n = step()
                dve.tensor_tensor_scan(rB[32:64, ::-1], reset[32:64, 1, N_TOK:0:-1], rI[32:64, ::-1], 0.0,
                                       ALU.mult, ALU.add).then_inc(*n)
                n = step()
                dve.tensor_tensor(rA[:, :], rA[:, :], rB[:, :], ALU.subtract).then_inc(*n)
                n = step()
                dve.memset(rI[:, :], 0.0).then_inc(*n)
                n = step()
                dve.tensor_copy(rI[0:32, P::P], rB[0:32, P - 1:N_TOK - 1:P]).then_inc(*n)
                for z_i in range(1, TILES):
                    i, before = ORDER[1][z_i], ORDER[1][z_i - 1]
                    n = step()
                    dve.tensor_copy(rI[32:64, P * i + P - 1:P * i + P], rB[32:64, P * before:P * before + 1]).then_inc(*n)
                n = step()
                dve.tensor_tensor_scan(rP[0:32, :], rI[0:32, :], rA[0:32, :], 0.0, ALU.add, ALU.max).then_inc(*n)
                n = step()
                dve.tensor_tensor_scan(rP[32:64, N_CTX - 1::-1], rI[32:64, N_CTX - 1::-1], rA[32:64, N_CTX - 1::-1],
                                       0.0, ALU.add, ALU.max).then_inc(*n)
                n = step()
                dve.tensor_tensor_scan(rP[32:64, N_TOK - 1:N_CTX - 1:-1], rI[32:64, N_TOK - 1:N_CTX - 1:-1],
                                       rA[32:64, N_TOK - 1:N_CTX - 1:-1], rP[32:64, 0:1], ALU.add, ALU.max).then_inc(*n)
                n = step()
                dve.tensor_tensor(rB[:, :], rB[:, :], rP[:, :], ALU.add).then_inc(*n)
                n = step()
                dve.memset(mstart[:, :], 0.0).then_inc(*n)
                for z in range(2):
                    rows = slice(32 * z, 32 * z + 32)
                    end = P - 1 if z == 0 else 0
                    for z_i in range(1, TILES):
                        i, before = ORDER[z][z_i], ORDER[z][z_i - 1]
                        n = step()
                        dve.tensor_copy(mstart[rows, i:i + 1], rB[rows, P * before + end:P * before + end + 1]).then_inc(*n)
                    n = step()
                    dve.tensor_copy(pend[rows, :], rP[rows, end::P]).then_inc(*n)
                by_tile = lambda t: t.rearrange("p (i t) -> p i t", t=P)
                wide = lambda t: t.unsqueeze(2).to_broadcast([64, TILES, P])
                n = step()
                dve.tensor_tensor(by_tile(rI[:, :]), wide(mstart[:, :]), by_tile(rP[:, :]), ALU.subtract).then_inc(*n)
                n = step()
                dve.tensor_tensor(by_tile(tmp[0:64, :]), by_tile(rA[:, :]), wide(pend[:, :]), ALU.subtract).then_inc(*n)
                dve.wait_ge(*own.last())
                dve.tensor_scalar(rP[:, :], rP[:, :], -1.0, None, ALU.mult).then_inc(*own.one(row_args))

            mlstm_rows()
            cm = lambda z, neg: cmask[:, 2 * neg + z, :]
            for un, (n, z, i) in enumerate(UNITS):
                b = un % 2
                dve.wait_ge(ga_done.sem, un + 1)
                dve.wait_ge(*own.last())
                if un >= 2:
                    dve.wait_ge(gi_done.sem, 2 * (un - 1))
                dve.tensor_tensor(gsc[:, b, :, :, :], ps[:, 0:2, 0:2 * P].rearrange("q b (p c) -> q b p c", p=2),
                                  cm(z, 0).unsqueeze(1).unsqueeze(1).to_broadcast([P, 2, GLA_PAIRS, P]), ALU.mult)\
                   .then_inc(*own.one(gsc_ready))
                dve.wait_ge(gkv_done.sem, un + 1)
                for c in range(2):
                    cc = c if z == 0 else 1 - c
                    dve.wait_ge(gS_ready.sem, 2 * un + c + 1)
                    dve.wait_ge(*own.last())
                    for hh in range(2):
                        rows = slice(64 * hh, 64 * hh + 64)
                        dve.tensor_tensor(gT[rows, z, :, hh, :], gS[rows, c, :, hh, :],
                                          ps[rows, 3 + cc, :].rearrange("q (p b c) -> q p b c", p=2, b=2)[:, :, hh, :],
                                          ALU.add).then_inc(*own.one(gT_ready if hh else dve_own))
                dve.wait_ge(gi_done.sem, 2 * un + 2)
                dve.wait_ge(*own.last())
                src = ps[:, 5 + b, :].rearrange("p (a t) -> p a t", a=HEADS)
                dst = gla_o[:, :, tile(i)]
                if FRESH[un]:
                    dve.tensor_copy(dst, src).then_inc(*own.one(go_taken))
                else:
                    dve.tensor_tensor(dst, src, dst, ALU.add).then_inc(*own.one(go_taken))
                if un % 4 == 3:
                    take_mod(1 + un // 4)

            dve.wait_ge(*own.last())
            dve.memset(mC[:, :, :, :], 0.0).then_inc(*own.one(mC_zero))
            for un, (n, z, i) in enumerate(UNITS):
                four = lambda t: t.rearrange("p (a b) -> p a b", a=HEADS)
                dve.wait_ge(ml_lw.sem, un + 1)
                dve.wait_ge(*own.last())
                dve.tensor_tensor(mD[:, :, :], four(ps[:, 0, :]),
                                  cm(z, 1).unsqueeze(1).to_broadcast([P, HEADS, P]), ALU.add)\
                   .then_inc(*own.one(lw_ready))
                dve.wait_ge(ml_iw.sem, un + 1)
                if un >= 1:
                    dve.wait_ge(mh_done.sem, un)
                dve.tensor_tensor(mqs[:, :, :], mqk[:, 0:HEADS, tile(i)], four(ps[:, 2, :]), ALU.mult)\
                   .then_inc(*own.one(mqs_ready))
                dve.wait_ge(*own.last())
                end = P - 1 if z == 0 else 0
                dve.tensor_copy(mdec[:, :], ps[:, 2, end::P]).then_inc(*own.one(iw_taken))
                dve.wait_ge(mD_ready.sem, un + 1)
                dve.wait_ge(ml_sc.sem, un + 1)
                dve.tensor_tensor(msc[:, :, :], four(ps[:, 1, :]), mD[:, :, :], ALU.mult).then_inc(*own.one(msc_ready))
                dve.wait_ge(mkv_done.sem, un + 1)
                dve.wait_ge(mh_done.sem, un + 1)
                dve.wait_ge(*own.last())
                for hd in range(HEADS):
                    dve.scalar_tensor_tensor(out=mC[:, z, hd, :], in0=mC[:, z, hd, :], scalar=mdec[:, hd:hd + 1],
                                             in1=ps[:, 5 + hd // 2, 256 * (hd % 2):256 * (hd % 2) + 256],
                                             op0=ALU.mult, op1=ALU.add)\
                       .then_inc(*own.one(mC_ready if hd == HEADS - 1 else dve_own))
                dve.wait_ge(megs_ready.sem, un + 1)
                dve.wait_ge(*own.last())
                dve.scalar_tensor_tensor(out=mden[:, :, :], in0=four(ps[:, 4, :]), scalar=-1.0, in1=megs[:, :, :],
                                         op0=ALU.mult, op1=ALU.max).then_inc(*own.one(mden_ready))
                dve.wait_ge(*own.last())
                dve.tensor_tensor(mden[:, :, :], four(ps[:, 4, :]), mden[:, :, :], ALU.max).then_inc(*own.one(dve_own))
                dve.wait_ge(*own.last())
                dve.reciprocal(mden[:, :, :], mden[:, :, :]).then_inc(*own.one(dve_own))
                dve.wait_ge(*own.last())
                dst = ml_o[:, :, tile(i)]
                if FRESH[un]:
                    dve.tensor_tensor(dst, four(ps[:, 3, :]), mden[:, :, :], ALU.mult).then_inc(*own.one(mh_taken))
                else:
                    dve.tensor_tensor(mden[:, :, :], four(ps[:, 3, :]), mden[:, :, :], ALU.mult)\
                       .then_inc(*own.one(dve_own))
                    dve.wait_ge(*own.last())
                    dve.tensor_tensor(dst, dst, mden[:, :, :], ALU.add).then_inc(*own.one(mh_taken))
                if un in (3, 7):
                    take_mod(4 + un // 4)

            for f in range(KT):
                o = gla_o[:, f, :] if f < 4 else ml_o[:, f - 4, :]
                w = V_GLAN if f < 4 else V_MLN
                dve.wait_ge(g_root.sem, 2 * (f + 1))
                dve.wait_ge(*own.last())
                dve.reciprocal(grt[:, f % 2, :], grt[:, f % 2, :]).then_inc(*own.one(dve_own))
                dve.wait_ge(*own.last())
                dve.scalar_tensor_tensor(out=gy[:, f % 2, :], in0=o, scalar=vec[:, w:w + 1], in1=grt[:, f % 2, :],
                                         op0=ALU.mult, op1=ALU.mult).then_inc(*own.one(dve_own))
                dve.wait_ge(*own.last())
                dve.tensor_tensor(gy[:, f % 2, :], gy[:, f % 2, :], gates[:, f, :], ALU.mult).then_inc(*own.one(g_y))
                dve.wait_ge(g_hi.sem, f + 1)
                dve.tensor_tensor(u[:, f, 1, :], gy[:, f % 2, :], u[:, f, 0, :].bitcast(F32), ALU.subtract)\
                   .then_inc(*own.one(g_lo))

            def gate_of(layer, part, m, r):
                c = (layer * MOD_PARTS + part) * KT + m
                return modm[:, c, r:r + 1]

            def add_out(q, s0, layer):
                for m in range(N_OUT):
                    dve.wait_ge(block_used.sem, s0 + m + 1)
                    dve.wait_ge(*own.last())
                    if layer == 0:
                        dve.scalar_tensor_tensor(out=h[:, m, CTX], in0=cx_bank(m),
                                                 scalar=gate_of(layer, 2, m, 1), in1=h[:, m, CTX],
                                                 op0=ALU.mult, op1=ALU.add).then_inc(*own.one(dve_own))
                    dve.scalar_tensor_tensor(out=h[:, m, LAT], in0=ps[:, m % 2, :], scalar=gate_of(layer, 2, m, 0),
                                             in1=h[:, m, LAT], op0=ALU.mult, op1=ALU.add)\
                       .then_inc(*own.one(q.out_updated))

            def feed_forward(q, layer, s_up, s_down, toks):
                lo, w = (0, CW) if layer == 0 else (L0C, N_LAT)
                cv = V_CONV + layer * FT * 4
                dve.wait_ge(*own.last())
                for c0 in (0, N_CTX + 1, L0C):
                    dve.memset(apad[:, :, c0:c0 + 1], 0.0).then_inc(*own.one(dve_own))
                dve.memset(apad[:, :, PADW - 1:PADW], 0.0).then_inc(*own.one(q.pad_zero))

                def up(j, i):
                    par = j % 2
                    c = at_(vec, cv + 4 * j, 8 * i)
                    dve.wait_ge(q.c_ready.sem, j + 1 + 2 * i)
                    dve.wait_ge(*own.last())
                    dve.scalar_tensor_tensor(out=conv[:, par, lo:lo + w], in0=apad[:, par, lo:lo + w], scalar=c(0),
                                             in1=conv[:, par, lo:lo + w], op0=ALU.mult, op1=ALU.add)\
                       .then_inc(*own.one(dve_own))
                    dve.wait_ge(*own.last())
                    dve.scalar_tensor_tensor(out=conv[:, par, lo:lo + w], in0=apad[:, par, lo + 2:lo + 2 + w],
                                             scalar=c(2), in1=conv[:, par, lo:lo + w], op0=ALU.mult, op1=ALU.add)\
                       .then_inc(*own.one(q.conv_done))
                    dve.wait_ge(q.gel_ready.sem, j + 1 + 2 * i)
                    dve.wait_ge(block_used.sem, s_up + 2 * j + 2 + 4 * i)
                    if layer == 0:
                        dve.tensor_tensor(hid_at(j, i, CTX, 2), gel[:, par, 0:N_CTX], cx_bank(1), ALU.mult)\
                           .then_inc(*own.one(dve_own))
                    dve.tensor_tensor(hid_at(j, i, LAT, 2), gel[:, par, L0C:L0C + N_LAT], ps[:, 1, :], ALU.mult)\
                       .then_inc(*own.one(q.g_taken))

                for j in range(2):
                    up(j, 0)
                with own.loop((FT - 2) // 2, {q.conv_done: 2, q.g_taken: 2, dve_own: 4 if layer == 0 else 2}) as i:
                    for j in range(2, 4):
                        up(j, i)

                def hidden_low(k, kx, i=0):
                    dve.wait_ge(q.hh_ready.sem, k + 1 + 8 * i)
                    dve.wait_ge(*own.last())
                    dve.tensor_tensor(hsp[:, k % 2, 1, toks], hid_at(kx, i, toks),
                                      hsp[:, k % 2, 0, toks].bitcast(F32), ALU.subtract)\
                       .then_inc(*own.one(q.hl_ready))

                for g in range(2):
                    k0 = FT * g
                    for kx in range(6):
                        hidden_low(k0 + kx, kx)
                    with own.loop((FT - 6) // 8, {q.hl_ready: 8}) as i:
                        for kx in range(6, 14):
                            hidden_low(k0 + kx, kx, i)
                    if g == 1:
                        pass
                    dve.wait_ge(block_used.sem, s_down + FT // 2 * (g + 1))
                    for mm in range(M_GROUP):
                        m = M_GROUP * g + mm
                        dve.wait_ge(*own.last())
                        if layer == 0:
                            dve.scalar_tensor_tensor(out=h[:, m, CTX],
                                                     in0=ps[:, 4 + mm // 2, 256 * (mm % 2):256 * (mm % 2) + 256],
                                                     scalar=gate_of(layer, 5, m, 1), in1=h[:, m, CTX],
                                                     op0=ALU.mult, op1=ALU.add).then_inc(*own.one(dve_own))
                        dve.scalar_tensor_tensor(out=h[:, m, LAT], in0=ps[:, mm, :], scalar=gate_of(layer, 5, m, 0),
                                                 in1=h[:, m, LAT], op0=ALU.mult, op1=ALU.add)\
                           .then_inc(*own.one(q.h_updated))

            dve.wait_ge(x_again.sem, 16)
            add_out(ffn[0], S_OUT0, 0)
            normalise(norm[1], slice(0, N_TOK))
            feed_forward(ffn[0], 0, S_UP0, S_DOWN0, slice(0, N_TOK))
            normalise(norm[2], slice(0, N_TOK), permute=True)

            for cg in range(2):
                dve.wait_ge(block_used.sem, S_V1 + 4 * cg + 4)
                for i in range(1, TILES, 2):
                    dve.wait_ge(*own.last())
                    dve.tensor_copy(nav[:, i, 512 * cg:512 * cg + 512], ps[:, i, :]).then_inc(*own.one(nav_dve))

            N_NA = NA_HEADS * NA_TILES
            for un in range(N_NA + 2):
                if un < N_NA:
                    hd, j = un // NA_TILES, un % NA_TILES
                    x = un % 2
                    if j == 0:
                        dve.wait_ge(bias_loaded[hd % 2].sem, 16 * (hd // 2 + 1))
                    dve.wait_ge(s_done.sem, un + 1)
                    if un >= 2:
                        dve.wait_ge(p_turned.sem, un - 1)
                    dve.wait_ge(*own.last())
                    dve.tensor_tensor(nas[:, x, 0:256], ps[:, x, 0:256], nab[:, hd % 2, j, :], ALU.add)\
                       .then_inc(*own.one(bias_used if j == NA_TILES - 1 else s_lat))
                    dve.wait_ge(s_ctx.sem, un + 1)
                    dve.wait_ge(*own.last())
                    dve.tensor_reduce(nast[:, x, 0:1], nas[:, x, :], AX_X, ALU.max, negate=True)\
                       .then_inc(*own.one(neg_max))
                if un >= 2:
                    e = un - 2
                    hd, j = e // NA_TILES, e % NA_TILES
                    if hd % 2 == 1 and j == NA_TILES - 1:
                        m = hd // 2
                        dve.wait_ge(o_done.sem, e + 1)
                        dve.wait_ge(*own.last())
                        out = ps[:, 4 + m % 2, :].rearrange("p (g r c) -> p r g c", g=8, c=8)
                        dst = nay[:, m % 2, :].rearrange("p (r g c) -> p r g c", g=8, c=8)
                        dve.tensor_copy(dst[:, :, 1:8, :], out[:, :, 0:7, :]).then_inc(*own.one(dve_own))
                        dve.tensor_copy(dst[:, :, 0:1, :], out[:, :, 7:8, :]).then_inc(*own.one(y_taken))
                        dve.wait_ge(y_hi.sem, m + 1)
                        dve.wait_ge(*own.last())
                        dve.tensor_tensor(u[:, m, 1, LAT], nay[:, m % 2, :], u[:, m, 0, LAT].bitcast(F32),
                                          ALU.subtract).then_inc(*own.one(y_lo))
                if un < N_NA:
                    dve.wait_ge(p_exp.sem, un + 1)
                    dve.wait_ge(*own.last())
                    dve.reciprocal(nast[:, x, 2:3], nast[:, x, 1:2]).then_inc(*own.one(dve_own))
                    dve.wait_ge(*own.last())
                    dve.tensor_scalar(nas[:, x, :], nas[:, x, :], nast[:, x, 2:3], None, ALU.mult)\
                       .then_inc(*own.one(p_ready))

            add_out(ffn[1], S_OUT1, 1)
            normalise(norm[3], LAT)
            feed_forward(ffn[1], 1, S_UP1, S_DOWN1, LAT)
            normalise(norm[4], LAT, final=True)

        @block.tensor
        def _(pe):
            own = Own(pe)

            def modulation(m):
                r = mod_raw_index(m)
                pe.wait_ge(raw_loaded[r % 4].sem, 16 * (r // 4 + 1))
                if m == 0:
                    pe.wait_ge(c_ready.sem, 1)
                if m % 16 == 0 and m:
                    pe.wait_ge(mod_taken.sem, m // 16)
                for k in range(KT):
                    mm = pe.matmul(ps[:, 7, 2 * (m % 16):2 * (m % 16) + 2], raw[:, r % 4, tile(k)], cvec[:, k, :],
                                   start=(k == 0), stop=(k == KT - 1))
                mm.then_inc(*own.one(mod_done))

            def normalise(q, last_tok):
                for k in range(KT):
                    pe.wait_ge(q.sq_ready.sem, k + 1)
                    for t, bank, w in ((CTX, q.cx_bank, N_CTX), (LAT, 6, N_LAT)):
                        if t == CTX and last_tok == LAT:
                            continue
                        mm = pe.matmul(ps[:, bank, 0:w], ones[:, :], sq[:, k % 2, t], start=(k == 0), stop=(k == KT - 1))
                    mm.then_inc(*own.one(q.sq_summed))

            PASSES = ((0, 0), (0, 1), (1, 0))

            def features(s, i, lat, cx, x, ready=None):
                pe.wait_ge(lo_ready.sem, s_count(s, i))
                for k in range(KT):
                    if ready is not None:
                        pe.wait_ge(ready.sem, k + 1)
                    for a, (wp, xp) in enumerate(PASSES):
                        w = wsp[:, s % 2, wp, tile(k)]
                        first, last = k == 0 and a == 0, k == KT - 1 and a == 2
                        if cx is not None:
                            pe.matmul(cx, w, x[:, k, xp, CTX], start=first, stop=last)
                        mm = pe.matmul(lat, w, x[:, k, xp, LAT], start=first, stop=last)
                mm.then_inc(*own.one(block_used))

            def tokens(s, b, taken):
                pe.wait_ge(lo_ready.sem, s + 1)
                for kk in range(2):
                    k = 2 * b + kk
                    for i in range(TILES):
                        if k == 0:
                            for q, n in taken:
                                pe.wait_ge(q.sem, n)
                        for a, (wp, xp) in enumerate(PASSES):
                            mm = pe.matmul(ps[:, i, :], u[:, k, xp, tile(i)], wsp[:, s % 2, wp, 512 * kk:512 * kk + 512],
                                           start=(k == 0 and a == 0), stop=(k == KT - 1 and a == 2),
                                           skip_group_check=True)
                mm.then_inc(*own.one(block_used))

            for m in range(MOD_FIRST):
                modulation(m)
            pe.wait_ge(ones_ready.sem, 2)
            pe.wait_ge(mod_taken.sem, 1)
            normalise(norm[0], slice(0, N_TOK))

            def projection(n, i=0):
                if n >= 2:
                    pe.wait_ge(in_act_took.sem, n - 1 + 4 * i)
                if 3 <= n <= 14:
                    pe.wait_ge(in_dve_took.sem, n - 2 + 4 * i)
                features(S_IN + n, i, ps[:, n % 2, :], cx_bank(n), u, norm[0].lo_ready if n == 0 else None)

            def decay_inputs(zp):
                b = 3 + 2 * (zp % 2)
                if zp >= 2:
                    pe.wait_ge(apre_taken.sem, 2 * (zp - 1))
                for t, bank, w in ((LAT, b, N_LAT), (CTX, b + 1, N_CTX)):
                    mm = pe.matmul(ps[:, bank, 0:w], aup[:, zp // 2, tile(zp % 2)], small[:, t], start=True, stop=True)
                mm.then_inc(*own.one(apre_done))

            for n in range(3):
                projection(n)
            pe.wait_ge(const_loaded.sem, 16 * 6)
            for zp in range(2):
                decay_inputs(zp)
            with own.loop(2, {block_used: 4}) as i:
                for n in range(3, 7):
                    projection(n, i)
            for zp in range(2, 4):
                decay_inputs(zp)
            for n in range(11, 15):
                projection(n)
            for n in range(15, N_IN):
                projection(n)

            for cg in range(2):
                taken = [(in_act_took, N_IN), (apre_taken, 8)] if cg == 0 else [(v_act, 3), (v_dve, 3)]
                for b in range(4):
                    tokens(S_V + 4 * cg + b, b, taken)

            pe.wait_ge(v_act.sem, 6)
            pe.wait_ge(v_dve.sem, 6)
            for c, b in ((0, 3), (1, 5)):
                for t, bank, w in ((LAT, b, N_LAT), (CTX, b + 1, N_CTX)):
                    mm = pe.matmul(ps[0:64, bank, 0:w], sel[:, c, :], small[:, t], start=True, stop=True)
                mm.then_inc(*own.one(rows_done))

            pe.wait_ge(dec_ready.sem, 4)
            pe.wait_ge(rows_taken.sem, 4)
            for un, (n, z, i) in enumerate(UNITS):
                if un >= 1:
                    pe.wait_ge(gsc_ready.sem, un)
                    pe.wait_ge(gktok_ready.sem, un)
                for p in range(GLA_PAIRS):
                    zp = 2 * z + p
                    for hh in range(2):
                        rows = slice(64 * hh, 64 * hh + 64)
                        pe.matmul(ps[:, hh, P * p:P * p + P], kd[rows, zp, tile(i)], qd[rows, zp, tile(i)],
                                  start=True, stop=True)
                    mm = pe.transpose(ps[:, 2, P * p:P * p + P], kd[:, zp, tile(i)], ident[:, :])
                mm.then_inc(*own.one(ga_done))
                for m in range(MOD_FIRST + 4 * un, MOD_FIRST + 4 * un + 4):
                    modulation(m)
                pe.wait_ge(gktok_ready.sem, un + 1)
                if un >= 1:
                    pe.wait_ge(gT_ready.sem, 2 * un)
                for cc in range(2):
                    rows = slice(64 * cc, 64 * cc + 64)
                    for p in range(GLA_PAIRS):
                        mm = pe.matmul(ps[:, 3 + cc, 256 * p:256 * p + 256], gktok[rows, un % 2, tile(p)],
                                       gv[rows, i, 256 * p:256 * p + 256], start=True, stop=True)
                mm.then_inc(*own.one(gkv_done))
                pe.wait_ge(gsc_ready.sem, un + 1)
                if un >= 2:
                    pe.wait_ge(go_taken.sem, un - 1)
                for hd in range(HEADS):
                    pe.matmul(ps[:, 5 + un % 2, tile(hd)], gv[:, i, tile(hd)], gsc[:, un % 2, hd % 2, hd // 2, :],
                              start=(hd == 0), stop=False, skip_group_check=True)
                for c in range(2):
                    cc = c if z == 0 else 1 - c
                    pe.wait_ge(gS_ready.sem, 2 * un + c + 1)
                    for hd in range(HEADS):
                        t0 = 64 * cc
                        mm = pe.matmul(ps[:, 5 + un % 2, P * hd + t0:P * hd + t0 + 64], gS[:, c, hd // 2, hd % 2, :],
                                       qd[:, 2 * z + hd // 2, P * i + t0:P * i + t0 + 64],
                                       start=False, stop=(c == 1), skip_group_check=True)
                    mm.then_inc(*own.one(gi_done))

            pe.wait_ge(row_exp.sem, 3)
            pe.wait_ge(go_taken.sem, len(UNITS))
            for i in range(TILES):
                mm = pe.transpose(ps[:, 5, 64 * i:64 * i + 64], tmp[0:64, tile(i)], ident[0:64, 0:64])
            mm.then_inc(*own.one(wend_turned))
            for i in range(TILES):
                if i >= 2:
                    pe.wait_ge(ktok_ready.sem, i - 1)
                for hd in range(HEADS):
                    mm = pe.transpose(ps[:, i % 2, tile(hd)], mqk[:, HEADS + hd, tile(i)], ident[:, :])
                mm.then_inc(*own.one(ktok_turned))
            pe.wait_ge(mC_zero.sem, 1)
            pe.wait_ge(ktok_ready.sem, TILES)
            pe.wait_ge(wend_ready.sem, 1)
            for un, (n, z, i) in enumerate(UNITS):
                row = lambda hd: ident[0:64, 32 * z + hd:32 * z + hd + 1].to_broadcast([64, P])
                if un >= 1:
                    pe.wait_ge(lw_ready.sem, un)
                    pe.wait_ge(msc_ready.sem, un)
                    pe.wait_ge(megs_ready.sem, un)
                for hd in range(HEADS):
                    pe.matmul(ps[:, 0, tile(hd)], row(hd), rP[:, tile(i)], start=True, stop=False)
                    mm = pe.matmul(ps[:, 0, tile(hd)], rA[:, tile(i)], row(hd), start=False, stop=True)
                mm.then_inc(*own.one(ml_lw))
                for hd in range(HEADS):
                    mm = pe.matmul(ps[:, 2, tile(hd)], row(hd), rI[:, tile(i)], start=True, stop=True)
                mm.then_inc(*own.one(ml_iw))
                for hd in range(HEADS):
                    mm = pe.matmul(ps[:, 1, tile(hd)], mqk[:, HEADS + hd, tile(i)], mqk[:, hd, tile(i)],
                                   start=True, stop=True)
                mm.then_inc(*own.one(ml_sc))
                if un < 8:
                    for m in range(MOD_FIRST + 48 + 4 * un, MOD_FIRST + 52 + 4 * un):
                        modulation(m)
                pe.wait_ge(mks_ready.sem, un + 1)
                if un >= 1:
                    pe.wait_ge(mC_ready.sem, un)
                for hd in range(HEADS):
                    kv = ps[:, 5 + hd // 2, 256 * (hd % 2):256 * (hd % 2) + 256]
                    pe.matmul(kv[:, 0:P], mks[:, hd, :], mv[:, i, tile(hd)], start=True, stop=True)
                    mm = pe.matmul(kv[:, P:2 * P], mks[:, hd, :], ones[:, :], start=True, stop=True)
                mm.then_inc(*own.one(mkv_done))
                pe.wait_ge(iw_taken.sem, un + 1)
                for hd in range(HEADS):
                    mm = pe.matmul(ps[:, 2, tile(hd)], row(hd), rB[:, tile(i)], start=True, stop=True)
                mm.then_inc(*own.one(eg_done))
                pe.wait_ge(mqs_ready.sem, un + 1)
                pe.wait_ge(msc_ready.sem, un + 1)
                if un >= 1:
                    pe.wait_ge(mh_taken.sem, un)
                for hd in range(HEADS):
                    pe.matmul(ps[:, 3, tile(hd)], mv[:, i, tile(hd)], msc[:, hd, :], start=True, stop=False)
                    pe.matmul(ps[:, 3, tile(hd)], mC[:, z, hd, 0:P], mqs[:, hd, :], start=False, stop=True)
                    pe.matmul(ps[:, 4, tile(hd)], ones[:, :], msc[:, hd, :], start=True, stop=False)
                    mm = pe.matmul(ps[:, 4, tile(hd)], mC[:, z, hd, P:2 * P], mqs[:, hd, :], start=False, stop=True)
                mm.then_inc(*own.one(mh_done))

            for f in range(KT):
                pe.wait_ge(g_sq.sem, f + 1)
                if f == 0:
                    pe.wait_ge(mh_taken.sem, len(UNITS))
                if f >= 2:
                    pe.wait_ge(g_root.sem, 2 * (f - 1))
                for t, bank, w in ((LAT, 2 * (f % 2), N_LAT), (CTX, 2 * (f % 2) + 1, N_CTX)):
                    mm = pe.matmul(ps[:, bank, 0:w], ones[:, :], gsq[:, f % 2, t], start=True, stop=True)
                mm.then_inc(*own.one(g_sum))

            def out_projection(q, s0, layer, ready):
                pe.wait_ge(ready.sem, KT)
                if layer == 0:
                    pe.wait_ge(g_root.sem, 2 * KT)
                for m in range(N_OUT):
                    if m >= 2:
                        pe.wait_ge(q.out_updated.sem, m - 1)
                    features(s0 + m, 0, ps[:, m % 2, :], cx_bank(m) if layer == 0 else None, u)

            def feed_forward(q, n, layer, s_up, s_down, toks):
                pe.wait_ge(n.lo_ready.sem, KT)

                def up(b, i):
                    if b >= 2:
                        pe.wait_ge((q.g_taken if b % 2 else q.a_taken).sem, b // 2 + 2 * i)
                    features(s_up + b, i, ps[:, b % 2, :], cx_bank(b) if layer == 0 else None, u)

                blocks(own.loop, {block_used: 4}, N_UP, up)

                def down(b, i):
                    g, first = b // (FT // 2), b % (FT // 2) == 0
                    end = b % (FT // 2) == FT // 2 - 1
                    pe.wait_ge(lo_ready.sem, s_count(s_down + b, i))
                    for kk in range(2):
                        pe.wait_ge(q.hl_ready.sem, 2 * b + kk + 1 + 8 * i)
                        for mm_ in range(M_GROUP):
                            if first and kk == 0 and g == 1 and mm_ % 2 == 0:
                                pe.wait_ge(q.h_updated.sem, mm_ + 2)
                            if first and kk == 0 and g == 0 and mm_ == 0:
                                pe.wait_ge(q.g_taken.sem, FT)
                            lat = ps[:, mm_, :]
                            cx = ps[:, 4 + mm_ // 2, 256 * (mm_ % 2):256 * (mm_ % 2) + 256]
                            for a, (wp, xp) in enumerate(PASSES):
                                w = wsp[:, (s_down + b) % 2, wp, 512 * kk + P * mm_:512 * kk + P * mm_ + P]
                                one, last = first and kk == 0 and a == 0, end and kk == 1 and a == 2
                                if layer == 0:
                                    pe.matmul(cx, w, hsp[:, kk, xp, CTX], start=(one and mm_ % 2 == 0), stop=last,
                                              skip_group_check=True)
                                mm = pe.matmul(lat, w, hsp[:, kk, xp, LAT], start=one, stop=last,
                                               skip_group_check=True)
                        if kk == 0:
                            mm.then_inc(*own.one(q.hid_used))
                        else:
                            mm.then_inc(*own.one(block_used))

                half = FT // 2
                for g0 in (0, half):
                    down(g0, 0)
                    with own.loop(2, {block_used: 4, q.hid_used: 4}) as i:
                        for b in range(g0 + 1, g0 + 5):
                            down(b, i)
                    for b in range(g0 + 9, g0 + half):
                        down(b, 0)

            out_projection(ffn[0], S_OUT0, 0, g_lo)
            normalise(norm[1], slice(0, N_TOK))
            feed_forward(ffn[0], norm[1], 0, S_UP0, S_DOWN0, slice(0, N_TOK))
            normalise(norm[2], slice(0, N_TOK))

            pe.wait_ge(norm[2].lo_ready.sem, KT)
            for n in range(N_QK):
                if n >= 2:
                    pe.wait_ge(qk_taken.sem, n - 1)
                features(S_QK + n, 0, ps[:, n % 2, :], cx_bank(n) if n >= KT else None, u)
            for cg in range(2):
                taken = [(qk_taken, N_QK)] if cg == 0 else [(nav_act, 3), (nav_dve, 3)]
                for b in range(4):
                    tokens(S_V1 + 4 * cg + b, b, taken)

            pe.wait_ge(nav_act.sem, 6)
            pe.wait_ge(nav_dve.sem, 6)
            N_NA = NA_HEADS * NA_TILES
            for un in range(N_NA + 2):
                if un < N_NA:
                    hd, j = un // NA_TILES, un % NA_TILES
                    rows, m, x = slice(64 * (hd % 2), 64 * (hd % 2) + 64), hd // 2, un % 2
                    if un >= 2:
                        pe.wait_ge(s_ctx.sem, un - 1)
                        pe.wait_ge(neg_max.sem, un - 1)
                    if j < NA_TILES - 1:
                        keys = nak[rows, m, N_CTX + P * j:N_CTX + P * j + 256]
                        parts = [(slice(0, P), slice(64 * (2 * j + 1), 64 * (2 * j + 3)))]
                    else:
                        keys = nak[rows, m, LAT].rearrange("p (i t) -> p i t", t=P)[:, 0::3, :]
                        parts = [(slice(0, 64), slice(448, 512)), (slice(64, P), slice(0, 64))]
                    for out_rows, cols in parts:
                        pe.matmul(ps[out_rows, x, 0:256], naq[rows, m, cols], keys, start=True, stop=True)
                        mm = pe.matmul(ps[out_rows, 6 + x, 0:256], naq[rows, m, cols], nak[rows, m, CTX],
                                       start=True, stop=True)
                    mm.then_inc(*own.one(s_done))
                if 1 <= un <= N_NA:
                    e = un - 1
                    pe.wait_ge(p_ready.sem, e + 1)
                    if e >= 2:
                        pe.wait_ge(pt_ready.sem, e - 1)
                    for c in range(4):
                        mm = pe.transpose(ps[:, 2 + e % 2, tile(c)], nas[:, e % 2, tile(c)], ident[:, :])
                    mm.then_inc(*own.one(p_turned))
                if un >= 2:
                    e = un - 2
                    hd, j = e // NA_TILES, e % NA_TILES
                    m = hd // 2
                    pe.wait_ge(pt_ready.sem, e + 1)
                    if m >= 2 and hd % 2 == 0 and j == 0:
                        pe.wait_ge(y_taken.sem, m - 1)
                    keys = (2 + j, 3 + j, 0, 1) if j < NA_TILES - 1 else (2, 5, 0, 1)
                    for c, t in enumerate(keys):
                        mm = pe.matmul(ps[64 * (hd % 2):64 * (hd % 2) + 64, 4 + m % 2, tile(j)],
                                       nav[:, t, NA_DH * hd:NA_DH * hd + NA_DH], nap[:, e % 2, c, :],
                                       start=(c == 0), stop=(c == 3))
                    mm.then_inc(*own.one(o_done))

            out_projection(ffn[1], S_OUT1, 1, y_lo)
            normalise(norm[3], LAT)
            feed_forward(ffn[1], norm[3], 1, S_UP1, S_DOWN1, LAT)
            normalise(norm[4], LAT)


def rope_table():
    pos = np.arange(N_LAT)
    row, col = (pos // GRID_W).astype(np.float32), (pos % GRID_W).astype(np.float32)
    out = np.zeros((P, 4, N_LAT), np.float32)
    for a, dh in enumerate((GLA_DK, ML_DH)):
        n = dh // 4
        inv = (np.float32(10000.0) ** (-np.arange(n, dtype=np.float32) / np.float32(n))).astype(np.float32)
        ang = np.concatenate([row[:, None] * inv, col[:, None] * inv], axis=-1).astype(np.float32)
        d = np.arange(P) % dh
        sign = np.where(d < dh // 2, -1.0, 1.0).astype(np.float32)
        out[:, 2 * a] = np.cos(ang).T[d % (dh // 2)]
        out[:, 2 * a + 1] = sign[:, None] * np.sin(ang).T[d % (dh // 2)]
    return out


def reset_table():
    t = np.arange(N_TOK + 1)
    out = np.stack([(t % GLA_CHUNK != 0), (t % P != 0)]).astype(np.float32)
    return np.broadcast_to(out, (P, 2, N_TOK + 1)).copy()


def packed_constants():
    out = np.zeros((P, 6 * P), np.float32)
    out[:, 0:P] = np.eye(P)
    for z in range(2):
        for hd in range(HEADS):
            out[64 + 4 * z + hd, P + 32 * z + hd] = 1.0
            out[96 + 4 * z + hd, P + 64 + 32 * z + hd] = 1.0
    s, t = np.arange(P)[:, None], np.arange(P)[None, :]
    for z in range(2):
        order = (s <= t) if z == 0 else (s >= t)
        out[:, (2 + z) * P:(3 + z) * P] = order & (s // GLA_CHUNK == t // GLA_CHUNK)
        out[:, (4 + z) * P:(5 + z) * P] = np.where(order, 0.0, NEG)
    return out


def bias_places():
    g8 = lambda g: [(r, 8 * g + c) for r in range(GRID_H) for c in range(8)]
    out = np.zeros((NA_TILES, P, 256), np.int64)
    pad = (2 * 8 - 1) * (2 * NA_WIN_W - 1)
    for j in range(NA_TILES):
        qs = [(2 * j + 1) % 8, (2 * j + 2) % 8]
        ks = range(2 * j, 2 * j + 4) if j < NA_TILES - 1 else (0, 1, 6, 7)
        q = np.array([x for g in qs for x in g8(g)])
        k = np.array([x for g in ks for x in g8(g)])
        start = np.clip(q[:, 1] - NA_WIN_W // 2, 0, GRID_W - NA_WIN_W)
        dr = k[None, :, 0] - q[:, None, 0] + 7
        dc = k[None, :, 1] - q[:, None, 1] + NA_WIN_W - 1
        inside = (k[None, :, 1] >= start[:, None]) & (k[None, :, 1] < start[:, None] + NA_WIN_W)
        out[j] = np.where(inside, dr * (2 * NA_WIN_W - 1) + np.clip(dc, 0, 2 * NA_WIN_W - 2), pad)
    return out


def column_blocks(w):
    m = w.shape[1] // P
    return w.reshape(KT, P, m, P).transpose(2, 1, 0, 3).reshape(m, P, BLOCK)


def row_blocks(w):
    k = w.shape[0] // P
    return w.reshape(k // 2, 2, P, 2, 512).transpose(3, 0, 2, 1, 4).reshape(k, P, BLOCK)


def kernel(**inputs):
    import concourse.bacc as bacc
    from concourse.bass_utils import run_bass_kernel_spmd

    g = {k: np.asarray(v) for k, v in inputs.items()}
    tokens = np.concatenate([g["ctx"][0], g["x"][0]], axis=0)
    xT = tokens.T.reshape(KT, P, N_TOK).transpose(1, 0, 2)

    win = g["ev_w_in"][0]
    sizes = (256, 256, 512, 512, 32, 512, 512, 512, 512, 16)
    at = np.concatenate([[0], np.cumsum(sizes)])
    gq, gk, gv, gg, ga, mq, mk, mv, mo, mg = (win[:, a:b] for a, b in zip(at[:-1], at[1:]))
    mg = mg.reshape(D, 2, 2, HEADS)
    gate_cols = np.zeros((D, P), win.dtype)
    for z in range(2):
        gate_cols[:, 32 * z:32 * z + 16] = ga[:, 16 * z:16 * z + 16]
        gate_cols[:, 64 + 4 * z:68 + 4 * z] = mg[:, z, 0]
        gate_cols[:, 96 + 4 * z:100 + 4 * z] = mg[:, z, 1]
    stream = [column_blocks(x) for x in (gate_cols, gq, gk, mq, mk, gg, mo)]
    stream += [row_blocks(np.concatenate([gv, mv], axis=1)), column_blocks(g["ev_w_out"][0])]

    def up(w):
        a, b = column_blocks(w[:, :D_FF]), column_blocks(w[:, D_FF:])
        return np.stack([a, b], axis=1).reshape(2 * FT, P, BLOCK)

    qkv = g["na_w_qkv"][0]
    stream += [up(g["ffn_w_up"][0]), row_blocks(g["ffn_w_down"][0])]
    stream += [column_blocks(qkv[:, :2 * D]), row_blocks(qkv[:, 2 * D:]), column_blocks(g["na_w_out"][0])]
    stream += [up(g["ffn_w_up"][1]), row_blocks(g["ffn_w_down"][1])]
    stream = np.concatenate(stream, axis=0)
    mods = np.concatenate([column_blocks(g["mod_w"][0]), column_blocks(g["mod_w"][1])], axis=0)
    weights = np.concatenate([mods[:MOD_FIRST], stream[:S_OUT0], mods[MOD_FIRST:], stream[S_OUT0:]], axis=0)

    by_part = lambda v: v.reshape(-1, P).T
    vecs = np.zeros((P, V_N), np.float32)
    for l in range(2):
        vecs[:, V_NMIX + KT * l:V_NMIX + KT * l + KT] = by_part(g["norm_mix_w"][l])
        vecs[:, V_NFFN + KT * l:V_NFFN + KT * l + KT] = by_part(g["norm_ffn_w"][l])
        vecs[:, V_MODB + 48 * l:V_MODB + 48 * l + 48] = by_part(g["mod_b"][l])
        cv = np.stack([by_part(g["ffn_conv_w"][l, t]) for t in range(3)] + [by_part(g["ffn_conv_b"][l])], axis=2)
        vecs[:, V_CONV + 4 * FT * l:V_CONV + 4 * FT * l + 4 * FT] = cv.reshape(P, 4 * FT)
    vecs[:, V_NFIN:V_NFIN + KT] = by_part(g["final_norm_w"])
    vecs[:, V_GLAN] = g["gla_norm_w"][0]
    vecs[:, V_MLN] = g["ml_norm_w"][0]
    vecs[:, V_ABIAS:V_ABIAS + 4] = by_part(g["gla_a_bias"][0].reshape(-1))
    for z in range(2):
        vecs[32 * z:32 * z + HEADS, V_GATEB:V_GATEB + 2] = g["ml_gate_bias"][0, z].T
    vecs[:, V_C:V_C + 2 * KT] = np.stack([by_part(g["c"][0]), by_part(g["c_ctx"])], axis=2).reshape(P, 2 * KT)
    a_up = np.zeros((P, 2, 256), np.float32)
    for z in range(2):
        a_up[32 * z:32 * z + 16, z] = g["gla_a_up"][0, z]
    rpb = g["na_rpb"][0].reshape(NA_HEADS, -1)
    rpb = np.concatenate([rpb, np.full((NA_HEADS, 1), NEG, rpb.dtype)], axis=1)
    na_bias = rpb[:, bias_places()].transpose(0, 2, 1, 3)

    arrays = {"in_x": xT, "in_vecs": vecs, "in_consts": packed_constants(), "in_rope": rope_table(),
              "in_reset": reset_table(), "in_aup": a_up, "in_nabias": na_bias, "in_weights": weights}
    arrays = {k: np.ascontiguousarray(v) for k, v in arrays.items()}
    nc = bacc.Bacc("TRN2", target_bir_lowering=False, num_devices=1)
    aps = [nc.dram_tensor(k, a.shape, mybir.dt.from_np(a.dtype), kind="ExternalInput").ap() for k, a in arrays.items()]
    out = nc.dram_tensor("out_0", (P, KT, N_LAT), F32, kind="ExternalOutput").ap()
    build(nc, *aps, out)
    r = run_bass_kernel_spmd(nc, [arrays], core_ids=[0])
    y = r.results[0]["out_0"]
    return y.transpose(1, 0, 2).reshape(D, N_LAT).T.reshape(1, N_LAT, D)
```

```python
from contextlib import ExitStack, contextmanager

import numpy as np

import concourse.bass as bass
from concourse import mybir

ALU = mybir.AluOpType
ACT = mybir.ActivationFunctionType
AX_X = mybir.AxisListType.X
F32 = mybir.dt.float32
F32R = mybir.dt.float32r

P = 128
D = 1024
KT = D // P
N_CTX, N_LAT = 256, 512
N_TOK = N_CTX + N_LAT
CTX, LAT = slice(0, N_CTX), slice(N_CTX, N_TOK)
TILES = N_TOK // P
GRID_W, GRID_H = 64, N_LAT // 64
EPS = 1e-6

GLA_CHUNK = 64
GLA_DK, ML_DH = 64, 128
HEADS = 4
GLA_PAIRS = HEADS // 2
GLA_TAU = 16.0

NA_HEADS, NA_DH = 16, 64
NA_WIN_W = 16
NA_TILES = N_LAT // P

D_FF = ((8 * D // 3 + 255) // 256) * 256
FT = D_FF // P
M_GROUP = 4

BLOCK = 1024
RAW_SLOTS, SPLIT_SLOTS = 4, 2
N_IN, N_V, N_OUT, N_UP, N_DOWN, N_QK = 21, 8, 8, 2 * FT, FT, 16
S_IN = 0
S_V = S_IN + N_IN
S_OUT0 = S_V + N_V
S_UP0 = S_OUT0 + N_OUT
S_DOWN0 = S_UP0 + N_UP
S_QK = S_DOWN0 + N_DOWN
S_V1 = S_QK + N_QK
S_OUT1 = S_V1 + N_V
S_UP1 = S_OUT1 + N_OUT
S_DOWN1 = S_UP1 + N_UP
S_END = S_DOWN1 + N_DOWN
MOD_PARTS = 6
MOD_TILES = 2 * MOD_PARTS * KT
MOD_FIRST = 2 * KT
S_MIX = MOD_TILES - MOD_FIRST
S_NO_CTX = 8 * KT - MOD_FIRST
assert S_MIX % 4 == 0 and S_UP0 + 40 < S_MIX < S_DOWN0
NEG = -1e30

V_NMIX, V_NFFN, V_NFIN = 0, 16, 32
V_MODB = 40
V_GLAN, V_MLN = V_MODB + MOD_TILES, V_MODB + MOD_TILES + 1
V_ABIAS = V_MLN + 1
V_CONV = V_ABIAS + 4
V_GATEB = V_CONV + 2 * FT * 4
V_N = V_GATEB + 2


def raw_index(s):
    return MOD_FIRST + 2 * s if s < S_MIX else MOD_TILES + s


def raw_turn(s):
    return 8 if s < S_MIX else 4


def q_scale(n):
    return GLA_DK ** -0.5 if n in (1, 2) else ML_DH ** -0.5 if n >= 9 else 1.0


def mod_raw_index(m):
    return m if m < MOD_FIRST else 2 * m - MOD_FIRST + 1


class Signal:

    def __init__(self, sem):
        self.sem, self.base, self.k, self.per, self.i = sem, 0, 0, 0, 0

    def count(self):
        return self.base + self.k + self.per * self.i if self.per else self.base + self.k


class Own:

    def __init__(self, eng):
        self.eng, self.newest = eng, None

    def one(self, signal):
        signal.k += 1
        self.newest = signal
        return signal.sem, 1

    def last(self):
        return self.newest.sem, self.newest.count()

    @contextmanager
    def loop(self, trips, per):
        self.eng.wait_ge(*self.last())
        with self.eng.Fori(0, trips) as i:
            for s, n in per.items():
                s.base, s.k, s.per, s.i = s.base + s.k, 0, n, i
            yield i
            self.eng.wait_ge(*self.last())
        for s, n in per.items():
            assert s.k == n, (s.sem, s.k, n)
            s.base, s.k, s.per, s.i = s.base + n * trips, 0, 0, 0


def build(nc, xT, vecs, consts_d, rope_d, reset_d, a_up_d, na_bias_d, c_rows, weights, outT):
    ctx = ExitStack()
    with ctx:
        SB0 = 16512
        T = N_TOK * 4
        place = [SB0]

        def at(name, shape, off, dt=F32):
            assert off % 32 == 0
            return nc.alloc_sbuf_tensor_at(name, shape, dt, offset=off)

        def take(name, shape, dt=F32):
            n = 4
            for x in shape[1:]:
                n *= x
            t = at(name, shape, place[0], dt)
            place[0] += (n + 31) // 32 * 32
            return t

        h_off = place[0]
        h = take("h", [P, KT, N_TOK])
        gates = at("gates", [P, KT, N_TOK], h_off)
        u_off = place[0]
        u = take("u", [P, KT, 2, N_TOK], F32R)
        raw = take("raw", [P, RAW_SLOTS, BLOCK])
        wsp = take("wsp", [P, SPLIT_SLOTS, 2, BLOCK], F32R)
        ident = take("ident", [P, P])
        ones = take("ones", [P, P])
        vec = take("vec", [P, V_N])
        modm = take("modm", [P, MOD_TILES, 2])
        amod = take("amod", [P, 4, KT, 2])
        epsc = take("epsc", [P, 1])
        mdec = take("mdec", [P, 2, HEADS])
        mstart = take("mstart", [64, TILES])
        pend = take("pend", [64, TILES])
        ar = place[0]
        AR_END = 229344

        sq = at("sq", [P, 2, N_TOK], ar)
        nt = at("nt", [P, 2, N_TOK], ar + 2 * T)
        rstd = at("rstd", [P, N_TOK], ar + 4 * T)
        fout = at("fout", [P, KT, N_LAT], ar + 5 * T)
        gqk = at("gqk", [P, 4, N_TOK], ar)
        gv = at("gv", [P, TILES, 512], ar + 4 * T)
        mqk = at("mqk", [P, 8, N_TOK], ar + 8 * T)
        mv = at("mv", [P, TILES, 512], ar + 16 * T)
        o0 = ar + 20 * T
        small = at("small", [P, N_TOK], o0)
        tmp = at("tmp", [P, N_TOK], o0 + T)
        reset = at("reset", [P, 2, N_TOK + 1], o0 + 2 * T)
        o1 = o0 + 2 * T + 6176
        cmask = at("cmask", [P, 4, P], o1)
        sel = at("sel", [P, 2, 64], o1 + 2048)
        aup = at("aup", [P, 2, 256], o1 + 2560)
        wend = at("wend", [P, TILES, 64], o1 + 4608)
        gdec = at("gdec", [P, 4, N_TOK // GLA_CHUNK], o1 + 6144)
        o2 = o1 + 6336
        rope = at("rope", [P, 4, N_LAT], o2)
        xs = at("xs", [P, N_LAT], o2 + 8192)
        cum = at("cum", [P, 4, N_TOK], o2 + 10240)
        assert o2 + 10240 + 4 * T <= AR_END
        qd = at("qd", [P, 4, N_TOK], u_off)
        kd = at("kd", [P, 4, N_TOK], u_off + 4 * T)
        gla_o = at("gla_o", [P, HEADS, N_TOK], u_off + 12 * T)
        gsc = at("gsc", [P, 2, 2, GLA_PAIRS, P], o2)
        gktok = at("gktok", [P, 2, 2 * P], o2 + 4096)
        gT = at("gT", [P, 2, GLA_PAIRS, 2, P], o2 + 6144)
        gS = at("gS", [P, 2, 2, GLA_PAIRS, 2, P], o2 + 10240)
        rA = at("rA", [64, N_TOK], u_off + 8 * T)
        rB = at("rB", [64, N_TOK], u_off + 9 * T)
        rP = at("rP", [64, N_TOK], u_off + 10 * T)
        rI = at("rI", [64, N_TOK], u_off + 11 * T)
        mktok = at("mktok", [P, TILES, 512], u_off)
        ml_o = at("ml_o", [P, HEADS, N_TOK], ar)
        mD = at("mD", [P, 2, HEADS, P], o2)
        msc = at("msc", [P, 2, HEADS, P], o2 + 4096)
        mqs = at("mqs", [P, 2, HEADS, P], o2 + 8192)
        mC = at("mC", [P, 2, HEADS, 2 * P], o2 + 12288)
        mks = at("mks", [P, 2, HEADS, P], u_off + 4 * T)
        megs = at("megs", [P, 2, HEADS, P], u_off + 4 * T + 4096)
        mden = at("mden", [P, HEADS, P], u_off + 4 * T + 8192)
        assert o2 + 12288 + 8192 <= AR_END
        c_early = at("c_early", [P, 2, D], ar + 16 * T)
        c_late = at("c_late", [P, 2, D], ar + FT * T + 18528)
        left_early = at("left_early", [P, D], ar + 16 * T + 8192)
        left_late = at("left_late", [P, D], ar + FT * T + 18528 + 8192)
        gsq = at("gsq", [P, 2, N_TOK], ar + 4 * T)
        grt = at("grt", [P, 2, N_TOK], ar + 6 * T)
        gy = at("gy", [P, 2, N_TOK], ar + 8 * T)
        PADW = N_TOK + 4
        CW = N_TOK + 2
        L0C = N_CTX + 2
        hid = at("hid", [P, FT, N_TOK], ar)
        f0 = ar + FT * T
        apad = at("apad", [P, 2, PADW], f0)
        conv = at("conv", [P, 2, CW], f0 + 6176)
        gel = at("gel", [P, 2, CW], f0 + 12352)
        hsp = at("hsp", [P, 2, 2, N_TOK], f0 + 18528, F32R)
        assert f0 + 18528 + 4 * T <= AR_END
        naq = at("naq", [P, KT, N_LAT], ar)
        nak = at("nak", [P, KT, N_TOK], ar + 16384)
        nav = at("nav", [P, TILES, D], ar + 16384 + 8 * T)
        n0 = ar + 16384 + 16 * T
        nab = at("nab", [P, 2, NA_TILES, 256], n0)
        nas = at("nas", [P, 4, 512], n0 + 8192)
        nap = at("nap", [P, 2, 4, P], n0 + 16384)
        nay = at("nay", [P, 2, N_LAT], n0 + 20480)
        nast = at("nast", [P, 4, 4], n0 + 24576)
        assert n0 + 24640 <= AR_END

        ps = ctx.enter_context(nc.psum_tensor("ps", [P, 8, 512], F32))

        def sem(name):
            return Signal(ctx.enter_context(nc.semaphore(name)))

        vec_loaded, x_loaded, const_loaded, x_again, out_stored, c_loaded, c_again = map(
            sem, ("vec_loaded", "x_loaded", "const_loaded", "x_again", "out_stored", "c_loaded", "c_again"))
        raw_loaded = [sem(f"raw_loaded{i}") for i in range(RAW_SLOTS)]
        bias_loaded = [sem(f"bias_loaded{i}") for i in range(2)]
        hi_ready, lo_ready, block_used = map(sem, ("hi_ready", "lo_ready", "block_used"))
        mod_done = sem("mod_done")
        act_own, dve_own, pool_own = map(sem, ("act_own", "dve_own", "pool_own"))
        ones_ready, c_ready, pre_ready = map(sem, ("ones_ready", "c_ready", "pre_ready"))

        class Norm:
            def __init__(self, n):
                self.cx_bank = 5 if n == 1 else 7
                self.sq_ready = sem(f"norm{n}_sq_ready")
                self.sq_summed = sem(f"norm{n}_sq_summed")
                self.root_ready = sem(f"norm{n}_root_ready")
                self.t_ready = sem(f"norm{n}_t_ready")
                self.hi_ready = sem(f"norm{n}_hi_ready")
                self.lo_ready = sem(f"norm{n}_lo_ready")
        norm = [Norm(n) for n in range(5)]
        (in_act_took, in_dve_took, xs_used, apre_done, apre_taken, apre_log, cum_ready, v_act, v_dve,
         rows_done, rows_taken, row_abs, row_ln, row_lf, row_args, row_exp, wend_turned, wend_ready,
         dec_exp, dec_ready, state_zero) = map(sem, (
             "in_act_took", "in_dve_took", "xs_used", "apre_done", "apre_taken", "apre_log", "cum_ready", "v_act",
             "v_dve", "rows_done", "rows_taken", "row_abs", "row_ln", "row_lf", "row_args", "row_exp",
             "wend_turned", "wend_ready", "dec_exp", "dec_ready", "state_zero"))
        ga_done, gsc_ready, gktok_ready, gkv_done, gS_ready, gT_ready, gi_done, go_taken = map(sem, (
            "ga_done", "gsc_ready", "gktok_ready", "gkv_done", "gS_ready", "gT_ready", "gi_done", "go_taken"))
        ktok_turned, ktok_ready, mC_zero = map(sem, ("ktok_turned", "ktok_ready", "mC_zero"))
        ml_lw, ml_sc, ml_iw, lw_ready, mD_ready, mqs_ready, iw_taken, msc_ready, mks_ready = map(sem, (
            "ml_lw", "ml_sc", "ml_iw", "lw_ready", "mD_ready", "mqs_ready", "iw_taken", "msc_ready", "mks_ready"))
        eg_done, megs_ready, mkv_done, mC_ready, mh_done, mden_ready, mh_taken = map(sem, (
            "eg_done", "megs_ready", "mkv_done", "mC_ready", "mh_done", "mden_ready", "mh_taken"))
        g_sq, g_sum, g_root, g_y, g_hi, g_lo = map(sem, ("g_sq", "g_sum", "g_root", "g_y", "g_hi", "g_lo"))

        class Ffn:
            def __init__(self, n):
                self.pad_zero = sem(f"ffn{n}_pad_zero")
                self.a_taken = sem(f"ffn{n}_a_taken")
                self.c_ready = sem(f"ffn{n}_c_ready")
                self.conv_done = sem(f"ffn{n}_conv_done")
                self.gel_ready = sem(f"ffn{n}_gel_ready")
                self.g_taken = sem(f"ffn{n}_g_taken")
                self.hh_ready = sem(f"ffn{n}_hh_ready")
                self.hl_ready = sem(f"ffn{n}_hl_ready")
                self.hid_used = sem(f"ffn{n}_hid_used")
                self.h_updated = sem(f"ffn{n}_h_updated")
                self.out_updated = sem(f"ffn{n}_out_updated")
        ffn = [Ffn(n) for n in range(2)]
        (qk_taken, nav_act, nav_dve, s_done, s_ctx, s_lat, neg_max, p_exp, p_ready, p_turned, pt_ready,
         o_done, y_taken, y_hi, y_lo, bias_used) = map(sem, (
             "qk_taken", "nav_act", "nav_dve", "s_done", "s_ctx", "s_lat", "neg_max", "p_exp", "p_ready",
             "p_turned", "pt_ready", "o_done", "y_taken", "y_hi", "y_lo", "bias_used"))

        ORDER = [list(range(TILES)), [1, 0, 5, 4, 3, 2]]
        UNITS = [(n, z, ORDER[z][n]) for n in range(TILES) for z in range(2)]
        seen, FRESH = set(), []
        for _, _, i in UNITS:
            FRESH.append(i not in seen)
            seen.add(i)

        def tile(i):
            return slice(P * i, P * i + P)

        def halves(t):
            return ((CTX, 1), (LAT, 0))

        def blocks(eng_loop, per, count, body, first=4, last=0):
            for n in range(min(first, count)):
                body(n, 0)
            turns = (count - first - last) // 4
            if turns > 0:
                with eng_loop(turns, per) as i:
                    for n in range(first, first + 4):
                        body(n, i)
            for n in range(first + 4 * max(turns, 0), count):
                body(n, 0)

        def kv_bank(un, c):
            return (3, 4, 7)[(2 * un + c) % 3]

        def s_count(s, i):
            return s + 4 * i + 1

        def at_(t, col, off):
            if isinstance(off, int):
                return lambda n: t[:, col + off + n:col + off + n + 1]
            return lambda n: t[:, bass.ds(off + (col + n), 1)]

        def hid_at(k, i, toks, step=8):
            if isinstance(i, int):
                return hid[:, k + step * i, toks]
            return hid[:, bass.ds(i * step + k, 1), toks].rearrange("p a n -> p (a n)")

        def cx_bank(n):
            return ps[:, 2 if n % 2 == 0 else 7, 0:N_CTX]

        block = ctx.enter_context(nc.Block())

        @block.sync
        def _(sp):
            sp.dma_start(c_early[:, :, :], c_rows).then_inc(c_loaded.sem, 16)

            def load(r, i, used, least, turn=4):
                if used is not None:
                    sp.wait_ge(used.sem, least + 4 * i)
                src = weights[r] if isinstance(i, int) else \
                    weights[bass.ds(i * turn + r, 1), :, :].rearrange("a p n -> (a p) n")
                sp.dma_start(raw[:, r % 4, :], src).then_inc(raw_loaded[r % 4].sem, 16)

            def run(a, b, used, least):
                turns = (b - a) // 4
                if turns > 1:
                    with sp.Fori(0, turns) as i:
                        for n in range(4):
                            load(a + n, i, used, least + n)
                    a, least = a + 4 * turns, least + 4 * turns
                for n in range(b - a):
                    load(a + n, 0, used, least + n)

            for r in range(RAW_SLOTS):
                load(r, 0, None, 0)
            sp.dma_start(vec[:, :], vecs).then_inc(vec_loaded.sem, 16)
            sp.dma_start(h[:, :, :], xT).then_inc(x_loaded.sem, 16)
            run(RAW_SLOTS, MOD_FIRST, mod_done, 1)
            sp.dma_start(ident[:, :], consts_d[:, 0:P]).then_inc(const_loaded.sem, 16)
            sp.dma_start(rope[:, :, :], rope_d).then_inc(const_loaded.sem, 16)
            sp.dma_start(sel[:, :, :], consts_d[:, P:2 * P].rearrange("p (a b) -> p a b", a=2)).then_inc(const_loaded.sem, 16)
            sp.dma_start(cmask[:, :, :], consts_d[:, 2 * P:6 * P].rearrange("p (a b) -> p a b", a=4)).then_inc(const_loaded.sem, 16)
            sp.dma_start(reset[:, :, :], reset_d).then_inc(const_loaded.sem, 16)
            sp.dma_start(aup[:, :, :], a_up_d).then_inc(const_loaded.sem, 16)
            for s in range(2):
                load(raw_index(s), 0, mod_done, MOD_FIRST - 3 + 2 * s)
                load(raw_index(s) + 1, 0, mod_done, MOD_FIRST - 2 + 2 * s)
            for s in range(2, 4):
                load(raw_index(s), 0, lo_ready, s - 1)
                load(raw_index(s) + 1, 0, mod_done, MOD_FIRST + s - 1)
            with sp.Fori(0, (S_MIX - 4) // 4) as i:
                for s in range(4, 8):
                    load(raw_index(s), i, lo_ready, s - 1, turn=8)
                    load(raw_index(s) + 1, i, mod_done, MOD_FIRST + s - 1, turn=8)
            for s in range(S_MIX, S_MIX + 4):
                if s % 2 == 0:
                    load(raw_index(s), 0, lo_ready, S_MIX - 1 + (s - S_MIX) // 2)
                else:
                    load(raw_index(s), 0, mod_done, MOD_TILES - 1 + (s - S_MIX) // 2)
            run(raw_index(S_MIX + 4), raw_index(S_END), lo_ready, S_MIX + 1)
            for k in range(KT):
                sp.wait_ge(norm[4].t_ready.sem, k + 1)
                sp.dma_start(outT[:, k, :], fout[:, k, :]).then_inc(out_stored.sem, 16)
            sp.wait_ge(out_stored.sem, 16 * KT)

        @block.gpsimd
        def _(pool):
            own = Own(pool)
            pool.memset(ones[:, :], 1.0).then_inc(*own.one(ones_ready))
            pool.memset(epsc[:, :], EPS).then_inc(*own.one(ones_ready))

            def low(s, i):
                pool.wait_ge(*own.last())
                pool.wait_ge(hi_ready.sem, s_count(s, i))
                pool.tensor_tensor(wsp[:, s % 2, 1, :], raw[:, raw_index(s) % 4, :],
                                   wsp[:, s % 2, 0, :].bitcast(F32), ALU.subtract).then_inc(*own.one(lo_ready))

            blocks(own.loop, {lo_ready: 4}, S_MIX, low)
            blocks(own.loop, {lo_ready: 4}, S_END - S_MIX, lambda n, i: low(S_MIX + n, i))

        @block.scalar
        def _(act):
            own = Own(act)

            def high(s, i=0):
                if isinstance(i, int):
                    if s + 4 * i >= S_END:
                        return
                act.wait_ge(*own.last())
                raw_s = raw_index(s)
                act.wait_ge(raw_loaded[raw_s % 4].sem, 16 * (raw_s // 4 + 1) + 4 * raw_turn(s) * i)
                if s >= 2:
                    act.wait_ge(block_used.sem, s_count(s, i) - 2)
                act.activation(wsp[:, s % 2, 0, :], raw[:, raw_s % 4, :], ACT.Copy).then_inc(*own.one(hi_ready))

            act.wait_ge(c_loaded.sem, 16)
            act.activation(c_early[:, :, :], c_early[:, :, :], ACT.Silu).then_inc(*own.one(c_ready))

            def normalise(q, idx, A, B, updated, last_tok, permute=False):
                for k in range(KT):
                    act.wait_ge(*own.last())
                    if updated is not None:
                        act.wait_ge(updated.sem, k + 1 if updated is not x_loaded else 16)
                    if k >= 2:
                        act.wait_ge(q.sq_summed.sem, k - 1)
                    act.activation(sq[:, k % 2, last_tok], h[:, k, last_tok], ACT.Square)\
                       .then_inc(*own.one(q.sq_ready))
                act.wait_ge(ones_ready.sem, 2)
                act.wait_ge(q.sq_summed.sem, KT)
                for t, bank, w in ((LAT, 6, N_LAT), (CTX, q.cx_bank, N_CTX)):
                    if t == CTX and last_tok == LAT:
                        continue
                    act.wait_ge(*own.last())
                    act.activation(rstd[:, t], ps[:, bank, 0:w], ACT.Sqrt, bias=epsc[:, 0:1], scale=1.0 / D)\
                       .then_inc(*own.one(q.root_ready))
                if A is None:
                    return
                for k in range(KT):
                    act.wait_ge(q.t_ready.sem, k + 1)
                    act.wait_ge(*own.last())
                    if last_tok != LAT:
                        act.activation(u[:, k, 0, CTX], nt[:, k % 2, CTX], ACT.Identity, bias=B(k, 1))\
                           .then_inc(*own.one(act_own))
                    dst, src = u[:, k, 0, LAT], nt[:, k % 2, LAT]
                    if permute:
                        dst = dst.rearrange("p (g r c) -> p r g c", g=8, c=8)
                        src = src.rearrange("p (r g c) -> p r g c", g=8, c=8)
                    act.activation(dst, src, ACT.Identity, bias=B(k, 0)).then_inc(*own.one(q.hi_ready))

            def shift(layer, part):
                return lambda k, r: modm[:, (layer * MOD_PARTS + part) * KT + k, r:r + 1]

            act.wait_ge(vec_loaded.sem, 16)
            high(0)
            high(1)
            normalise(norm[0], 0, amod[:, 0], shift(0, 0), x_loaded, slice(0, N_TOK))

            def log_sigmoid_parts(src_abs, rows, out_signal):
                act.wait_ge(*own.last())
                act.activation(tmp[0:rows, :], src_abs, ACT.Abs).then_inc(*own.one(act_own))
                act.wait_ge(*own.last())
                act.activation(tmp[0:rows, :], tmp[0:rows, :], ACT.Exp, scale=-1.0).then_inc(*own.one(act_own))
                act.wait_ge(*own.last())
                act.activation(tmp[0:rows, :], tmp[0:rows, :], ACT.Ln, bias=1.0).then_inc(*own.one(out_signal))

            def decay_logs(zp):
                b = 3 + 2 * (zp % 2)
                act.wait_ge(apre_done.sem, zp + 1)
                for t, bank, w in ((LAT, b, N_LAT), (CTX, b + 1, N_CTX)):
                    act.wait_ge(*own.last())
                    act.activation(cum[:, zp, t], ps[:, bank, 0:w], ACT.Identity,
                                   bias=vec[:, V_ABIAS + zp:V_ABIAS + zp + 1]).then_inc(*own.one(apre_taken))
                if zp:
                    act.wait_ge(cum_ready.sem, zp)
                log_sigmoid_parts(cum[:, zp, :], P, apre_log)

            act.wait_ge(const_loaded.sem, 16 * 6)
            for n in range(N_IN):
                act.wait_ge(block_used.sem, n + 1)
                high(n + 2)
                lat, cx = ps[:, n % 2, :], cx_bank(n)
                act.wait_ge(*own.last())
                if n == 0:
                    act.activation(small[:, CTX], cx, ACT.Copy).then_inc(*own.one(act_own))
                    act.activation(small[:, LAT], lat, ACT.Copy).then_inc(*own.one(in_act_took))
                elif n <= 12:
                    dst = gqk[:, n - 1, :] if n <= 4 else mqk[:, n - 5, :]
                    half = GLA_DK // 2 if n <= 4 else ML_DH // 2
                    act.activation(dst[:, CTX], cx, ACT.Copy, scale=q_scale(n)).then_inc(*own.one(act_own))
                    if n >= 2:
                        act.wait_ge(xs_used.sem, n - 1)
                    for a in range(0, P, half):
                        b = a ^ half
                        last = a + half == P
                        act.activation(xs[a:a + half, :], ps[b:b + half, n % 2, :], ACT.Copy)\
                           .then_inc(*own.one(in_act_took if last else act_own))
                else:
                    f = n - 13
                    func = ACT.Silu if f < 4 else ACT.Sigmoid
                    act.activation(gates[:, f, CTX], cx, func).then_inc(*own.one(act_own))
                    act.activation(gates[:, f, LAT], lat, func).then_inc(*own.one(in_act_took))
                if n in (2, 10):
                    decay_logs(0 if n == 2 else 2)
                    decay_logs(1 if n == 2 else 3)
            for cg, dst in enumerate((gv, mv)):
                for b in range(4):
                    act.wait_ge(block_used.sem, S_V + 4 * cg + b + 1)
                    high(S_V + 4 * cg + b + 2)
                if cg == 1:
                    act.wait_ge(mod_done.sem, MOD_FIRST + S_OUT0)
                for i in range(0, TILES, 2):
                    act.wait_ge(*own.last())
                    act.activation(dst[:, i, :], ps[:, i, :], ACT.Copy).then_inc(*own.one(v_act))

            for zp in range(4):
                act.wait_ge(cum_ready.sem, 4)
                act.wait_ge(*own.last())
                act.activation(qd[:, zp, :], cum[:, zp, :], ACT.Exp, scale=1.0 / GLA_TAU).then_inc(*own.one(act_own))
                act.activation(kd[:, zp, :], cum[:, zp, :], ACT.Exp, scale=-1.0 / GLA_TAU).then_inc(*own.one(act_own))
                end = GLA_CHUNK - 1 if zp < 2 else 0
                act.activation(gdec[:, zp, :], cum[:, zp, end::GLA_CHUNK], ACT.Exp, scale=1.0 / GLA_TAU)\
                   .then_inc(*own.one(dec_exp))

            act.wait_ge(rows_done.sem, 2)
            for row, b, col in ((rA, 3, 0), (rB, 5, 1)):
                for t, bank, w in ((LAT, b, N_LAT), (CTX, b + 1, N_CTX)):
                    act.wait_ge(*own.last())
                    act.activation(row[:, t], ps[0:64, bank, 0:w], ACT.Identity,
                                   bias=vec[0:64, V_GATEB + col:V_GATEB + col + 1]).then_inc(*own.one(rows_taken))
            act.wait_ge(cum_ready.sem, 4)
            log_sigmoid_parts(rB[:, :], 64, row_ln)

            def row_exps():
                act.wait_ge(row_args.sem, 1)
                act.wait_ge(*own.last())
                act.activation(rI[:, :], rI[:, :], ACT.Exp).then_inc(*own.one(row_exp))
                act.activation(tmp[0:64, :], tmp[0:64, :], ACT.Exp).then_inc(*own.one(row_exp))
                act.activation(rB[:, :], rB[:, :], ACT.Exp, scale=-1.0).then_inc(*own.one(row_exp))

            def keys_turned(un):
                act.wait_ge(ga_done.sem, un + 1)
                act.wait_ge(*own.last())
                if un >= 2:
                    act.wait_ge(gkv_done.sem, 2 * (un - 1))
                act.activation(gktok[:, un % 2, :], ps[:, 2, 0:2 * P], ACT.Copy).then_inc(*own.one(gktok_ready))

            keys_turned(0)
            act.wait_ge(state_zero.sem, 1)
            for un, (n, z, i) in enumerate(UNITS):
                if un + 1 < len(UNITS):
                    keys_turned(un + 1)
                for c in range(2):
                    if c == 1:
                        before = 2 * i + (0 if z == 0 else 1)
                    else:
                        j = ORDER[z][n - 1] if n else i
                        before = 2 * j + (1 if z == 0 else 0)
                    if un >= 2:
                        act.wait_ge(gi_done.sem, 2 * (un - 2) + c + 1)
                        act.wait_ge(gT_ready.sem, 2 * (un - 1))
                    if c == 1:
                        act.wait_ge(gT_ready.sem, 2 * un + 1)
                    act.wait_ge(*own.last())
                    for p in range(GLA_PAIRS):
                        zp = 2 * z + p
                        act.activation(gS[:, z, c, p, :, :], gT[:, z, p, :, :], ACT.Copy,
                                       scale=gdec[:, zp, before:before + 1])\
                           .then_inc(*own.one(gS_ready if p else act_own))
                if un == 6:
                    row_exps()

            act.wait_ge(wend_turned.sem, 1)
            act.wait_ge(*own.last())
            act.activation(wend[:, :, :], ps[:, 5, 0:TILES * 64].rearrange("p (i r) -> p i r", r=64), ACT.Copy)\
               .then_inc(*own.one(wend_ready))
            for i in range(TILES):
                act.wait_ge(ktok_turned.sem, i + 1)
                act.wait_ge(*own.last())
                act.activation(mktok[:, i, :], ps[:, i % 2, :], ACT.Copy).then_inc(*own.one(ktok_ready))
            for un, (n, z, i) in enumerate(UNITS):
                b = un % 2
                act.wait_ge(*own.last())
                if un >= 2:
                    act.wait_ge(mkv_done.sem, un - 1)
                for hd in range(HEADS):
                    r = 32 * z + hd
                    act.activation(mks[:, b, hd, :], mktok[:, i, tile(hd)], ACT.Copy, scale=wend[:, i, r:r + 1])\
                       .then_inc(*own.one(mks_ready if hd == HEADS - 1 else act_own))
                act.wait_ge(lw_ready.sem, un + 1)
                act.activation(mD[:, b, :, :], mD[:, b, :, :], ACT.Exp).then_inc(*own.one(mD_ready))
                act.wait_ge(eg_done.sem, un + 1)
                if un >= 2:
                    act.wait_ge(mden_ready.sem, un - 1)
                act.activation(megs[:, b, :, :], ps[:, 7, :].rearrange("p (a b) -> p a b", a=HEADS), ACT.Copy)\
                   .then_inc(*own.one(megs_ready))

            for f in range(KT + 1):
                if f < KT:
                    if f == 0:
                        act.wait_ge(go_taken.sem, len(UNITS))
                        act.wait_ge(mh_taken.sem, len(UNITS))
                        act.wait_ge(mC_ready.sem, len(UNITS))
                        act.dma_start(c_late[:, :, :], c_rows).then_inc(c_again.sem, 16)
                    act.wait_ge(*own.last())
                    if f >= 2:
                        act.wait_ge(g_sum.sem, f - 1)
                    o = gla_o[:, f, :] if f < 4 else ml_o[:, f - 4, :]
                    act.activation(gsq[:, f % 2, :], o, ACT.Square).then_inc(*own.one(g_sq))
                if f >= 1:
                    e = f - 1
                    act.wait_ge(g_sum.sem, e + 1)
                    if e >= 2:
                        act.wait_ge(g_y.sem, e - 1)
                    for t, bank, w in ((LAT, 2 * (e % 2), N_LAT), (CTX, 2 * (e % 2) + 1, N_CTX)):
                        act.wait_ge(*own.last())
                        act.activation(grt[:, e % 2, t], ps[:, bank, 0:w], ACT.Sqrt, bias=epsc[:, 0:1], scale=1.0 / P)\
                           .then_inc(*own.one(g_root))
                    act.wait_ge(g_y.sem, e + 1)
                    act.wait_ge(*own.last())
                    act.activation(u[:, e, 0, :], gy[:, e % 2, :], ACT.Copy).then_inc(*own.one(g_hi))
            act.wait_ge(c_again.sem, 16)
            act.wait_ge(*own.last())
            act.activation(c_late[:, :, :], c_late[:, :, :], ACT.Silu).then_inc(*own.one(c_ready))
            act.dma_start(h[:, :, :], xT).then_inc(x_again.sem, 16)
            for m in range(N_OUT):
                act.wait_ge(block_used.sem, S_OUT0 + m + 1)
                high(S_OUT0 + m + 2)

            def feed_forward(q, layer, s_up, s_down, toks):
                lo, w = (0, CW) if layer == 0 else (L0C, N_LAT)
                cv = V_CONV + layer * FT * 4

                def up(n, i):
                    j, par = n // 2, (n // 2) % 2
                    act.wait_ge(block_used.sem, s_count(s_up + n, i))
                    high(s_up + n + 2, i)
                    act.wait_ge(*own.last())
                    if n % 2 == 0:
                        if n == 0:
                            act.wait_ge(q.pad_zero.sem, 1)
                        if j >= 2:
                            act.wait_ge(q.conv_done.sem, j - 1 + 2 * i)
                            act.wait_ge(q.gel_ready.sem, j - 1 + 2 * i)
                        if layer == 0:
                            act.activation(apad[:, par, 1:1 + N_CTX], cx_bank(0), ACT.Copy)\
                               .then_inc(*own.one(act_own))
                        act.activation(apad[:, par, L0C + 1:L0C + 1 + N_LAT], ps[:, 0, :], ACT.Copy)\
                           .then_inc(*own.one(q.a_taken))
                        act.wait_ge(*own.last())
                        c = at_(vec, cv + 4 * j, 8 * i)
                        act.activation(conv[:, par, lo:lo + w], apad[:, par, lo + 1:lo + 1 + w], ACT.Identity,
                                       bias=c(3), scale=c(1)).then_inc(*own.one(q.c_ready))
                    else:
                        act.wait_ge(q.conv_done.sem, j + 1 + 2 * i)
                        if j >= 2:
                            act.wait_ge(q.g_taken.sem, j - 1 + 2 * i)
                        act.activation(gel[:, par, lo:lo + w], conv[:, par, lo:lo + w], ACT.Gelu_apprx_tanh)\
                           .then_inc(*own.one(q.gel_ready))

                blocks(own.loop, {hi_ready: 4, q.a_taken: 2, q.c_ready: 2, q.gel_ready: 2,
                                  **({act_own: 2} if layer == 0 else {})}, N_UP, up, last=4 if layer == 0 else 0)

                def hidden_high(k, kx, i=0):
                    act.wait_ge(*own.last())
                    if k < 2:
                        act.wait_ge(q.g_taken.sem, FT)
                    if k >= 2 and k % 2 == 0:
                        act.wait_ge(q.hid_used.sem, k // 2 + 4 * i)
                    elif k >= 2:
                        act.wait_ge(block_used.sem, s_down + k // 2 + 4 * i)
                    act.activation(hsp[:, k % 2, 0, toks], hid_at(kx, i, toks), ACT.Copy)\
                       .then_inc(*own.one(q.hh_ready))

                hidden_high(0, 0)
                hidden_high(1, 1)

                def down(b, i):
                    g0 = b // (FT // 2) * (FT // 2)
                    for kk in range(2):
                        k = 2 * b + kk + 2
                        if k < 2 * FT:
                            hidden_high(k, k - (FT if k >= FT else 0), i)
                    act.wait_ge(block_used.sem, s_count(s_down + b, i))
                    high(s_down + b + 2, i)

                half = FT // 2
                for g0 in (0, half):
                    down(g0, 0)
                    with own.loop(2, {q.hh_ready: 8, hi_ready: 4}) as i:
                        for b in range(g0 + 1, g0 + 5):
                            down(b, i)
                    for b in range(g0 + 9, g0 + half):
                        down(b, 0)

            normalise(norm[1], 1, amod[:, 1], shift(0, 3), ffn[0].out_updated, slice(0, N_TOK))
            feed_forward(ffn[0], 0, S_UP0, S_DOWN0, slice(0, N_TOK))
            normalise(norm[2], 2, amod[:, 2], shift(1, 0), ffn[0].h_updated, slice(0, N_TOK), permute=True)

            def qk(n, i, first):
                act.wait_ge(block_used.sem, s_count(S_QK + n, i))
                high(S_QK + n + 2, i)
                act.wait_ge(*own.last())
                lat, cx = ps[:, n % 2, :], cx_bank(n)
                if n < KT:
                    act.activation(naq[:, n, :], lat, ACT.Copy, scale=NA_DH ** -0.5).then_inc(*own.one(qk_taken))
                else:
                    act.activation(nak[:, n - KT, CTX], cx, ACT.Copy).then_inc(*own.one(act_own))
                    act.activation(nak[:, n - KT, LAT], lat, ACT.Copy).then_inc(*own.one(qk_taken))

            for n in range(N_QK):
                qk(n, 0, 0)
            for cg in range(2):
                for b in range(4):
                    act.wait_ge(block_used.sem, S_V1 + 4 * cg + b + 1)
                    high(S_V1 + 4 * cg + b + 2)
                for i in range(0, TILES, 2):
                    act.wait_ge(*own.last())
                    act.activation(nav[:, i, 512 * cg:512 * cg + 512], ps[:, i, :], ACT.Copy).then_inc(*own.one(nav_act))

            def load_bias(hd):
                act.dma_start(nab[:, hd % 2, :, :], na_bias_d[hd]).then_inc(bias_loaded[hd % 2].sem, 16)

            for hd in range(2):
                load_bias(hd)
            N_NA = NA_HEADS * NA_TILES
            for un in range(N_NA + 4):
                if un < N_NA:
                    act.wait_ge(*own.last())
                    act.wait_ge(s_done.sem, un + 1)
                    if un >= 4:
                        act.wait_ge(p_turned.sem, un - 3)
                    act.activation(nas[:, un % 4, 256:512], ps[:, 6 + un % 2, 0:256], ACT.Copy).then_inc(*own.one(s_ctx))
                if 1 <= un <= N_NA:
                    e = un - 1
                    act.wait_ge(neg_max.sem, e + 1)
                    act.wait_ge(*own.last())
                    act.activation(nas[:, e % 4, :], nas[:, e % 4, :], ACT.Exp, bias=nast[:, e % 4, 0:1],
                                   accum_out=nast[:, e % 4, 1:2]).then_inc(*own.one(p_exp))
                if un % NA_TILES == NA_TILES - 1 and un // NA_TILES + 2 < NA_HEADS:
                    hd = un // NA_TILES
                    act.wait_ge(bias_used.sem, hd + 1)
                    load_bias(hd + 2)
                if 3 <= un <= N_NA + 2:
                    e = un - 3
                    act.wait_ge(p_turned.sem, e + 1)
                    act.wait_ge(*own.last())
                    if e >= 2:
                        act.wait_ge(o_done.sem, e - 1)
                    act.activation(nap[:, e % 2, :, :], ps[:, 2 + e % 2, :].rearrange("p (a b) -> p a b", a=4), ACT.Copy)\
                       .then_inc(*own.one(pt_ready))
                if un >= 4 and (un - 4) % 8 == 7:
                    m = (un - 4) // 8
                    act.wait_ge(y_taken.sem, m + 1)
                    act.wait_ge(*own.last())
                    act.activation(u[:, m, 0, LAT], nay[:, m % 2, :], ACT.Copy).then_inc(*own.one(y_hi))
            for m in range(N_OUT):
                act.wait_ge(block_used.sem, S_OUT1 + m + 1)
                high(S_OUT1 + m + 2)
            normalise(norm[3], 3, amod[:, 3], shift(1, 3), ffn[1].out_updated, LAT)
            feed_forward(ffn[1], 1, S_UP1, S_DOWN1, LAT)
            normalise(norm[4], 4, None, None, ffn[1].h_updated, LAT)

        @block.vector
        def _(dve):
            own = Own(dve)

            def modulate(m, i, early=True, cols=2):
                r = mod_raw_index(m)
                c, left = (c_early, left_early) if early else (c_late, left_late)
                dve.wait_ge(raw_loaded[r % 4].sem, 16 * (r // 4 + 1) + 32 * i)
                if own.newest:
                    dve.wait_ge(*own.last())
                for col in range(cols - 1, -1, -1):
                    out = modm[:, m, col:col + 1] if isinstance(i, int) else \
                        modm[:, bass.ds(i * 4 + m, 1), col:col + 1].rearrange("p a b -> p (a b)")
                    dve.scalar_tensor_tensor(out=raw[:, r % 4, :] if col == 0 else left[:, :], in0=raw[:, r % 4, :],
                                             scalar=1.0, in1=c[:, col, :], op0=ALU.mult, op1=ALU.mult,
                                             accum_out=out).then_inc(*own.one(mod_done if col == 0 else pre_ready))

            def take_mod(a, b):
                dve.wait_ge(*own.last())
                bias = vec[:, V_MODB + a:V_MODB + b].unsqueeze(2).to_broadcast([P, b - a, 2])
                dve.tensor_tensor(modm[:, a:b, :], modm[:, a:b, :], bias, ALU.add).then_inc(*own.one(dve_own))

            def norm_scale(idx):
                layer, ff = idx // 2, idx % 2
                sc = (layer * MOD_PARTS + 1 + 3 * ff) * KT
                w0 = (V_NFFN if ff else V_NMIX) + layer * KT
                w = vec[:, w0:w0 + KT].unsqueeze(2).to_broadcast([P, KT, 2])
                dve.wait_ge(*own.last())
                dve.scalar_tensor_tensor(out=amod[:, idx, :, :], in0=modm[:, sc:sc + KT, :], scalar=1.0, in1=w,
                                         op0=ALU.add, op1=ALU.mult).then_inc(*own.one(dve_own))

            def normalise(q, idx, B, last_tok, permute=False):
                A = amod[:, idx, :, :] if idx is not None else None
                roots = 2 if last_tok != LAT else 1
                dve.wait_ge(q.root_ready.sem, roots)
                dve.wait_ge(*own.last())
                dve.reciprocal(rstd[:, last_tok], rstd[:, last_tok]).then_inc(*own.one(dve_own))
                parts = ((CTX, 1), (LAT, 0)) if last_tok != LAT else ((LAT, 0),)
                for k in range(KT + 1):
                    if k < KT:
                        dve.wait_ge(*own.last())
                        if idx is None:
                            dve.scalar_tensor_tensor(out=fout[:, k, :], in0=h[:, k, LAT],
                                                     scalar=vec[:, V_NFIN + k:V_NFIN + k + 1], in1=rstd[:, LAT],
                                                     op0=ALU.mult, op1=ALU.mult).then_inc(*own.one(q.t_ready))
                            continue
                        for t, r in parts:
                            dve.scalar_tensor_tensor(out=nt[:, k % 2, t], in0=h[:, k, t], scalar=A[:, k, r:r + 1],
                                                     in1=rstd[:, t], op0=ALU.mult, op1=ALU.mult)\
                               .then_inc(*own.one(q.t_ready if r == 0 else dve_own))
                    if k >= 1 and idx is not None:
                        e = k - 1
                        dve.wait_ge(q.hi_ready.sem, e + 1)
                        dve.wait_ge(*own.last())
                        for t, r in parts:
                            src, hi, dst = nt[:, e % 2, t], u[:, e, 0, t].bitcast(F32), u[:, e, 1, t]
                            if permute and r == 0:
                                for row in range(GRID_H):
                                    gr = lambda x: x.rearrange("p (g r c) -> p r g c", g=8, c=8)[:, row, :, :]
                                    dve.scalar_tensor_tensor(
                                        out=gr(dst), in0=src[:, 64 * row:64 * row + 64].rearrange("p (g c) -> p g c", c=8),
                                        scalar=B(e, r), in1=gr(hi), op0=ALU.add, op1=ALU.subtract)\
                                       .then_inc(*own.one(q.lo_ready if row == GRID_H - 1 else dve_own))
                                continue
                            dve.scalar_tensor_tensor(out=dst, in0=src, scalar=B(e, r), in1=hi, op0=ALU.add,
                                                     op1=ALU.subtract)\
                               .then_inc(*own.one(q.lo_ready if r == 0 else dve_own))

            def shift(layer, part):
                return lambda k, r: modm[:, (layer * MOD_PARTS + part) * KT + k, r:r + 1]

            dve.memset(modm[:, :, :], 0.0).then_inc(*own.one(dve_own))
            dve.wait_ge(c_ready.sem, 1)
            for m in range(MOD_FIRST):
                modulate(m, 0)
            dve.wait_ge(vec_loaded.sem, 16)
            take_mod(0, MOD_FIRST)
            norm_scale(0)
            dve.wait_ge(x_loaded.sem, 16)
            normalise(norm[0], 0, shift(0, 0), slice(0, N_TOK))

            def running_sum(zp):
                dve.wait_ge(apre_log.sem, zp + 1)
                dve.wait_ge(*own.last())
                dve.scalar_tensor_tensor(out=tmp[:, :], in0=cum[:, zp, :], scalar=0.0, in1=tmp[:, :],
                                         op0=ALU.min, op1=ALU.subtract).then_inc(*own.one(dve_own))
                dve.wait_ge(*own.last())
                if zp < 2:
                    dve.tensor_tensor_scan(cum[:, zp, :], reset[:, 0, 0:N_TOK], tmp[:, :], 0.0, ALU.mult, ALU.add)\
                       .then_inc(*own.one(cum_ready))
                else:
                    dve.tensor_tensor_scan(cum[:, zp, ::-1], reset[:, 0, N_TOK:0:-1], tmp[:, ::-1], 0.0,
                                           ALU.mult, ALU.add).then_inc(*own.one(cum_ready))

            dve.wait_ge(const_loaded.sem, 16 * 6)
            for n in range(N_IN):
                modulate(MOD_FIRST + n, 0)
                if not 1 <= n <= 12:
                    continue
                dve.wait_ge(block_used.sem, n + 1)
                dve.wait_ge(*own.last())
                dst = (gqk[:, n - 1, :] if n <= 4 else mqk[:, n - 5, :])[:, LAT]
                cos, sin = (0, 1) if n <= 4 else (2, 3)
                dve.wait_ge(in_act_took.sem, n + 1)
                dve.scalar_tensor_tensor(out=dst, in0=ps[:, n % 2, :], scalar=q_scale(n), in1=rope[:, cos, :],
                                         op0=ALU.mult, op1=ALU.mult).then_inc(*own.one(in_dve_took))
                dve.wait_ge(*own.last())
                dve.scalar_tensor_tensor(out=xs[:, :], in0=xs[:, :], scalar=q_scale(n), in1=rope[:, sin, :],
                                         op0=ALU.mult, op1=ALU.mult).then_inc(*own.one(dve_own))
                dve.wait_ge(*own.last())
                dve.tensor_tensor(dst, dst, xs[:, :], ALU.add).then_inc(*own.one(xs_used))
                if n in (2, 10):
                    running_sum(0 if n == 2 else 2)
                    running_sum(1 if n == 2 else 3)
            for cg, dst in enumerate((gv, mv)):
                for n in range(4):
                    modulate(MOD_FIRST + S_V + 4 * cg + n, 0)
                dve.wait_ge(block_used.sem, S_V + 4 * cg + 4)
                for i in range(1, TILES, 2):
                    dve.wait_ge(*own.last())
                    dve.tensor_copy(dst[:, i, :], ps[:, i, :]).then_inc(*own.one(v_dve))

            take_mod(2 * KT, 5 * KT)
            norm_scale(1)
            for zp in range(4):
                dve.wait_ge(dec_exp.sem, zp + 1)
                dve.wait_ge(*own.last())
                dve.tensor_tensor(qd[:, zp, :], qd[:, zp, :], gqk[:, zp % 2, :], ALU.mult).then_inc(*own.one(dve_own))
                dve.tensor_tensor(kd[:, zp, :], kd[:, zp, :], gqk[:, 2 + zp % 2, :], ALU.mult)\
                   .then_inc(*own.one(dec_ready))
            dve.wait_ge(*own.last())
            dve.memset(gT[:, :, :, :, :], 0.0).then_inc(*own.one(state_zero))

            def step():
                dve.wait_ge(*own.last())
                return own.one(dve_own)

            def rows_sums():
                dve.wait_ge(row_ln.sem, 1)
                n = step()
                dve.scalar_tensor_tensor(out=rI[:, :], in0=rB[:, :], scalar=0.0, in1=tmp[0:64, :],
                                         op0=ALU.min, op1=ALU.subtract).then_inc(*n)
                n = step()
                dve.tensor_tensor_scan(rB[0:32, :], reset[0:32, 1, 0:N_TOK], rI[0:32, :], 0.0, ALU.mult, ALU.add)\
                   .then_inc(*n)
                n = step()
                dve.tensor_tensor_scan(rB[32:64, ::-1], reset[32:64, 1, N_TOK:0:-1], rI[32:64, ::-1], 0.0,
                                       ALU.mult, ALU.add).then_inc(*n)
                n = step()
                dve.tensor_tensor(rA[:, :], rA[:, :], rB[:, :], ALU.subtract).then_inc(*n)

            def rows_gains():
                n = step()
                dve.memset(rI[:, :], 0.0).then_inc(*n)
                n = step()
                dve.tensor_copy(rI[0:32, P::P], rB[0:32, P - 1:N_TOK - 1:P]).then_inc(*n)
                for z_i in range(1, TILES):
                    i, before = ORDER[1][z_i], ORDER[1][z_i - 1]
                    n = step()
                    dve.tensor_copy(rI[32:64, P * i + P - 1:P * i + P], rB[32:64, P * before:P * before + 1]).then_inc(*n)

            def rows_maxima():
                n = step()
                dve.tensor_tensor_scan(rP[0:32, :], rI[0:32, :], rA[0:32, :], 0.0, ALU.add, ALU.max).then_inc(*n)
                n = step()
                dve.tensor_tensor_scan(rP[32:64, N_CTX - 1::-1], rI[32:64, N_CTX - 1::-1], rA[32:64, N_CTX - 1::-1],
                                       0.0, ALU.add, ALU.max).then_inc(*n)
                n = step()
                dve.tensor_tensor_scan(rP[32:64, N_TOK - 1:N_CTX - 1:-1], rI[32:64, N_TOK - 1:N_CTX - 1:-1],
                                       rA[32:64, N_TOK - 1:N_CTX - 1:-1], rP[32:64, 0:1], ALU.add, ALU.max).then_inc(*n)
                n = step()
                dve.tensor_tensor(rB[:, :], rB[:, :], rP[:, :], ALU.add).then_inc(*n)

            def rows_starts():
                n = step()
                dve.memset(mstart[:, :], 0.0).then_inc(*n)
                for z in range(2):
                    rows = slice(32 * z, 32 * z + 32)
                    end = P - 1 if z == 0 else 0
                    for z_i in range(1, TILES):
                        i, before = ORDER[z][z_i], ORDER[z][z_i - 1]
                        n = step()
                        dve.tensor_copy(mstart[rows, i:i + 1], rB[rows, P * before + end:P * before + end + 1]).then_inc(*n)
                    n = step()
                    dve.tensor_copy(pend[rows, :], rP[rows, end::P]).then_inc(*n)

            def rows_weights():
                by_tile = lambda t: t.rearrange("p (i t) -> p i t", t=P)
                wide = lambda t: t.unsqueeze(2).to_broadcast([64, TILES, P])
                n = step()
                dve.tensor_tensor(by_tile(rI[:, :]), wide(mstart[:, :]), by_tile(rP[:, :]), ALU.subtract).then_inc(*n)
                n = step()
                dve.tensor_tensor(by_tile(tmp[0:64, :]), by_tile(rA[:, :]), wide(pend[:, :]), ALU.subtract).then_inc(*n)
                dve.wait_ge(*own.last())
                dve.tensor_scalar(rP[:, :], rP[:, :], -1.0, None, ALU.mult).then_inc(*own.one(row_args))

            cm = lambda z, neg: cmask[:, 2 * neg + z, :]

            def scores_masked(un):
                z, b = UNITS[un][1], un % 2
                dve.wait_ge(ga_done.sem, un + 1)
                dve.wait_ge(*own.last())
                if un >= 2:
                    dve.wait_ge(gi_done.sem, 2 * (un - 1))
                dve.tensor_tensor(gsc[:, b, :, :, :], ps[:, 0:2, 0:2 * P].rearrange("q b (p c) -> q b p c", p=2),
                                  cm(z, 0).unsqueeze(1).unsqueeze(1).to_broadcast([P, 2, GLA_PAIRS, P]), ALU.mult)\
                   .then_inc(*own.one(gsc_ready))

            rows_stages = (rows_sums, rows_gains, rows_maxima, rows_starts, rows_weights)
            scores_masked(0)
            for un, (n, z, i) in enumerate(UNITS):
                if un + 1 < len(UNITS):
                    scores_masked(un + 1)
                for c in range(2):
                    dve.wait_ge(gkv_done.sem, 2 * un + c + 1)
                    dve.wait_ge(gS_ready.sem, 2 * un + c + 1)
                    dve.wait_ge(*own.last())
                    for hh in range(2):
                        rows = slice(64 * hh, 64 * hh + 64)
                        dve.tensor_tensor(gT[rows, z, :, hh, :], gS[rows, z, c, :, hh, :],
                                          ps[rows, kv_bank(un, c), :].rearrange("q (p b c) -> q p b c", p=2, b=2)[:, :, hh, :],
                                          ALU.add).then_inc(*own.one(gT_ready if hh else dve_own))
                dve.wait_ge(gi_done.sem, 2 * un + 2)
                dve.wait_ge(*own.last())
                src = ps[:, 5 + un % 2, :].rearrange("p (a t) -> p a t", a=HEADS)
                dst = gla_o[:, :, tile(i)]
                if FRESH[un]:
                    dve.tensor_copy(dst, src).then_inc(*own.one(go_taken))
                else:
                    dve.tensor_tensor(dst, src, dst, ALU.add).then_inc(*own.one(go_taken))
                if un < len(rows_stages):
                    rows_stages[un]()

            dve.wait_ge(*own.last())
            dve.memset(mC[:, :, :, :], 0.0).then_inc(*own.one(mC_zero))
            four = lambda t: t.rearrange("p (a b) -> p a b", a=HEADS)

            def weigh(un):
                (n, z, i), b = UNITS[un], un % 2
                dve.wait_ge(ml_lw.sem, un + 1)
                dve.wait_ge(*own.last())
                dve.tensor_tensor(mD[:, b, :, :], four(ps[:, 0, :]),
                                  cm(z, 1).unsqueeze(1).to_broadcast([P, HEADS, P]), ALU.add)\
                   .then_inc(*own.one(lw_ready))
                dve.wait_ge(ml_iw.sem, un + 1)
                if un >= 2:
                    dve.wait_ge(mh_done.sem, un - 1)
                dve.tensor_tensor(mqs[:, b, :, :], mqk[:, 0:HEADS, tile(i)], four(ps[:, 2, :]), ALU.mult)\
                   .then_inc(*own.one(mqs_ready))
                dve.wait_ge(*own.last())
                end = P - 1 if z == 0 else 0
                dve.tensor_copy(mdec[:, b, :], ps[:, 2, end::P]).then_inc(*own.one(iw_taken))
                dve.wait_ge(mD_ready.sem, un + 1)
                dve.wait_ge(ml_sc.sem, un + 1)
                dve.tensor_tensor(msc[:, b, :, :], four(ps[:, 1, :]), mD[:, b, :, :], ALU.mult)\
                   .then_inc(*own.one(msc_ready))

            weigh(0)
            for un, (n, z, i) in enumerate(UNITS):
                if un + 1 < len(UNITS):
                    weigh(un + 1)
                b = un % 2
                dve.wait_ge(megs_ready.sem, un + 1)
                dve.wait_ge(mh_done.sem, un + 1)
                dve.wait_ge(*own.last())
                dve.scalar_tensor_tensor(out=mden[:, :, :], in0=four(ps[:, 4, :]), scalar=-1.0, in1=megs[:, b, :, :],
                                         op0=ALU.mult, op1=ALU.max).then_inc(*own.one(mden_ready))
                dve.wait_ge(*own.last())
                dve.tensor_tensor(mden[:, :, :], four(ps[:, 4, :]), mden[:, :, :], ALU.max).then_inc(*own.one(dve_own))
                dve.wait_ge(*own.last())
                dve.reciprocal(mden[:, :, :], mden[:, :, :]).then_inc(*own.one(dve_own))
                dve.wait_ge(*own.last())
                dst = ml_o[:, :, tile(i)]
                if FRESH[un]:
                    dve.tensor_tensor(dst, four(ps[:, 3, :]), mden[:, :, :], ALU.mult).then_inc(*own.one(mh_taken))
                else:
                    dve.tensor_tensor(mden[:, :, :], four(ps[:, 3, :]), mden[:, :, :], ALU.mult)\
                       .then_inc(*own.one(dve_own))
                    dve.wait_ge(*own.last())
                    dve.tensor_tensor(dst, dst, mden[:, :, :], ALU.add).then_inc(*own.one(mh_taken))
                dve.wait_ge(mkv_done.sem, un + 1)
                dve.wait_ge(*own.last())
                for hd in range(HEADS):
                    dve.scalar_tensor_tensor(out=mC[:, z, hd, :], in0=mC[:, z, hd, :], scalar=mdec[:, b, hd:hd + 1],
                                             in1=ps[:, 5 + hd // 2, 256 * (hd % 2):256 * (hd % 2) + 256],
                                             op0=ALU.mult, op1=ALU.add)\
                       .then_inc(*own.one(mC_ready if hd == HEADS - 1 else dve_own))

            for f in range(KT):
                o = gla_o[:, f, :] if f < 4 else ml_o[:, f - 4, :]
                w = V_GLAN if f < 4 else V_MLN
                dve.wait_ge(g_root.sem, 2 * (f + 1))
                dve.wait_ge(*own.last())
                dve.reciprocal(grt[:, f % 2, :], grt[:, f % 2, :]).then_inc(*own.one(dve_own))
                dve.wait_ge(*own.last())
                dve.scalar_tensor_tensor(out=gy[:, f % 2, :], in0=o, scalar=vec[:, w:w + 1], in1=grt[:, f % 2, :],
                                         op0=ALU.mult, op1=ALU.mult).then_inc(*own.one(dve_own))
                dve.wait_ge(*own.last())
                dve.tensor_tensor(gy[:, f % 2, :], gy[:, f % 2, :], gates[:, f, :], ALU.mult).then_inc(*own.one(g_y))
                dve.wait_ge(g_hi.sem, f + 1)
                dve.tensor_tensor(u[:, f, 1, :], gy[:, f % 2, :], u[:, f, 0, :].bitcast(F32), ALU.subtract)\
                   .then_inc(*own.one(g_lo))

            def gate_of(layer, part, m, r):
                c = (layer * MOD_PARTS + part) * KT + m
                return modm[:, c, r:r + 1]

            def add_out(q, s0, layer):
                if layer == 0:
                    dve.wait_ge(c_ready.sem, 2)
                for m in range(N_OUT):
                    if layer == 0:
                        modulate(MOD_FIRST + S_OUT0 + m, 0, early=False)
                    dve.wait_ge(block_used.sem, s0 + m + 1)
                    dve.wait_ge(*own.last())
                    if layer == 0:
                        dve.scalar_tensor_tensor(out=h[:, m, CTX], in0=cx_bank(m),
                                                 scalar=gate_of(layer, 2, m, 1), in1=h[:, m, CTX],
                                                 op0=ALU.mult, op1=ALU.add).then_inc(*own.one(dve_own))
                    dve.scalar_tensor_tensor(out=h[:, m, LAT], in0=ps[:, m % 2, :], scalar=gate_of(layer, 2, m, 0),
                                             in1=h[:, m, LAT], op0=ALU.mult, op1=ALU.add)\
                       .then_inc(*own.one(q.out_updated))

            def feed_forward(q, layer, s_up, s_down, toks):
                lo, w = (0, CW) if layer == 0 else (L0C, N_LAT)
                cv = V_CONV + layer * FT * 4
                dve.wait_ge(*own.last())
                for c0 in (0, N_CTX + 1, L0C):
                    dve.memset(apad[:, :, c0:c0 + 1], 0.0).then_inc(*own.one(dve_own))
                dve.memset(apad[:, :, PADW - 1:PADW], 0.0).then_inc(*own.one(q.pad_zero))

                def modulations(j, i, cols):
                    for s in range(s_up + 2 * j, s_up + 2 * j + 2):
                        if s < S_MIX:
                            modulate(MOD_FIRST + s, i, early=False, cols=cols)

                def up(j, i):
                    par = j % 2
                    c = at_(vec, cv + 4 * j, 8 * i)
                    dve.wait_ge(q.c_ready.sem, j + 1 + 2 * i)
                    dve.wait_ge(*own.last())
                    dve.scalar_tensor_tensor(out=conv[:, par, lo:lo + w], in0=apad[:, par, lo:lo + w], scalar=c(0),
                                             in1=conv[:, par, lo:lo + w], op0=ALU.mult, op1=ALU.add)\
                       .then_inc(*own.one(dve_own))
                    dve.wait_ge(*own.last())
                    dve.scalar_tensor_tensor(out=conv[:, par, lo:lo + w], in0=apad[:, par, lo + 2:lo + 2 + w],
                                             scalar=c(2), in1=conv[:, par, lo:lo + w], op0=ALU.mult, op1=ALU.add)\
                       .then_inc(*own.one(q.conv_done))
                    dve.wait_ge(q.gel_ready.sem, j + 1 + 2 * i)
                    dve.wait_ge(block_used.sem, s_up + 2 * j + 2 + 4 * i)
                    if layer == 0:
                        dve.tensor_tensor(hid_at(j, i, CTX, 2), gel[:, par, 0:N_CTX], cx_bank(1), ALU.mult)\
                           .then_inc(*own.one(dve_own))
                    dve.tensor_tensor(hid_at(j, i, LAT, 2), gel[:, par, L0C:L0C + N_LAT], ps[:, 1, :], ALU.mult)\
                       .then_inc(*own.one(q.g_taken))

                given = {q.conv_done: 2, q.g_taken: 2, dve_own: 4 if layer == 0 else 2}
                if layer == 1:
                    for j in range(2):
                        up(j, 0)
                    with own.loop((FT - 2) // 2, given) as i:
                        for j in range(2, 4):
                            up(j, i)
                else:
                    both = 6
                    for j in range(2):
                        modulations(j, 0, 2)
                        up(j, 0)
                    with own.loop((both - 2) // 2, {**given, mod_done: 4, pre_ready: 4}) as i:
                        for j in range(2, 4):
                            modulations(j, i, 2)
                            up(j, i)
                    with own.loop((FT - 2 - both) // 2, {**given, mod_done: 4}) as i:
                        for j in range(both, both + 2):
                            modulations(j, i, 1)
                            up(j, i)
                    for j in range(FT - 2, FT):
                        modulations(j, 0, 1)
                        up(j, 0)
                    take_mod(6 * KT, MOD_TILES)
                    norm_scale(2)
                    norm_scale(3)

                def hidden_low(k, kx, i=0):
                    dve.wait_ge(q.hh_ready.sem, k + 1 + 8 * i)
                    dve.wait_ge(*own.last())
                    dve.tensor_tensor(hsp[:, k % 2, 1, toks], hid_at(kx, i, toks),
                                      hsp[:, k % 2, 0, toks].bitcast(F32), ALU.subtract)\
                       .then_inc(*own.one(q.hl_ready))

                for g in range(2):
                    k0 = FT * g
                    for kx in range(6):
                        hidden_low(k0 + kx, kx)
                    with own.loop((FT - 6) // 8, {q.hl_ready: 8}) as i:
                        for kx in range(6, 14):
                            hidden_low(k0 + kx, kx, i)
                    if g == 1:
                        pass
                    dve.wait_ge(block_used.sem, s_down + FT // 2 * (g + 1))
                    for mm in range(M_GROUP):
                        m = M_GROUP * g + mm
                        dve.wait_ge(*own.last())
                        if layer == 0:
                            dve.scalar_tensor_tensor(out=h[:, m, CTX],
                                                     in0=ps[:, 4 + mm // 2, 256 * (mm % 2):256 * (mm % 2) + 256],
                                                     scalar=gate_of(layer, 5, m, 1), in1=h[:, m, CTX],
                                                     op0=ALU.mult, op1=ALU.add).then_inc(*own.one(dve_own))
                        dve.scalar_tensor_tensor(out=h[:, m, LAT], in0=ps[:, mm, :], scalar=gate_of(layer, 5, m, 0),
                                                 in1=h[:, m, LAT], op0=ALU.mult, op1=ALU.add)\
                           .then_inc(*own.one(q.h_updated))

            dve.wait_ge(x_again.sem, 16)
            add_out(ffn[0], S_OUT0, 0)
            take_mod(5 * KT, 6 * KT)
            normalise(norm[1], 1, shift(0, 3), slice(0, N_TOK))
            feed_forward(ffn[0], 0, S_UP0, S_DOWN0, slice(0, N_TOK))
            normalise(norm[2], 2, shift(1, 0), slice(0, N_TOK), permute=True)

            for cg in range(2):
                dve.wait_ge(block_used.sem, S_V1 + 4 * cg + 4)
                for i in range(1, TILES, 2):
                    dve.wait_ge(*own.last())
                    dve.tensor_copy(nav[:, i, 512 * cg:512 * cg + 512], ps[:, i, :]).then_inc(*own.one(nav_dve))

            N_NA = NA_HEADS * NA_TILES
            for un in range(N_NA + 4):
                if un < N_NA:
                    hd, j = un // NA_TILES, un % NA_TILES
                    if j == 0:
                        dve.wait_ge(bias_loaded[hd % 2].sem, 16 * (hd // 2 + 1))
                    dve.wait_ge(s_done.sem, un + 1)
                    if un >= 4:
                        dve.wait_ge(p_turned.sem, un - 3)
                    dve.wait_ge(*own.last())
                    dve.tensor_tensor(nas[:, un % 4, 0:256], ps[:, un % 2, 0:256], nab[:, hd % 2, j, :], ALU.add)\
                       .then_inc(*own.one(bias_used if j == NA_TILES - 1 else s_lat))
                if 2 <= un <= N_NA + 1:
                    x = (un - 2) % 4
                    dve.wait_ge(p_exp.sem, un - 1)
                    dve.wait_ge(*own.last())
                    dve.reciprocal(nast[:, x, 2:3], nast[:, x, 1:2]).then_inc(*own.one(dve_own))
                    dve.wait_ge(*own.last())
                    dve.tensor_scalar(nas[:, x, :], nas[:, x, :], nast[:, x, 2:3], None, ALU.mult)\
                       .then_inc(*own.one(p_ready))
                if un < N_NA:
                    dve.wait_ge(s_ctx.sem, un + 1)
                    dve.wait_ge(*own.last())
                    dve.tensor_reduce(nast[:, un % 4, 0:1], nas[:, un % 4, :], AX_X, ALU.max, negate=True)\
                       .then_inc(*own.one(neg_max))
                if un >= 4 and (un - 4) % 8 == 7:
                    m = (un - 4) // 8
                    dve.wait_ge(o_done.sem, un - 3)
                    dve.wait_ge(*own.last())
                    out = ps[:, 4 + m % 2, :].rearrange("p (g r c) -> p r g c", g=8, c=8)
                    dst = nay[:, m % 2, :].rearrange("p (r g c) -> p r g c", g=8, c=8)
                    dve.tensor_copy(dst[:, :, 1:8, :], out[:, :, 0:7, :]).then_inc(*own.one(dve_own))
                    dve.tensor_copy(dst[:, :, 0:1, :], out[:, :, 7:8, :]).then_inc(*own.one(y_taken))
                    dve.wait_ge(y_hi.sem, m + 1)
                    dve.wait_ge(*own.last())
                    dve.tensor_tensor(u[:, m, 1, LAT], nay[:, m % 2, :], u[:, m, 0, LAT].bitcast(F32),
                                      ALU.subtract).then_inc(*own.one(y_lo))

            add_out(ffn[1], S_OUT1, 1)
            normalise(norm[3], 3, shift(1, 3), LAT)
            feed_forward(ffn[1], 1, S_UP1, S_DOWN1, LAT)
            normalise(norm[4], None, None, LAT)

        @block.tensor
        def _(pe):
            own = Own(pe)

            def normalise(q, last_tok):
                for k in range(KT):
                    pe.wait_ge(q.sq_ready.sem, k + 1)
                    for t, bank, w in ((CTX, q.cx_bank, N_CTX), (LAT, 6, N_LAT)):
                        if t == CTX and last_tok == LAT:
                            continue
                        mm = pe.matmul(ps[:, bank, 0:w], ones[:, :], sq[:, k % 2, t], start=(k == 0), stop=(k == KT - 1))
                    mm.then_inc(*own.one(q.sq_summed))

            PASSES = ((0, 0), (0, 1), (1, 0))

            def features(s, i, lat, cx, x, ready=None):
                pe.wait_ge(lo_ready.sem, s_count(s, i))
                for k in range(KT):
                    if ready is not None:
                        pe.wait_ge(ready.sem, k + 1)
                    for a, (wp, xp) in enumerate(PASSES):
                        w = wsp[:, s % 2, wp, tile(k)]
                        first, last = k == 0 and a == 0, k == KT - 1 and a == 2
                        if cx is not None:
                            pe.matmul(cx, w, x[:, k, xp, CTX], start=first, stop=last)
                        mm = pe.matmul(lat, w, x[:, k, xp, LAT], start=first, stop=last)
                mm.then_inc(*own.one(block_used))

            def tokens(s, b, taken):
                pe.wait_ge(lo_ready.sem, s + 1)
                for kk in range(2):
                    k = 2 * b + kk
                    for i in range(TILES):
                        if k == 0:
                            for q, n in taken:
                                pe.wait_ge(q.sem, n)
                        for a, (wp, xp) in enumerate(PASSES):
                            mm = pe.matmul(ps[:, i, :], u[:, k, xp, tile(i)], wsp[:, s % 2, wp, 512 * kk:512 * kk + 512],
                                           start=(k == 0 and a == 0), stop=(k == KT - 1 and a == 2),
                                           skip_group_check=True)
                mm.then_inc(*own.one(block_used))

            pe.wait_ge(ones_ready.sem, 2)
            normalise(norm[0], slice(0, N_TOK))

            def projection(n, i=0):
                if n >= 2:
                    pe.wait_ge(in_act_took.sem, n - 1 + 4 * i)
                if 3 <= n <= 14:
                    pe.wait_ge(in_dve_took.sem, n - 2 + 4 * i)
                features(S_IN + n, i, ps[:, n % 2, :], cx_bank(n), u, norm[0].lo_ready if n == 0 else None)

            def decay_inputs(zp):
                b = 3 + 2 * (zp % 2)
                if zp >= 2:
                    pe.wait_ge(apre_taken.sem, 2 * (zp - 1))
                for t, bank, w in ((LAT, b, N_LAT), (CTX, b + 1, N_CTX)):
                    mm = pe.matmul(ps[:, bank, 0:w], aup[:, zp // 2, tile(zp % 2)], small[:, t], start=True, stop=True)
                mm.then_inc(*own.one(apre_done))

            for n in range(3):
                projection(n)
            pe.wait_ge(const_loaded.sem, 16 * 6)
            for zp in range(2):
                decay_inputs(zp)
            with own.loop(2, {block_used: 4}) as i:
                for n in range(3, 7):
                    projection(n, i)
            for zp in range(2, 4):
                decay_inputs(zp)
            for n in range(11, 15):
                projection(n)
            for n in range(15, N_IN):
                projection(n)

            for cg in range(2):
                taken = [(in_act_took, N_IN), (apre_taken, 8)] if cg == 0 else [(v_act, 3), (v_dve, 3)]
                for b in range(4):
                    tokens(S_V + 4 * cg + b, b, taken)

            pe.wait_ge(v_act.sem, 6)
            pe.wait_ge(v_dve.sem, 6)
            for c, b in ((0, 3), (1, 5)):
                for t, bank, w in ((LAT, b, N_LAT), (CTX, b + 1, N_CTX)):
                    mm = pe.matmul(ps[0:64, bank, 0:w], sel[:, c, :], small[:, t], start=True, stop=True)
                mm.then_inc(*own.one(rows_done))

            pe.wait_ge(dec_ready.sem, 4)
            pe.wait_ge(rows_taken.sem, 4)
            def gla_scores(un):
                n, z, i = UNITS[un]
                if un >= 1:
                    pe.wait_ge(gsc_ready.sem, un)
                    pe.wait_ge(gktok_ready.sem, un)
                for p in range(GLA_PAIRS):
                    zp = 2 * z + p
                    for hh in range(2):
                        rows = slice(64 * hh, 64 * hh + 64)
                        pe.matmul(ps[:, hh, P * p:P * p + P], kd[rows, zp, tile(i)], qd[rows, zp, tile(i)],
                                  start=True, stop=True)
                    mm = pe.transpose(ps[:, 2, P * p:P * p + P], kd[:, zp, tile(i)], ident[:, :])
                mm.then_inc(*own.one(ga_done))

            def gla_keys_values(un):
                n, z, i = UNITS[un]
                pe.wait_ge(gktok_ready.sem, un + 1)
                for c in range(2):
                    if 2 * un + c >= 3:
                        pe.wait_ge(gT_ready.sem, 2 * un + c - 2)
                    cc = c if z == 0 else 1 - c
                    rows = slice(64 * cc, 64 * cc + 64)
                    for p in range(GLA_PAIRS):
                        mm = pe.matmul(ps[:, kv_bank(un, c), 256 * p:256 * p + 256], gktok[rows, un % 2, tile(p)],
                                       gv[rows, i, 256 * p:256 * p + 256], start=True, stop=True)
                    mm.then_inc(*own.one(gkv_done))

            gla_scores(0)
            gla_keys_values(0)
            for un, (n, z, i) in enumerate(UNITS):
                if un + 1 < len(UNITS):
                    gla_scores(un + 1)
                pe.wait_ge(gsc_ready.sem, un + 1)
                if un >= 2:
                    pe.wait_ge(go_taken.sem, un - 1)
                for hd in range(HEADS):
                    pe.matmul(ps[:, 5 + un % 2, tile(hd)], gv[:, i, tile(hd)], gsc[:, un % 2, hd % 2, hd // 2, :],
                              start=(hd == 0), stop=False, skip_group_check=True)
                if un + 1 < len(UNITS):
                    gla_keys_values(un + 1)
                for c in range(2):
                    cc = c if z == 0 else 1 - c
                    pe.wait_ge(gS_ready.sem, 2 * un + c + 1)
                    for hd in range(HEADS):
                        t0 = 64 * cc
                        mm = pe.matmul(ps[:, 5 + un % 2, P * hd + t0:P * hd + t0 + 64], gS[:, z, c, hd // 2, hd % 2, :],
                                       qd[:, 2 * z + hd // 2, P * i + t0:P * i + t0 + 64],
                                       start=False, stop=(c == 1), skip_group_check=True)
                    mm.then_inc(*own.one(gi_done))

            pe.wait_ge(row_exp.sem, 3)
            pe.wait_ge(go_taken.sem, len(UNITS))
            for i in range(TILES):
                mm = pe.transpose(ps[:, 5, 64 * i:64 * i + 64], tmp[0:64, tile(i)], ident[0:64, 0:64])
            mm.then_inc(*own.one(wend_turned))
            for i in range(TILES):
                if i >= 2:
                    pe.wait_ge(ktok_ready.sem, i - 1)
                for hd in range(HEADS):
                    mm = pe.transpose(ps[:, i % 2, tile(hd)], mqk[:, HEADS + hd, tile(i)], ident[:, :])
                mm.then_inc(*own.one(ktok_turned))
            pe.wait_ge(mC_zero.sem, 1)
            pe.wait_ge(ktok_ready.sem, TILES)
            pe.wait_ge(wend_ready.sem, 1)
            def row(z, hd):
                return ident[0:64, 32 * z + hd:32 * z + hd + 1].to_broadcast([64, P])

            def ml_weights(un):
                n, z, i = UNITS[un]
                if un >= 1:
                    pe.wait_ge(lw_ready.sem, un)
                    pe.wait_ge(iw_taken.sem, un)
                for hd in range(HEADS):
                    pe.matmul(ps[:, 0, tile(hd)], row(z, hd), rP[:, tile(i)], start=True, stop=False)
                    mm = pe.matmul(ps[:, 0, tile(hd)], rA[:, tile(i)], row(z, hd), start=False, stop=True)
                mm.then_inc(*own.one(ml_lw))
                for hd in range(HEADS):
                    mm = pe.matmul(ps[:, 2, tile(hd)], row(z, hd), rI[:, tile(i)], start=True, stop=True)
                mm.then_inc(*own.one(ml_iw))
                if un >= 1:
                    pe.wait_ge(msc_ready.sem, un)
                for hd in range(HEADS):
                    mm = pe.matmul(ps[:, 1, tile(hd)], mqk[:, HEADS + hd, tile(i)], mqk[:, hd, tile(i)],
                                   start=True, stop=True)
                mm.then_inc(*own.one(ml_sc))
                if un >= 1:
                    pe.wait_ge(megs_ready.sem, un)
                for hd in range(HEADS):
                    mm = pe.matmul(ps[:, 7, tile(hd)], row(z, hd), rB[:, tile(i)], start=True, stop=True)
                mm.then_inc(*own.one(eg_done))

            ml_weights(0)
            for un, (n, z, i) in enumerate(UNITS):
                b = un % 2
                if un + 1 < len(UNITS):
                    ml_weights(un + 1)
                pe.wait_ge(mks_ready.sem, un + 1)
                if un >= 1:
                    pe.wait_ge(mC_ready.sem, un)
                for hd in range(HEADS):
                    kv = ps[:, 5 + hd // 2, 256 * (hd % 2):256 * (hd % 2) + 256]
                    pe.matmul(kv[:, 0:P], mks[:, b, hd, :], mv[:, i, tile(hd)], start=True, stop=True)
                    mm = pe.matmul(kv[:, P:2 * P], mks[:, b, hd, :], ones[:, :], start=True, stop=True)
                mm.then_inc(*own.one(mkv_done))
                pe.wait_ge(mqs_ready.sem, un + 1)
                pe.wait_ge(msc_ready.sem, un + 1)
                if un >= 1:
                    pe.wait_ge(mh_taken.sem, un)
                for hd in range(HEADS):
                    pe.matmul(ps[:, 3, tile(hd)], mv[:, i, tile(hd)], msc[:, b, hd, :], start=True, stop=False)
                    pe.matmul(ps[:, 3, tile(hd)], mC[:, z, hd, 0:P], mqs[:, b, hd, :], start=False, stop=True)
                    pe.matmul(ps[:, 4, tile(hd)], ones[:, :], msc[:, b, hd, :], start=True, stop=False)
                    mm = pe.matmul(ps[:, 4, tile(hd)], mC[:, z, hd, P:2 * P], mqs[:, b, hd, :], start=False, stop=True)
                mm.then_inc(*own.one(mh_done))

            for f in range(KT):
                pe.wait_ge(g_sq.sem, f + 1)
                if f == 0:
                    pe.wait_ge(mh_taken.sem, len(UNITS))
                if f >= 2:
                    pe.wait_ge(g_root.sem, 2 * (f - 1))
                for t, bank, w in ((LAT, 2 * (f % 2), N_LAT), (CTX, 2 * (f % 2) + 1, N_CTX)):
                    mm = pe.matmul(ps[:, bank, 0:w], ones[:, :], gsq[:, f % 2, t], start=True, stop=True)
                mm.then_inc(*own.one(g_sum))

            def out_projection(q, s0, layer, ready):
                pe.wait_ge(ready.sem, KT)
                if layer == 0:
                    pe.wait_ge(g_root.sem, 2 * KT)
                for m in range(N_OUT):
                    if m >= 2:
                        pe.wait_ge(q.out_updated.sem, m - 1)
                    features(s0 + m, 0, ps[:, m % 2, :], cx_bank(m) if layer == 0 else None, u)

            def feed_forward(q, n, layer, s_up, s_down, toks):
                pe.wait_ge(n.lo_ready.sem, KT)

                def up(b, i):
                    if b >= 2:
                        pe.wait_ge((q.g_taken if b % 2 else q.a_taken).sem, b // 2 + 2 * i)
                    features(s_up + b, i, ps[:, b % 2, :], cx_bank(b) if layer == 0 else None, u)

                blocks(own.loop, {block_used: 4}, N_UP, up)

                def down(b, i):
                    g, first = b // (FT // 2), b % (FT // 2) == 0
                    end = b % (FT // 2) == FT // 2 - 1
                    pe.wait_ge(lo_ready.sem, s_count(s_down + b, i))
                    for kk in range(2):
                        pe.wait_ge(q.hl_ready.sem, 2 * b + kk + 1 + 8 * i)
                        for mm_ in range(M_GROUP):
                            if first and kk == 0 and g == 1 and mm_ % 2 == 0:
                                pe.wait_ge(q.h_updated.sem, mm_ + 2)
                            if first and kk == 0 and g == 0 and mm_ == 0:
                                pe.wait_ge(q.g_taken.sem, FT)
                            lat = ps[:, mm_, :]
                            cx = ps[:, 4 + mm_ // 2, 256 * (mm_ % 2):256 * (mm_ % 2) + 256]
                            for a, (wp, xp) in enumerate(PASSES):
                                w = wsp[:, (s_down + b) % 2, wp, 512 * kk + P * mm_:512 * kk + P * mm_ + P]
                                one, last = first and kk == 0 and a == 0, end and kk == 1 and a == 2
                                if layer == 0:
                                    pe.matmul(cx, w, hsp[:, kk, xp, CTX], start=(one and mm_ % 2 == 0), stop=last,
                                              skip_group_check=True)
                                mm = pe.matmul(lat, w, hsp[:, kk, xp, LAT], start=one, stop=last,
                                               skip_group_check=True)
                        if kk == 0:
                            mm.then_inc(*own.one(q.hid_used))
                        else:
                            mm.then_inc(*own.one(block_used))

                half = FT // 2
                for g0 in (0, half):
                    down(g0, 0)
                    with own.loop(2, {block_used: 4, q.hid_used: 4}) as i:
                        for b in range(g0 + 1, g0 + 5):
                            down(b, i)
                    for b in range(g0 + 9, g0 + half):
                        down(b, 0)

            out_projection(ffn[0], S_OUT0, 0, g_lo)
            normalise(norm[1], slice(0, N_TOK))
            feed_forward(ffn[0], norm[1], 0, S_UP0, S_DOWN0, slice(0, N_TOK))
            normalise(norm[2], slice(0, N_TOK))

            pe.wait_ge(norm[2].lo_ready.sem, KT)
            for n in range(N_QK):
                if n >= 2:
                    pe.wait_ge(qk_taken.sem, n - 1)
                features(S_QK + n, 0, ps[:, n % 2, :], cx_bank(n) if n >= KT else None, u)
            for cg in range(2):
                taken = [(qk_taken, N_QK)] if cg == 0 else [(nav_act, 3), (nav_dve, 3)]
                for b in range(4):
                    tokens(S_V1 + 4 * cg + b, b, taken)

            pe.wait_ge(nav_act.sem, 6)
            pe.wait_ge(nav_dve.sem, 6)
            N_NA = NA_HEADS * NA_TILES
            for un in range(N_NA + 4):
                if un < N_NA:
                    hd, j = un // NA_TILES, un % NA_TILES
                    rows, m, x = slice(64 * (hd % 2), 64 * (hd % 2) + 64), hd // 2, un % 2
                    if un >= 2:
                        pe.wait_ge(s_ctx.sem, un - 1)
                        pe.wait_ge(neg_max.sem, un - 1)
                    if j < NA_TILES - 1:
                        keys = nak[rows, m, N_CTX + P * j:N_CTX + P * j + 256]
                        parts = [(slice(0, P), slice(64 * (2 * j + 1), 64 * (2 * j + 3)))]
                    else:
                        keys = nak[rows, m, LAT].rearrange("p (i t) -> p i t", t=P)[:, 0::3, :]
                        parts = [(slice(0, 64), slice(448, 512)), (slice(64, P), slice(0, 64))]
                    for out_rows, cols in parts:
                        pe.matmul(ps[out_rows, x, 0:256], naq[rows, m, cols], keys, start=True, stop=True)
                        mm = pe.matmul(ps[out_rows, 6 + x, 0:256], naq[rows, m, cols], nak[rows, m, CTX],
                                       start=True, stop=True)
                    mm.then_inc(*own.one(s_done))
                if 3 <= un <= N_NA + 2:
                    e = un - 3
                    pe.wait_ge(p_ready.sem, e + 1)
                    if e >= 2:
                        pe.wait_ge(pt_ready.sem, e - 1)
                    for c in range(4):
                        mm = pe.transpose(ps[:, 2 + e % 2, tile(c)], nas[:, e % 4, tile(c)], ident[:, :])
                    mm.then_inc(*own.one(p_turned))
                if un >= 4:
                    e = un - 4
                    hd, j = e // NA_TILES, e % NA_TILES
                    m = hd // 2
                    pe.wait_ge(pt_ready.sem, e + 1)
                    if m >= 2 and hd % 2 == 0 and j == 0:
                        pe.wait_ge(y_taken.sem, m - 1)
                    keys = (2 + j, 3 + j, 0, 1) if j < NA_TILES - 1 else (2, 5, 0, 1)
                    for c, t in enumerate(keys):
                        mm = pe.matmul(ps[64 * (hd % 2):64 * (hd % 2) + 64, 4 + m % 2, tile(j)],
                                       nav[:, t, NA_DH * hd:NA_DH * hd + NA_DH], nap[:, e % 2, c, :],
                                       start=(c == 0), stop=(c == 3))
                    mm.then_inc(*own.one(o_done))

            out_projection(ffn[1], S_OUT1, 1, y_lo)
            normalise(norm[3], LAT)
            feed_forward(ffn[1], norm[3], 1, S_UP1, S_DOWN1, LAT)
            normalise(norm[4], LAT)


def rope_table():
    pos = np.arange(N_LAT)
    row, col = (pos // GRID_W).astype(np.float32), (pos % GRID_W).astype(np.float32)
    out = np.zeros((P, 4, N_LAT), np.float32)
    for a, dh in enumerate((GLA_DK, ML_DH)):
        n = dh // 4
        inv = (np.float32(10000.0) ** (-np.arange(n, dtype=np.float32) / np.float32(n))).astype(np.float32)
        ang = np.concatenate([row[:, None] * inv, col[:, None] * inv], axis=-1).astype(np.float32)
        d = np.arange(P) % dh
        sign = np.where(d < dh // 2, -1.0, 1.0).astype(np.float32)
        out[:, 2 * a] = np.cos(ang).T[d % (dh // 2)]
        out[:, 2 * a + 1] = sign[:, None] * np.sin(ang).T[d % (dh // 2)]
    return out


def reset_table():
    t = np.arange(N_TOK + 1)
    out = np.stack([(t % GLA_CHUNK != 0), (t % P != 0)]).astype(np.float32)
    return np.broadcast_to(out, (P, 2, N_TOK + 1)).copy()


def packed_constants():
    out = np.zeros((P, 6 * P), np.float32)
    out[:, 0:P] = np.eye(P)
    for z in range(2):
        for hd in range(HEADS):
            out[64 + 4 * z + hd, P + 32 * z + hd] = 1.0
            out[96 + 4 * z + hd, P + 64 + 32 * z + hd] = 1.0
    s, t = np.arange(P)[:, None], np.arange(P)[None, :]
    for z in range(2):
        order = (s <= t) if z == 0 else (s >= t)
        out[:, (2 + z) * P:(3 + z) * P] = order & (s // GLA_CHUNK == t // GLA_CHUNK)
        out[:, (4 + z) * P:(5 + z) * P] = np.where(order, 0.0, NEG)
    return out


def bias_places():
    g8 = lambda g: [(r, 8 * g + c) for r in range(GRID_H) for c in range(8)]
    out = np.zeros((NA_TILES, P, 256), np.int64)
    pad = (2 * 8 - 1) * (2 * NA_WIN_W - 1)
    for j in range(NA_TILES):
        qs = [(2 * j + 1) % 8, (2 * j + 2) % 8]
        ks = range(2 * j, 2 * j + 4) if j < NA_TILES - 1 else (0, 1, 6, 7)
        q = np.array([x for g in qs for x in g8(g)])
        k = np.array([x for g in ks for x in g8(g)])
        start = np.clip(q[:, 1] - NA_WIN_W // 2, 0, GRID_W - NA_WIN_W)
        dr = k[None, :, 0] - q[:, None, 0] + 7
        dc = k[None, :, 1] - q[:, None, 1] + NA_WIN_W - 1
        inside = (k[None, :, 1] >= start[:, None]) & (k[None, :, 1] < start[:, None] + NA_WIN_W)
        out[j] = np.where(inside, dr * (2 * NA_WIN_W - 1) + np.clip(dc, 0, 2 * NA_WIN_W - 2), pad)
    return out


def column_blocks(w):
    m = w.shape[1] // P
    return w.reshape(KT, P, m, P).transpose(2, 1, 0, 3).reshape(m, P, BLOCK)


def row_blocks(w):
    k = w.shape[0] // P
    return w.reshape(k // 2, 2, P, 2, 512).transpose(3, 0, 2, 1, 4).reshape(k, P, BLOCK)


def kernel(**inputs):
    import concourse.bacc as bacc
    from concourse.bass_utils import run_bass_kernel_spmd

    g = {k: np.asarray(v) for k, v in inputs.items()}
    tokens = np.concatenate([g["ctx"][0], g["x"][0]], axis=0)
    xT = tokens.T.reshape(KT, P, N_TOK).transpose(1, 0, 2)

    win = g["ev_w_in"][0]
    sizes = (256, 256, 512, 512, 32, 512, 512, 512, 512, 16)
    at = np.concatenate([[0], np.cumsum(sizes)])
    gq, gk, gv, gg, ga, mq, mk, mv, mo, mg = (win[:, a:b] for a, b in zip(at[:-1], at[1:]))
    mg = mg.reshape(D, 2, 2, HEADS)
    gate_cols = np.zeros((D, P), win.dtype)
    for z in range(2):
        gate_cols[:, 32 * z:32 * z + 16] = ga[:, 16 * z:16 * z + 16]
        gate_cols[:, 64 + 4 * z:68 + 4 * z] = mg[:, z, 0]
        gate_cols[:, 96 + 4 * z:100 + 4 * z] = mg[:, z, 1]
    stream = [column_blocks(x) for x in (gate_cols, gq, gk, mq, mk, gg, mo)]
    stream += [row_blocks(np.concatenate([gv, mv], axis=1)), column_blocks(g["ev_w_out"][0])]

    def up(w):
        a, b = column_blocks(w[:, :D_FF]), column_blocks(w[:, D_FF:])
        return np.stack([a, b], axis=1).reshape(2 * FT, P, BLOCK)

    qkv = g["na_w_qkv"][0]
    stream += [up(g["ffn_w_up"][0]), row_blocks(g["ffn_w_down"][0])]
    stream += [column_blocks(qkv[:, :2 * D]), row_blocks(qkv[:, 2 * D:]), column_blocks(g["na_w_out"][0])]
    stream += [up(g["ffn_w_up"][1]), row_blocks(g["ffn_w_down"][1])]
    stream = np.concatenate(stream, axis=0)
    mods = np.concatenate([g["mod_w"][l].T.reshape(-1, P, D) for l in range(2)], axis=0)
    mixed = np.stack([stream[:S_MIX], mods[MOD_FIRST:]], axis=1).reshape(-1, P, BLOCK)
    weights = np.concatenate([mods[:MOD_FIRST], mixed, stream[S_MIX:]], axis=0)

    by_part = lambda v: v.reshape(-1, P).T
    vecs = np.zeros((P, V_N), np.float32)
    for l in range(2):
        vecs[:, V_NMIX + KT * l:V_NMIX + KT * l + KT] = by_part(g["norm_mix_w"][l])
        vecs[:, V_NFFN + KT * l:V_NFFN + KT * l + KT] = by_part(g["norm_ffn_w"][l])
        vecs[:, V_MODB + 48 * l:V_MODB + 48 * l + 48] = by_part(g["mod_b"][l])
        cv = np.stack([by_part(g["ffn_conv_w"][l, t]) for t in range(3)] + [by_part(g["ffn_conv_b"][l])], axis=2)
        vecs[:, V_CONV + 4 * FT * l:V_CONV + 4 * FT * l + 4 * FT] = cv.reshape(P, 4 * FT)
    vecs[:, V_NFIN:V_NFIN + KT] = by_part(g["final_norm_w"])
    vecs[:, V_GLAN] = g["gla_norm_w"][0]
    vecs[:, V_MLN] = g["ml_norm_w"][0]
    vecs[:, V_ABIAS:V_ABIAS + 4] = by_part(g["gla_a_bias"][0].reshape(-1))
    for z in range(2):
        vecs[32 * z:32 * z + HEADS, V_GATEB:V_GATEB + 2] = g["ml_gate_bias"][0, z].T
    c_rows = np.broadcast_to(np.stack([g["c"][0], g["c_ctx"]]), (P, 2, D))
    a_up = np.zeros((P, 2, 256), np.float32)
    for z in range(2):
        a_up[32 * z:32 * z + 16, z] = g["gla_a_up"][0, z]
    rpb = g["na_rpb"][0].reshape(NA_HEADS, -1)
    rpb = np.concatenate([rpb, np.full((NA_HEADS, 1), NEG, rpb.dtype)], axis=1)
    na_bias = rpb[:, bias_places()].transpose(0, 2, 1, 3)

    arrays = {"in_x": xT, "in_vecs": vecs, "in_consts": packed_constants(), "in_rope": rope_table(),
              "in_reset": reset_table(), "in_aup": a_up, "in_nabias": na_bias, "in_crows": c_rows, "in_weights": weights}
    arrays = {k: np.ascontiguousarray(v) for k, v in arrays.items()}
    nc = bacc.Bacc("TRN2", target_bir_lowering=False, num_devices=1)
    aps = [nc.dram_tensor(k, a.shape, mybir.dt.from_np(a.dtype), kind="ExternalInput").ap() for k, a in arrays.items()]
    out = nc.dram_tensor("out_0", (P, KT, N_LAT), F32, kind="ExternalOutput").ap()
    build(nc, *aps, out)
    r = run_bass_kernel_spmd(nc, [arrays], core_ids=[0])
    y = r.results[0]["out_0"]
    return y.transpose(1, 0, 2).reshape(D, N_LAT).T.reshape(1, N_LAT, D)
```

```python
from contextlib import ExitStack, contextmanager

import numpy as np

import concourse.bass as bass
from concourse import mybir

ALU = mybir.AluOpType
ACT = mybir.ActivationFunctionType
AX_X = mybir.AxisListType.X
F32 = mybir.dt.float32
F32R = mybir.dt.float32r

P = 128
D = 1024
KT = D // P
N_CTX, N_LAT = 256, 512
N_TOK = N_CTX + N_LAT
CTX, LAT = slice(0, N_CTX), slice(N_CTX, N_TOK)
TILES = N_TOK // P
GRID_W, GRID_H = 64, N_LAT // 64
EPS = 1e-6

GLA_CHUNK = 64
GLA_DK, ML_DH = 64, 128
HEADS = 4
GLA_PAIRS = HEADS // 2
GLA_TAU = 16.0

NA_HEADS, NA_DH = 16, 64
NA_WIN_W = 16
NA_TILES = N_LAT // P

D_FF = ((8 * D // 3 + 255) // 256) * 256
FT = D_FF // P
M_GROUP = 4

BLOCK = 1024
RAW_SLOTS, SPLIT_SLOTS = 4, 2
N_IN, N_V, N_OUT, N_UP, N_DOWN, N_QK = 21, 8, 8, 2 * FT, FT, 16
S_IN = 0
S_V = S_IN + N_IN
S_OUT0 = S_V + N_V
S_UP0 = S_OUT0 + N_OUT
S_DOWN0 = S_UP0 + N_UP
S_QK = S_DOWN0 + N_DOWN
S_V1 = S_QK + N_QK
S_OUT1 = S_V1 + N_V
S_UP1 = S_OUT1 + N_OUT
S_DOWN1 = S_UP1 + N_UP
S_END = S_DOWN1 + N_DOWN
MOD_PARTS = 6
MOD_TILES = 2 * MOD_PARTS * KT
MOD_FIRST = 2 * KT
S_MIX = MOD_TILES - MOD_FIRST
S_NO_CTX = 8 * KT - MOD_FIRST
assert S_MIX % 4 == 0 and S_UP0 + 40 < S_MIX < S_DOWN0
NEG = -1e30

V_NMIX, V_NFFN, V_NFIN = 0, 16, 32
V_MODB = 40
V_GLAN, V_MLN = V_MODB + MOD_TILES, V_MODB + MOD_TILES + 1
V_ABIAS = V_MLN + 1
V_CONV = V_ABIAS + 4
V_GATEB = V_CONV + 2 * FT * 4
V_N = V_GATEB + 2


def raw_index(s):
    return MOD_FIRST + 2 * s if s < S_MIX else MOD_TILES + s


def raw_turn(s):
    return 8 if s < S_MIX else 4


def q_scale(n):
    return GLA_DK ** -0.5 if n in (1, 2) else ML_DH ** -0.5 if n >= 9 else 1.0


def mod_raw_index(m):
    return m if m < MOD_FIRST else 2 * m - MOD_FIRST + 1


class Signal:

    def __init__(self, sem):
        self.sem, self.base, self.k, self.per, self.i = sem, 0, 0, 0, 0

    def count(self):
        return self.base + self.k + self.per * self.i if self.per else self.base + self.k


class Own:

    def __init__(self, eng):
        self.eng, self.newest = eng, None

    def one(self, signal):
        signal.k += 1
        self.newest = signal
        return signal.sem, 1

    def last(self):
        return self.newest.sem, self.newest.count()

    @contextmanager
    def loop(self, trips, per):
        self.eng.wait_ge(*self.last())
        with self.eng.Fori(0, trips) as i:
            for s, n in per.items():
                s.base, s.k, s.per, s.i = s.base + s.k, 0, n, i
            yield i
            self.eng.wait_ge(*self.last())
        for s, n in per.items():
            assert s.k == n, (s.sem, s.k, n)
            s.base, s.k, s.per, s.i = s.base + n * trips, 0, 0, 0


def build(nc, xT, vecs, consts_d, rope_d, reset_d, a_up_d, na_bias_d, c_rows, weights, outT):
    ctx = ExitStack()
    with ctx:
        SB0 = 16512
        T = N_TOK * 4
        place = [SB0]

        def at(name, shape, off, dt=F32):
            assert off % 32 == 0
            return nc.alloc_sbuf_tensor_at(name, shape, dt, offset=off)

        def take(name, shape, dt=F32):
            n = 4
            for x in shape[1:]:
                n *= x
            t = at(name, shape, place[0], dt)
            place[0] += (n + 31) // 32 * 32
            return t

        h_off = place[0]
        h = take("h", [P, KT, N_TOK])
        gates = at("gates", [P, KT, N_TOK], h_off)
        u_off = place[0]
        u = take("u", [P, KT, 2, N_TOK], F32R)
        raw = take("raw", [P, RAW_SLOTS, BLOCK])
        wsp = take("wsp", [P, SPLIT_SLOTS, 2, BLOCK], F32R)
        ident = take("ident", [P, P])
        ones = take("ones", [P, P])
        vec = take("vec", [P, V_N])
        modm = take("modm", [P, MOD_TILES, 2])
        amod = take("amod", [P, 4, KT, 2])
        epsc = take("epsc", [P, 1])
        rt = take("rt", [P, TILES])
        mdec = take("mdec", [P, 2, HEADS])
        mstart = take("mstart", [64, TILES])
        pend = take("pend", [64, TILES])
        ar = place[0]
        AR_END = 229344

        def norm_buffers(name, off):
            return (at(name + "_sq", [P, 2, N_TOK], off), at(name + "_nt", [P, 2, N_TOK], off + 2 * T),
                    at(name + "_acc", [P, N_TOK], off + 4 * T))
        first_norm = norm_buffers("first_norm", ar)
        later_norm = norm_buffers("later_norm", ar + FT * T)
        fout = at("fout", [P, KT, N_LAT], ar + 5 * T)
        gqk = at("gqk", [P, 4, N_TOK], ar)
        gv = at("gv", [P, TILES, 512], ar + 4 * T)
        mqk = at("mqk", [P, 8, N_TOK], ar + 8 * T)
        mv = at("mv", [P, TILES, HEADS, ML_DH + 1], ar + 16 * T)
        o0 = ar + 20 * T + 96
        small = at("small", [P, N_TOK], o0)
        tmp = at("tmp", [P, N_TOK], o0 + T)
        reset = at("reset", [P, 2, N_TOK + 1], o0 + 2 * T)
        o1 = o0 + 2 * T + 6176
        cmask = at("cmask", [P, 4, P], o1)
        sel = at("sel", [P, 2, 64], o1 + 2048)
        aup = at("aup", [P, 2, 256], o1 + 2560)
        wend = at("wend", [P, TILES, 64], o1 + 4608)
        gdec = at("gdec", [P, 4, N_TOK // GLA_CHUNK], o1 + 6144)
        o2 = o1 + 6336
        rope = at("rope", [P, 4, N_LAT], o2)
        xs = at("xs", [P, N_LAT], o2 + 8192)
        cum = at("cum", [P, 4, N_TOK], o2 + 10240)
        assert o2 + 10240 + 4 * T <= AR_END
        qd = at("qd", [P, 4, N_TOK], u_off)
        kd = at("kd", [P, 4, N_TOK], u_off + 4 * T)
        gla_o = at("gla_o", [P, HEADS, N_TOK], u_off + 12 * T)
        gsc = at("gsc", [P, 2, 2, GLA_PAIRS, P], o2)
        gktok = at("gktok", [P, 2, 2 * P], o2 + 4096)
        gT = at("gT", [P, 2, GLA_PAIRS, 2, P], o2 + 6144)
        gS = at("gS", [P, 2, 2, GLA_PAIRS, 2, P], o2 + 10240)
        rA = at("rA", [64, N_TOK], u_off + 8 * T)
        rB = at("rB", [64, N_TOK], u_off + 9 * T)
        rP = at("rP", [64, N_TOK], u_off + 10 * T)
        rI = at("rI", [64, N_TOK], u_off + 11 * T)
        mktok = at("mktok", [P, TILES, 512], u_off)
        ml_t = at("ml_t", [P, TILES, HEADS, P], ar)
        ml_o = at("ml_o", [P, HEADS, N_TOK], ar + 4 * T)
        mD = at("mD", [P, 2, HEADS, P], o2)
        msc = at("msc", [P, 2, HEADS, P], o2 + 4096)
        mqs = at("mqs", [P, 2, HEADS, P], o2 + 8192)
        mC = at("mC", [P, 2, HEADS, ML_DH + 1], o2 + 12288)
        mks = at("mks", [P, 2, HEADS, P], u_off + 4 * T)
        guard = at("guard", [P, TILES, 64], u_off + 4 * T + 4096)
        mden = at("mden", [P, 2, 2], u_off + 4 * T + 5632)
        assert o2 + 12288 + 8192 <= AR_END
        c_early = at("c_early", [P, 2, D], ar + 16 * T)
        c_late = at("c_late", [P, 2, D], ar + FT * T + 18528)
        left_early = at("left_early", [P, D], ar + 16 * T + 8192)
        left_late = at("left_late", [P, D], ar + FT * T + 18528 + 8192)
        gsq = at("gsq", [P, 2, N_TOK], ar + 8 * T)
        grt = at("grt", [P, KT, TILES], ar + 12 * T)
        gy = at("gy", [P, 2, N_TOK], ar + 10 * T)
        PADW = N_TOK + 4
        CW = N_TOK + 2
        L0C = N_CTX + 2
        hid = at("hid", [P, FT, N_TOK], ar)
        f0 = ar + FT * T
        apad = at("apad", [P, 2, PADW], f0)
        conv = at("conv", [P, 2, CW], f0 + 6176)
        gel = at("gel", [P, 2, CW], f0 + 12352)
        hsp = at("hsp", [P, 2, 2, N_TOK], f0 + 18528, F32R)
        assert f0 + 18528 + 4 * T <= AR_END
        naq = at("naq", [P, KT, N_LAT], ar)
        nak = at("nak", [P, KT, N_TOK], ar + 16384)
        nav = at("nav", [P, TILES, D], ar + 16384 + 8 * T)
        n0 = ar + 16384 + 16 * T
        nab = at("nab", [P, 2, NA_TILES, 256], n0)
        nas = at("nas", [P, 4, 512], n0 + 8192)
        nap = at("nap", [P, 2, 4, P], n0 + 16384)
        nay = at("nay", [P, 2, N_LAT], n0 + 20480)
        nast = at("nast", [P, 4, 4], n0 + 24576)
        assert n0 + 24640 <= AR_END

        ps = ctx.enter_context(nc.psum_tensor("ps", [P, 8, 512], F32))

        def sem(name):
            return Signal(ctx.enter_context(nc.semaphore(name)))

        vec_loaded, const_loaded, ident_loaded, x_again, out_stored, c_loaded, c_again = map(
            sem, ("vec_loaded", "const_loaded", "ident_loaded", "x_again", "out_stored", "c_loaded", "c_again"))
        raw_loaded = [sem(f"raw_loaded{i}") for i in range(RAW_SLOTS)]
        x_loaded = sem("x_loaded")
        bias_loaded = [sem(f"bias_loaded{i}") for i in range(2)]
        hi_ready, lo_ready, block_used = map(sem, ("hi_ready", "lo_ready", "block_used"))
        mod_done = sem("mod_done")
        act_own, dve_own = map(sem, ("act_own", "dve_own"))
        ones_ready, c_ready, pre_ready = map(sem, ("ones_ready", "c_ready", "pre_ready"))

        norm_root, norm_rt, norm_spread = map(sem, ("norm_root", "norm_rt", "norm_spread"))

        class Norm:
            def __init__(self, n, direct):
                self.cx_bank = 5 if n == 1 else 7
                self.sq, self.nt, self.acc = later_norm if n else first_norm
                self.direct = direct
                self.acc_added = sem(f"norm{n}_acc_added")
                self.turn = n + 1
                self.sq_ready = sem(f"norm{n}_sq_ready")
                self.sq_summed = sem(f"norm{n}_sq_summed")
                self.t_ready = sem(f"norm{n}_t_ready")
                self.hi_ready = sem(f"norm{n}_hi_ready")
                self.lo_ready = sem(f"norm{n}_lo_ready")
        norm = [Norm(n, direct) for n, direct in enumerate((1, KT - 1, 4, KT - 1, 4))]
        (in_act_took, in_dve_took, xs_used, apre_done, apre_taken, apre_log, cum_ready, v_act, v_dve,
         rows_done, rows_taken, row_ln, row_args, row_exp, wend_turned, wend_ready,
         dec_exp, dec_ready, state_zero) = map(sem, (
             "in_act_took", "in_dve_took", "xs_used", "apre_done", "apre_taken", "apre_log", "cum_ready", "v_act",
             "v_dve", "rows_done", "rows_taken", "row_ln", "row_args", "row_exp",
             "wend_turned", "wend_ready", "dec_exp", "dec_ready", "state_zero"))
        ga_done, gsc_ready, gktok_ready, gkv_done, gS_ready, gT_ready, gi_done, go_taken = map(sem, (
            "ga_done", "gsc_ready", "gktok_ready", "gkv_done", "gS_ready", "gT_ready", "gi_done", "go_taken"))
        ktok_turned, ktok_ready, mC_zero = map(sem, ("ktok_turned", "ktok_ready", "mC_zero"))
        ml_lw, ml_sc, ml_iw, lw_ready, mD_ready, mqs_ready, iw_taken, msc_ready, mks_ready = map(sem, (
            "ml_lw", "ml_sc", "ml_iw", "lw_ready", "mD_ready", "mqs_ready", "iw_taken", "msc_ready", "mks_ready"))
        out_turned, out_ready, mkv_done, mC_ready, mh_done, mden_ready, mh_taken = map(sem, (
            "out_turned", "out_ready", "mkv_done", "mC_ready", "mh_done", "mden_ready", "mh_taken"))
        g_rt, g_spread, g_scaled, g_sq, g_sum, g_root, g_y, g_hi, g_lo = map(sem, ("g_rt", "g_spread", "g_scaled", "g_sq", "g_sum", "g_root", "g_y", "g_hi", "g_lo"))

        class Ffn:
            def __init__(self, n):
                self.norm = norm[2 * n + 2]
                self.pad_zero = sem(f"ffn{n}_pad_zero")
                self.a_taken = sem(f"ffn{n}_a_taken")
                self.c_ready = sem(f"ffn{n}_c_ready")
                self.conv_done = sem(f"ffn{n}_conv_done")
                self.gel_ready = sem(f"ffn{n}_gel_ready")
                self.g_taken = sem(f"ffn{n}_g_taken")
                self.hh_ready = sem(f"ffn{n}_hh_ready")
                self.hl_ready = sem(f"ffn{n}_hl_ready")
                self.hid_used = sem(f"ffn{n}_hid_used")
                self.h_updated = sem(f"ffn{n}_h_updated")
                self.out_updated = sem(f"ffn{n}_out_updated")
        ffn = [Ffn(n) for n in range(2)]
        (qk_taken, nav_act, nav_dve, s_done, s_ctx, s_lat, neg_max, p_exp, p_ready, p_turned, pt_ready,
         o_done, y_taken, y_hi, y_lo, bias_used) = map(sem, (
             "qk_taken", "nav_act", "nav_dve", "s_done", "s_ctx", "s_lat", "neg_max", "p_exp", "p_ready",
             "p_turned", "pt_ready", "o_done", "y_taken", "y_hi", "y_lo", "bias_used"))

        ORDER = [list(range(TILES)), [1, 0, 5, 4, 3, 2]]
        UNITS = [(n, z, ORDER[z][n]) for n in range(TILES) for z in range(2)]
        seen, FRESH = set(), []
        for _, _, i in UNITS:
            FRESH.append(i not in seen)
            seen.add(i)

        def tile(i):
            return slice(P * i, P * i + P)

        def halves(t):
            return ((CTX, 1), (LAT, 0))

        def blocks(eng_loop, per, count, body, first=4, last=0):
            for n in range(min(first, count)):
                body(n, 0)
            turns = (count - first - last) // 4
            if turns > 0:
                with eng_loop(turns, per) as i:
                    for n in range(first, first + 4):
                        body(n, i)
            for n in range(first + 4 * max(turns, 0), count):
                body(n, 0)

        def kv_bank(un, c):
            return (3, 4, 7)[(2 * un + c) % 3]

        def s_count(s, i):
            return s + 4 * i + 1

        def at_(t, col, off):
            if isinstance(off, int):
                return lambda n: t[:, col + off + n:col + off + n + 1]
            return lambda n: t[:, bass.ds(off + (col + n), 1)]

        def hid_at(k, i, toks, step=8):
            if isinstance(i, int):
                return hid[:, k + step * i, toks]
            return hid[:, bass.ds(i * step + k, 1), toks].rearrange("p a n -> p (a n)")

        def cx_bank(n):
            return ps[:, 2 if n % 2 == 0 else 7, 0:N_CTX]

        block = ctx.enter_context(nc.Block())

        @block.sync
        def _(sp):
            sp.dma_start(c_early[:, :, :], c_rows).then_inc(c_loaded.sem, 16)

            def load(r, i, used, least, turn=4):
                if used is not None:
                    sp.wait_ge(used.sem, least + 4 * i)
                src = weights[r] if isinstance(i, int) else \
                    weights[bass.ds(i * turn + r, 1), :, :].rearrange("a p n -> (a p) n")
                sp.dma_start(raw[:, r % 4, :], src).then_inc(raw_loaded[r % 4].sem, 16)

            def run(a, b, used, least):
                turns = (b - a) // 4
                if turns > 1:
                    with sp.Fori(0, turns) as i:
                        for n in range(4):
                            load(a + n, i, used, least + n)
                    a, least = a + 4 * turns, least + 4 * turns
                for n in range(b - a):
                    load(a + n, 0, used, least + n)

            for r in range(RAW_SLOTS):
                load(r, 0, None, 0)
            sp.dma_start(vec[:, :], vecs).then_inc(vec_loaded.sem, 16)
            sp.dma_start(ident[:, :], consts_d[:, 0:P]).then_inc(ident_loaded.sem, 16)
            for k in range(KT):
                sp.dma_start(h[:, k, :], xT[:, k, :]).then_inc(x_loaded.sem, 16)
            run(RAW_SLOTS, MOD_FIRST, mod_done, 1)
            sp.dma_start(rope[:, :, :], rope_d).then_inc(const_loaded.sem, 16)
            sp.dma_start(sel[:, :, :], consts_d[:, P:2 * P].rearrange("p (a b) -> p a b", a=2)).then_inc(const_loaded.sem, 16)
            sp.dma_start(cmask[:, :, :], consts_d[:, 2 * P:6 * P].rearrange("p (a b) -> p a b", a=4)).then_inc(const_loaded.sem, 16)
            sp.dma_start(reset[:, :, :], reset_d).then_inc(const_loaded.sem, 16)
            sp.dma_start(aup[:, :, :], a_up_d).then_inc(const_loaded.sem, 16)
            for s in range(2):
                load(raw_index(s), 0, mod_done, MOD_FIRST - 3 + 2 * s)
                load(raw_index(s) + 1, 0, mod_done, MOD_FIRST - 2 + 2 * s)
            for s in range(2, 4):
                load(raw_index(s), 0, lo_ready, s - 1)
                load(raw_index(s) + 1, 0, mod_done, MOD_FIRST + s - 1)
            with sp.Fori(0, (S_MIX - 4) // 4) as i:
                for s in range(4, 8):
                    load(raw_index(s), i, lo_ready, s - 1, turn=8)
                    load(raw_index(s) + 1, i, mod_done, MOD_FIRST + s - 1, turn=8)
            for s in range(S_MIX, S_MIX + 4):
                if s % 2 == 0:
                    load(raw_index(s), 0, lo_ready, S_MIX - 1 + (s - S_MIX) // 2)
                else:
                    load(raw_index(s), 0, mod_done, MOD_TILES - 1 + (s - S_MIX) // 2)
            run(raw_index(S_MIX + 4), raw_index(S_END), lo_ready, S_MIX + 1)
            for k in range(KT):
                sp.wait_ge(norm[4].t_ready.sem, k + 1)
                sp.dma_start(outT[:, k, :], fout[:, k, :]).then_inc(out_stored.sem, 16)
            sp.wait_ge(out_stored.sem, 16 * KT)

        @block.gpsimd
        def _(pool):
            own = Own(pool)
            pool.memset(ones[:, :], 1.0).then_inc(*own.one(ones_ready))
            pool.memset(epsc[:, :], EPS).then_inc(*own.one(ones_ready))

            def low(s, i):
                pool.wait_ge(*own.last())
                pool.wait_ge(hi_ready.sem, s_count(s, i))
                pool.tensor_tensor(wsp[:, s % 2, 1, :], raw[:, raw_index(s) % 4, :],
                                   wsp[:, s % 2, 0, :].bitcast(F32), ALU.subtract).then_inc(*own.one(lo_ready))

            blocks(own.loop, {lo_ready: 4}, S_MIX, low)
            blocks(own.loop, {lo_ready: 4}, S_END - S_MIX, lambda n, i: low(S_MIX + n, i))

        @block.scalar
        def _(act):
            own = Own(act)

            def high(s, i=0):
                if isinstance(i, int):
                    if s + 4 * i >= S_END:
                        return
                act.wait_ge(*own.last())
                raw_s = raw_index(s)
                act.wait_ge(raw_loaded[raw_s % 4].sem, 16 * (raw_s // 4 + 1) + 4 * raw_turn(s) * i)
                if s >= 2:
                    act.wait_ge(block_used.sem, s_count(s, i) - 2)
                act.activation(wsp[:, s % 2, 0, :], raw[:, raw_s % 4, :], ACT.Copy).then_inc(*own.one(hi_ready))

            act.wait_ge(c_loaded.sem, 16)
            act.activation(c_early[:, :, :], c_early[:, :, :], ACT.Silu).then_inc(*own.one(c_ready))

            def square(q, k, toks, updated):
                act.wait_ge(*own.last())
                act.wait_ge(*updated)
                if 3 <= k and k - 2 < q.direct:
                    act.wait_ge(q.acc_added.sem, k - 2)
                elif k >= 3:
                    act.wait_ge(q.sq_summed.sem, k - q.direct)
                dst = q.sq[:, k % 2, toks] if k else q.acc[:, toks]
                act.activation(dst, h[:, k, toks], ACT.Square).then_inc(*own.one(q.sq_ready))

            def normalise(q, B, toks, permute=False):
                first = toks.start // P
                act.wait_ge(ones_ready.sem, 2)
                act.wait_ge(q.sq_summed.sem, KT - q.direct + 1)
                act.wait_ge(*own.last())
                act.activation(rt[:, first:], ps[:, q.cx_bank, 2 * first:2 * TILES:2], ACT.Sqrt, bias=epsc[:, 0:1],
                               scale=1.0 / D).then_inc(*own.one(norm_root))
                if B is None:
                    return
                for k in range(KT):
                    act.wait_ge(q.t_ready.sem, k + 1)
                    act.wait_ge(*own.last())
                    if toks != LAT:
                        act.activation(u[:, k, 0, CTX], q.nt[:, k % 2, CTX], ACT.Identity, bias=B(k, 1))\
                           .then_inc(*own.one(act_own))
                    dst, src = u[:, k, 0, LAT], q.nt[:, k % 2, LAT]
                    if permute:
                        act.activation(src, src, ACT.Identity, bias=B(k, 0)).then_inc(*own.one(act_own))
                        act.wait_ge(*own.last())
                        act.activation(dst.rearrange("p (g r c) -> p r g c", g=8, c=8),
                                       src.rearrange("p (r g c) -> p r g c", g=8, c=8), ACT.Copy)\
                           .then_inc(*own.one(q.hi_ready))
                    else:
                        act.activation(dst, src, ACT.Identity, bias=B(k, 0)).then_inc(*own.one(q.hi_ready))

            def out_projection(s0, q, f, toks):
                for m in range(N_OUT):
                    act.wait_ge(block_used.sem, s0 + m + 1)
                    high(s0 + m + 2)
                    if m:
                        square(q, m - 1, toks, (f.out_updated.sem, m))
                square(q, KT - 1, toks, (f.out_updated.sem, KT))

            def shift(layer, part):
                return lambda k, r: modm[:, (layer * MOD_PARTS + part) * KT + k, r:r + 1]

            act.wait_ge(vec_loaded.sem, 16)
            all_tokens = slice(0, N_TOK)
            for k in range(KT):
                square(norm[0], k, all_tokens, (x_loaded.sem, 16 * KT))
            high(0)
            high(1)
            normalise(norm[0], shift(0, 0), all_tokens)

            def log_sigmoid_parts(src_abs, rows, out_signal):
                act.wait_ge(*own.last())
                act.activation(tmp[0:rows, :], src_abs, ACT.Abs).then_inc(*own.one(act_own))
                act.wait_ge(*own.last())
                act.activation(tmp[0:rows, :], tmp[0:rows, :], ACT.Exp, scale=-1.0).then_inc(*own.one(act_own))
                act.wait_ge(*own.last())
                act.activation(tmp[0:rows, :], tmp[0:rows, :], ACT.Ln, bias=1.0).then_inc(*own.one(out_signal))

            def decay_logs(zp):
                b = 3 + 2 * (zp % 2)
                act.wait_ge(apre_done.sem, zp + 1)
                for t, bank, w in ((LAT, b, N_LAT), (CTX, b + 1, N_CTX)):
                    act.wait_ge(*own.last())
                    act.activation(cum[:, zp, t], ps[:, bank, 0:w], ACT.Identity,
                                   bias=vec[:, V_ABIAS + zp:V_ABIAS + zp + 1]).then_inc(*own.one(apre_taken))
                if zp:
                    act.wait_ge(cum_ready.sem, zp)
                log_sigmoid_parts(cum[:, zp, :], P, apre_log)

            act.wait_ge(const_loaded.sem, 16 * 5)
            for n in range(N_IN):
                act.wait_ge(block_used.sem, n + 1)
                high(n + 2)
                lat, cx = ps[:, n % 2, :], cx_bank(n)
                act.wait_ge(*own.last())
                if n == 0:
                    act.activation(small[:, CTX], cx, ACT.Copy).then_inc(*own.one(act_own))
                    act.activation(small[:, LAT], lat, ACT.Copy).then_inc(*own.one(in_act_took))
                elif n <= 12:
                    dst = gqk[:, n - 1, :] if n <= 4 else mqk[:, n - 5, :]
                    half = GLA_DK // 2 if n <= 4 else ML_DH // 2
                    act.activation(dst[:, CTX], cx, ACT.Copy, scale=q_scale(n)).then_inc(*own.one(act_own))
                    if n >= 2:
                        act.wait_ge(xs_used.sem, n - 1)
                    for a in range(0, P, half):
                        b = a ^ half
                        last = a + half == P
                        act.activation(xs[a:a + half, :], ps[b:b + half, n % 2, :], ACT.Copy)\
                           .then_inc(*own.one(in_act_took if last else act_own))
                else:
                    f = n - 13
                    func = ACT.Silu if f < 4 else ACT.Sigmoid
                    act.activation(gates[:, f, CTX], cx, func).then_inc(*own.one(act_own))
                    act.activation(gates[:, f, LAT], lat, func).then_inc(*own.one(in_act_took))
                if n in (2, 10):
                    decay_logs(0 if n == 2 else 2)
                    decay_logs(1 if n == 2 else 3)
            for cg, dst in enumerate((gv, mv)):
                for b in range(4):
                    act.wait_ge(block_used.sem, S_V + 4 * cg + b + 1)
                    high(S_V + 4 * cg + b + 2)
                if cg == 1:
                    act.wait_ge(mod_done.sem, MOD_FIRST + S_OUT0)
                for i in range(0, TILES, 2):
                    act.wait_ge(*own.last())
                    out, src = (dst[:, i, :], ps[:, i, :]) if cg == 0 else \
                        (dst[:, i, :, 0:ML_DH], ps[:, i, :].rearrange("p (a b) -> p a b", a=HEADS))
                    act.activation(out, src, ACT.Copy).then_inc(*own.one(v_act))

            for zp in range(4):
                act.wait_ge(cum_ready.sem, 4)
                act.wait_ge(*own.last())
                act.activation(qd[:, zp, :], cum[:, zp, :], ACT.Exp, scale=1.0 / GLA_TAU).then_inc(*own.one(act_own))
                act.activation(kd[:, zp, :], cum[:, zp, :], ACT.Exp, scale=-1.0 / GLA_TAU).then_inc(*own.one(act_own))
                end = GLA_CHUNK - 1 if zp < 2 else 0
                act.activation(gdec[:, zp, :], cum[:, zp, end::GLA_CHUNK], ACT.Exp, scale=1.0 / GLA_TAU)\
                   .then_inc(*own.one(dec_exp))

            act.wait_ge(rows_done.sem, 2)
            for row, b, col in ((rA, 3, 0), (rB, 5, 1)):
                for t, bank, w in ((LAT, b, N_LAT), (CTX, b + 1, N_CTX)):
                    act.wait_ge(*own.last())
                    act.activation(row[:, t], ps[0:64, bank, 0:w], ACT.Identity,
                                   bias=vec[0:64, V_GATEB + col:V_GATEB + col + 1]).then_inc(*own.one(rows_taken))
            act.wait_ge(cum_ready.sem, 4)
            log_sigmoid_parts(rB[:, :], 64, row_ln)

            def row_exps():
                act.wait_ge(row_args.sem, 1)
                act.wait_ge(*own.last())
                act.activation(rI[:, :], rI[:, :], ACT.Exp).then_inc(*own.one(row_exp))
                act.activation(tmp[0:64, :], tmp[0:64, :], ACT.Exp).then_inc(*own.one(row_exp))
                act.activation(rB[:, :], rB[:, :], ACT.Exp, scale=-1.0).then_inc(*own.one(row_exp))

            def keys_turned(un):
                act.wait_ge(ga_done.sem, un + 1)
                act.wait_ge(*own.last())
                if un >= 2:
                    act.wait_ge(gkv_done.sem, 2 * (un - 1))
                act.activation(gktok[:, un % 2, :], ps[:, 2, 0:2 * P], ACT.Copy).then_inc(*own.one(gktok_ready))

            keys_turned(0)
            act.wait_ge(state_zero.sem, 1)
            for un, (n, z, i) in enumerate(UNITS):
                if un + 1 < len(UNITS):
                    keys_turned(un + 1)
                for c in range(2):
                    if c == 1:
                        before = 2 * i + (0 if z == 0 else 1)
                    else:
                        j = ORDER[z][n - 1] if n else i
                        before = 2 * j + (1 if z == 0 else 0)
                    if un >= 2:
                        act.wait_ge(gi_done.sem, 2 * (un - 2) + c + 1)
                        act.wait_ge(gT_ready.sem, 2 * (un - 1))
                    if c == 1:
                        act.wait_ge(gT_ready.sem, 2 * un + 1)
                    act.wait_ge(*own.last())
                    for p in range(GLA_PAIRS):
                        zp = 2 * z + p
                        act.activation(gS[:, z, c, p, :, :], gT[:, z, p, :, :], ACT.Copy,
                                       scale=gdec[:, zp, before:before + 1])\
                           .then_inc(*own.one(gS_ready if p else act_own))
                if un == 6:
                    row_exps()

            act.wait_ge(wend_turned.sem, 1)
            act.wait_ge(*own.last())
            act.activation(wend[:, :, :], ps[:, 5, 0:TILES * 64].rearrange("p (i r) -> p i r", r=64), ACT.Copy)\
               .then_inc(*own.one(wend_ready))
            act.activation(guard[:, :, :], ps[:, 6, 0:TILES * 64].rearrange("p (i r) -> p i r", r=64), ACT.Copy)\
               .then_inc(*own.one(act_own))
            for i in range(TILES):
                act.wait_ge(ktok_turned.sem, i + 1)
                act.wait_ge(*own.last())
                act.activation(mktok[:, i, :], ps[:, i % 2, :], ACT.Copy).then_inc(*own.one(ktok_ready))
            for un, (n, z, i) in enumerate(UNITS):
                b = un % 2
                act.wait_ge(*own.last())
                if un >= 2:
                    act.wait_ge(mkv_done.sem, un - 1)
                for hd in range(HEADS):
                    r = 32 * z + hd
                    act.activation(mks[:, b, hd, :], mktok[:, i, tile(hd)], ACT.Copy, scale=wend[:, i, r:r + 1])\
                       .then_inc(*own.one(mks_ready if hd == HEADS - 1 else act_own))
                act.wait_ge(lw_ready.sem, un + 1)
                act.activation(mD[:, b, :, :], mD[:, b, :, :], ACT.Exp).then_inc(*own.one(mD_ready))

            for i in range(TILES):
                act.wait_ge(out_turned.sem, i + 1)
                act.wait_ge(*own.last())
                act.activation(ml_o[:, :, tile(i)], ps[:, i % 2, :].rearrange("p (a b) -> p a b", a=HEADS), ACT.Copy)\
                   .then_inc(*own.one(out_ready))

            act.wait_ge(go_taken.sem, len(UNITS))
            act.wait_ge(mh_taken.sem, len(UNITS))
            act.wait_ge(mC_ready.sem, len(UNITS))
            act.dma_start(c_late[:, :, :], c_rows).then_inc(c_again.sem, 16)
            for f in range(KT):
                act.wait_ge(*own.last())
                if f >= 2:
                    act.wait_ge(g_sum.sem, f - 1)
                o = gla_o[:, f, :] if f < 4 else ml_o[:, f - 4, :]
                act.activation(gsq[:, f % 2, :], o, ACT.Square).then_inc(*own.one(g_sq))
            act.wait_ge(g_sum.sem, KT)
            act.activation(grt[:, :, :], ps[:, 2, 0:2 * KT * TILES:2].rearrange("p (f i) -> p f i", i=TILES), ACT.Sqrt,
                           bias=epsc[:, 0:1], scale=1.0 / P).then_inc(*own.one(g_root))
            for f in range(KT):
                act.wait_ge(g_y.sem, f + 1)
                act.wait_ge(*own.last())
                act.activation(u[:, f, 0, :], gy[:, f % 2, :], ACT.Copy).then_inc(*own.one(g_hi))
            act.wait_ge(c_again.sem, 16)
            act.wait_ge(*own.last())
            act.activation(c_late[:, :, :], c_late[:, :, :], ACT.Silu).then_inc(*own.one(c_ready))
            act.dma_start(h[:, :, :], xT).then_inc(x_again.sem, 16)
            out_projection(S_OUT0, norm[1], ffn[0], all_tokens)

            def feed_forward(q, layer, s_up, s_down, toks):
                lo, w = (0, CW) if layer == 0 else (L0C, N_LAT)
                cv = V_CONV + layer * FT * 4

                def up(n, i):
                    j, par = n // 2, (n // 2) % 2
                    act.wait_ge(block_used.sem, s_count(s_up + n, i))
                    high(s_up + n + 2, i)
                    act.wait_ge(*own.last())
                    if n % 2 == 0:
                        if n == 0:
                            act.wait_ge(q.pad_zero.sem, 1)
                        if j >= 2:
                            act.wait_ge(q.conv_done.sem, j - 1 + 2 * i)
                            act.wait_ge(q.gel_ready.sem, j - 1 + 2 * i)
                        if layer == 0:
                            act.activation(apad[:, par, 1:1 + N_CTX], cx_bank(0), ACT.Copy)\
                               .then_inc(*own.one(act_own))
                        act.activation(apad[:, par, L0C + 1:L0C + 1 + N_LAT], ps[:, 0, :], ACT.Copy)\
                           .then_inc(*own.one(q.a_taken))
                        act.wait_ge(*own.last())
                        c = at_(vec, cv + 4 * j, 8 * i)
                        act.activation(conv[:, par, lo:lo + w], apad[:, par, lo + 1:lo + 1 + w], ACT.Identity,
                                       bias=c(3), scale=c(1)).then_inc(*own.one(q.c_ready))
                    else:
                        act.wait_ge(q.conv_done.sem, j + 1 + 2 * i)
                        if j >= 2:
                            act.wait_ge(q.g_taken.sem, j - 1 + 2 * i)
                        act.activation(gel[:, par, lo:lo + w], conv[:, par, lo:lo + w], ACT.Gelu_apprx_tanh)\
                           .then_inc(*own.one(q.gel_ready))

                blocks(own.loop, {hi_ready: 4, q.a_taken: 2, q.c_ready: 2, q.gel_ready: 2,
                                  **({act_own: 2} if layer == 0 else {})}, N_UP, up, last=4 if layer == 0 else 0)

                def hidden_high(k, kx, i=0):
                    act.wait_ge(*own.last())
                    if k < 2:
                        act.wait_ge(q.g_taken.sem, FT)
                    if k >= 2 and k % 2 == 0:
                        act.wait_ge(q.hid_used.sem, k // 2 + 4 * i)
                    elif k >= 2:
                        act.wait_ge(block_used.sem, s_down + k // 2 + 4 * i)
                    act.activation(hsp[:, k % 2, 0, toks], hid_at(kx, i, toks), ACT.Copy)\
                       .then_inc(*own.one(q.hh_ready))

                hidden_high(0, 0)
                hidden_high(1, 1)

                def down(b, i):
                    g0 = b // (FT // 2) * (FT // 2)
                    for kk in range(2):
                        k = 2 * b + kk + 2
                        if k < 2 * FT:
                            hidden_high(k, k - (FT if k >= FT else 0), i)
                    act.wait_ge(block_used.sem, s_count(s_down + b, i))
                    high(s_down + b + 2, i)

                half = FT // 2
                for g0 in (0, half):
                    down(g0, 0)
                    if g0:
                        for k in range(M_GROUP):
                            square(q.norm, k, toks, (q.h_updated.sem, k + 1))
                    with own.loop(2, {q.hh_ready: 8, hi_ready: 4}) as i:
                        for b in range(g0 + 1, g0 + 5):
                            down(b, i)
                    for b in range(g0 + 9, g0 + half):
                        down(b, 0)
                for k in range(M_GROUP, KT):
                    square(q.norm, k, toks, (q.h_updated.sem, k + 1))

            normalise(norm[1], shift(0, 3), all_tokens)
            feed_forward(ffn[0], 0, S_UP0, S_DOWN0, slice(0, N_TOK))
            normalise(norm[2], shift(1, 0), all_tokens, permute=True)

            def qk(n, i, first):
                act.wait_ge(block_used.sem, s_count(S_QK + n, i))
                high(S_QK + n + 2, i)
                act.wait_ge(*own.last())
                lat, cx = ps[:, n % 2, :], cx_bank(n)
                if n < KT:
                    act.activation(naq[:, n, :], lat, ACT.Copy, scale=NA_DH ** -0.5).then_inc(*own.one(qk_taken))
                else:
                    act.activation(nak[:, n - KT, CTX], cx, ACT.Copy).then_inc(*own.one(act_own))
                    act.activation(nak[:, n - KT, LAT], lat, ACT.Copy).then_inc(*own.one(qk_taken))

            for n in range(N_QK):
                qk(n, 0, 0)
            for cg in range(2):
                for b in range(4):
                    act.wait_ge(block_used.sem, S_V1 + 4 * cg + b + 1)
                    high(S_V1 + 4 * cg + b + 2)
                for i in range(0, TILES, 2):
                    act.wait_ge(*own.last())
                    act.activation(nav[:, i, 512 * cg:512 * cg + 512], ps[:, i, :], ACT.Copy).then_inc(*own.one(nav_act))

            def load_bias(hd):
                act.dma_start(nab[:, hd % 2, :, :], na_bias_d[hd]).then_inc(bias_loaded[hd % 2].sem, 16)

            for hd in range(2):
                load_bias(hd)
            N_NA = NA_HEADS * NA_TILES
            for un in range(N_NA + 4):
                if un < N_NA:
                    act.wait_ge(*own.last())
                    act.wait_ge(s_done.sem, un + 1)
                    if un >= 4:
                        act.wait_ge(p_turned.sem, un - 3)
                    act.activation(nas[:, un % 4, 256:512], ps[:, 6 + un % 2, 0:256], ACT.Copy).then_inc(*own.one(s_ctx))
                if 1 <= un <= N_NA:
                    e = un - 1
                    act.wait_ge(neg_max.sem, e + 1)
                    act.wait_ge(*own.last())
                    act.activation(nas[:, e % 4, :], nas[:, e % 4, :], ACT.Exp, bias=nast[:, e % 4, 0:1],
                                   accum_out=nast[:, e % 4, 1:2]).then_inc(*own.one(p_exp))
                if un % NA_TILES == NA_TILES - 1 and un // NA_TILES + 2 < NA_HEADS:
                    hd = un // NA_TILES
                    act.wait_ge(bias_used.sem, hd + 1)
                    load_bias(hd + 2)
                if 3 <= un <= N_NA + 2:
                    e = un - 3
                    act.wait_ge(p_turned.sem, e + 1)
                    act.wait_ge(*own.last())
                    if e >= 2:
                        act.wait_ge(o_done.sem, e - 1)
                    act.activation(nap[:, e % 2, :, :], ps[:, 2 + e % 2, :].rearrange("p (a b) -> p a b", a=4), ACT.Copy)\
                       .then_inc(*own.one(pt_ready))
                if un >= 4 and (un - 4) % 8 == 7:
                    m = (un - 4) // 8
                    act.wait_ge(y_taken.sem, m + 1)
                    act.wait_ge(*own.last())
                    act.activation(u[:, m, 0, LAT], nay[:, m % 2, :], ACT.Copy).then_inc(*own.one(y_hi))
            out_projection(S_OUT1, norm[3], ffn[1], LAT)
            normalise(norm[3], shift(1, 3), LAT)
            feed_forward(ffn[1], 1, S_UP1, S_DOWN1, LAT)
            normalise(norm[4], None, LAT)

        @block.vector
        def _(dve):
            own = Own(dve)

            def modulate(m, i, early=True, cols=2):
                r = mod_raw_index(m)
                c, left = (c_early, left_early) if early else (c_late, left_late)
                dve.wait_ge(raw_loaded[r % 4].sem, 16 * (r // 4 + 1) + 32 * i)
                if own.newest:
                    dve.wait_ge(*own.last())
                for col in range(cols - 1, -1, -1):
                    out = modm[:, m, col:col + 1] if isinstance(i, int) else \
                        modm[:, bass.ds(i * 4 + m, 1), col:col + 1].rearrange("p a b -> p (a b)")
                    dve.scalar_tensor_tensor(out=raw[:, r % 4, :] if col == 0 else left[:, :], in0=raw[:, r % 4, :],
                                             scalar=1.0, in1=c[:, col, :], op0=ALU.mult, op1=ALU.mult,
                                             accum_out=out).then_inc(*own.one(mod_done if col == 0 else pre_ready))

            def take_mod(a, b):
                dve.wait_ge(*own.last())
                bias = vec[:, V_MODB + a:V_MODB + b].unsqueeze(2).to_broadcast([P, b - a, 2])
                dve.tensor_tensor(modm[:, a:b, :], modm[:, a:b, :], bias, ALU.add).then_inc(*own.one(dve_own))

            def norm_scale(idx):
                layer, ff = idx // 2, idx % 2
                sc = (layer * MOD_PARTS + 1 + 3 * ff) * KT
                w0 = (V_NFFN if ff else V_NMIX) + layer * KT
                w = vec[:, w0:w0 + KT].unsqueeze(2).to_broadcast([P, KT, 2])
                dve.wait_ge(*own.last())
                dve.scalar_tensor_tensor(out=amod[:, idx, :, :], in0=modm[:, sc:sc + KT, :], scalar=1.0, in1=w,
                                         op0=ALU.add, op1=ALU.mult).then_inc(*own.one(dve_own))

            def add_squares(q, k, toks):
                dve.wait_ge(q.sq_ready.sem, k + 1)
                dve.wait_ge(*own.last())
                dve.tensor_tensor(q.acc[:, toks], q.acc[:, toks], q.sq[:, k % 2, toks], ALU.add)\
                   .then_inc(*own.one(q.acc_added))

            def normalise(q, idx, B, toks, permute=False):
                first = toks.start // P
                dve.wait_ge(norm_root.sem, q.turn)
                dve.wait_ge(*own.last())
                dve.reciprocal(rt[:, first:], rt[:, first:]).then_inc(*own.one(norm_rt))
                dve.wait_ge(norm_spread.sem, q.turn)
                spread = {0: ps[:, 6, :], 1: ps[:, q.cx_bank, 0:N_CTX]}
                parts = ((CTX, 1), (LAT, 0)) if toks != LAT else ((LAT, 0),)
                if idx is None:
                    for k in range(KT):
                        dve.wait_ge(*own.last())
                        dve.scalar_tensor_tensor(out=fout[:, k, :], in0=h[:, k, LAT],
                                                 scalar=vec[:, V_NFIN + k:V_NFIN + k + 1], in1=spread[0],
                                                 op0=ALU.mult, op1=ALU.mult).then_inc(*own.one(q.t_ready))
                    return
                for k in range(KT + 1):
                    if k < KT:
                        dve.wait_ge(*own.last())
                        for t, r in parts:
                            dve.scalar_tensor_tensor(out=q.nt[:, k % 2, t], in0=h[:, k, t],
                                                     scalar=amod[:, idx, k, r:r + 1], in1=spread[r],
                                                     op0=ALU.mult, op1=ALU.mult)\
                               .then_inc(*own.one(q.t_ready if r == 0 else dve_own))
                    if k >= 1:
                        e = k - 1
                        dve.wait_ge(q.hi_ready.sem, e + 1)
                        dve.wait_ge(*own.last())
                        for t, r in parts:
                            src, hi, dst = q.nt[:, e % 2, t], u[:, e, 0, t].bitcast(F32), u[:, e, 1, t]
                            if permute and r == 0:
                                grid = lambda x: x.rearrange("p (g r c) -> p r g c", g=8, c=8)
                                dve.tensor_tensor(grid(dst), src.rearrange("p (r g c) -> p r g c", g=8, c=8),
                                                  grid(hi), ALU.subtract).then_inc(*own.one(q.lo_ready))
                            else:
                                dve.scalar_tensor_tensor(out=dst, in0=src, scalar=B(e, r), in1=hi, op0=ALU.add,
                                                         op1=ALU.subtract)\
                                   .then_inc(*own.one(q.lo_ready if r == 0 else dve_own))

            def shift(layer, part):
                return lambda k, r: modm[:, (layer * MOD_PARTS + part) * KT + k, r:r + 1]

            dve.memset(modm[:, :, :], 0.0).then_inc(*own.one(dve_own))
            dve.wait_ge(c_ready.sem, 1)
            for m in range(MOD_FIRST):
                modulate(m, 0)
            dve.wait_ge(vec_loaded.sem, 16)
            take_mod(0, MOD_FIRST)
            norm_scale(0)
            normalise(norm[0], 0, shift(0, 0), slice(0, N_TOK))

            def running_sum(zp):
                dve.wait_ge(apre_log.sem, zp + 1)
                dve.wait_ge(*own.last())
                dve.scalar_tensor_tensor(out=tmp[:, :], in0=cum[:, zp, :], scalar=0.0, in1=tmp[:, :],
                                         op0=ALU.min, op1=ALU.subtract).then_inc(*own.one(dve_own))
                dve.wait_ge(*own.last())
                if zp < 2:
                    dve.tensor_tensor_scan(cum[:, zp, :], reset[:, 0, 0:N_TOK], tmp[:, :], 0.0, ALU.mult, ALU.add)\
                       .then_inc(*own.one(cum_ready))
                else:
                    dve.tensor_tensor_scan(cum[:, zp, ::-1], reset[:, 0, N_TOK:0:-1], tmp[:, ::-1], 0.0,
                                           ALU.mult, ALU.add).then_inc(*own.one(cum_ready))

            dve.wait_ge(const_loaded.sem, 16 * 5)
            for n in range(N_IN):
                modulate(MOD_FIRST + n, 0)
                if not 1 <= n <= 12:
                    continue
                dve.wait_ge(block_used.sem, n + 1)
                dve.wait_ge(*own.last())
                dst = (gqk[:, n - 1, :] if n <= 4 else mqk[:, n - 5, :])[:, LAT]
                cos, sin = (0, 1) if n <= 4 else (2, 3)
                dve.wait_ge(in_act_took.sem, n + 1)
                dve.scalar_tensor_tensor(out=dst, in0=ps[:, n % 2, :], scalar=q_scale(n), in1=rope[:, cos, :],
                                         op0=ALU.mult, op1=ALU.mult).then_inc(*own.one(in_dve_took))
                dve.wait_ge(*own.last())
                dve.scalar_tensor_tensor(out=xs[:, :], in0=xs[:, :], scalar=q_scale(n), in1=rope[:, sin, :],
                                         op0=ALU.mult, op1=ALU.mult).then_inc(*own.one(dve_own))
                dve.wait_ge(*own.last())
                dve.tensor_tensor(dst, dst, xs[:, :], ALU.add).then_inc(*own.one(xs_used))
                if n in (2, 10):
                    running_sum(0 if n == 2 else 2)
                    running_sum(1 if n == 2 else 3)
            for cg, dst in enumerate((gv, mv)):
                for n in range(4):
                    modulate(MOD_FIRST + S_V + 4 * cg + n, 0)
                dve.wait_ge(block_used.sem, S_V + 4 * cg + 4)
                for i in range(1, TILES, 2):
                    dve.wait_ge(*own.last())
                    out, src = (dst[:, i, :], ps[:, i, :]) if cg == 0 else \
                        (dst[:, i, :, 0:ML_DH], ps[:, i, :].rearrange("p (a b) -> p a b", a=HEADS))
                    dve.tensor_copy(out, src).then_inc(*own.one(v_dve))

            dve.wait_ge(*own.last())
            dve.memset(mv[:, :, :, ML_DH:ML_DH + 1], 1.0).then_inc(*own.one(dve_own))
            take_mod(2 * KT, 5 * KT)
            norm_scale(1)
            for zp in range(4):
                dve.wait_ge(dec_exp.sem, zp + 1)
                dve.wait_ge(*own.last())
                dve.tensor_tensor(qd[:, zp, :], qd[:, zp, :], gqk[:, zp % 2, :], ALU.mult).then_inc(*own.one(dve_own))
                dve.tensor_tensor(kd[:, zp, :], kd[:, zp, :], gqk[:, 2 + zp % 2, :], ALU.mult)\
                   .then_inc(*own.one(dec_ready))
            dve.wait_ge(*own.last())
            dve.memset(gT[:, :, :, :, :], 0.0).then_inc(*own.one(state_zero))

            def step():
                dve.wait_ge(*own.last())
                return own.one(dve_own)

            def rows_sums():
                dve.wait_ge(row_ln.sem, 1)
                n = step()
                dve.scalar_tensor_tensor(out=rI[:, :], in0=rB[:, :], scalar=0.0, in1=tmp[0:64, :],
                                         op0=ALU.min, op1=ALU.subtract).then_inc(*n)
                n = step()
                dve.tensor_tensor_scan(rB[0:32, :], reset[0:32, 1, 0:N_TOK], rI[0:32, :], 0.0, ALU.mult, ALU.add)\
                   .then_inc(*n)
                n = step()
                dve.tensor_tensor_scan(rB[32:64, ::-1], reset[32:64, 1, N_TOK:0:-1], rI[32:64, ::-1], 0.0,
                                       ALU.mult, ALU.add).then_inc(*n)
                n = step()
                dve.tensor_tensor(rA[:, :], rA[:, :], rB[:, :], ALU.subtract).then_inc(*n)

            def rows_gains():
                n = step()
                dve.memset(rI[:, :], 0.0).then_inc(*n)
                n = step()
                dve.tensor_copy(rI[0:32, P::P], rB[0:32, P - 1:N_TOK - 1:P]).then_inc(*n)
                for z_i in range(1, TILES):
                    i, before = ORDER[1][z_i], ORDER[1][z_i - 1]
                    n = step()
                    dve.tensor_copy(rI[32:64, P * i + P - 1:P * i + P], rB[32:64, P * before:P * before + 1]).then_inc(*n)

            def rows_maxima():
                n = step()
                dve.tensor_tensor_scan(rP[0:32, :], rI[0:32, :], rA[0:32, :], 0.0, ALU.add, ALU.max).then_inc(*n)
                n = step()
                dve.tensor_tensor_scan(rP[32:64, N_CTX - 1::-1], rI[32:64, N_CTX - 1::-1], rA[32:64, N_CTX - 1::-1],
                                       0.0, ALU.add, ALU.max).then_inc(*n)
                n = step()
                dve.tensor_tensor_scan(rP[32:64, N_TOK - 1:N_CTX - 1:-1], rI[32:64, N_TOK - 1:N_CTX - 1:-1],
                                       rA[32:64, N_TOK - 1:N_CTX - 1:-1], rP[32:64, 0:1], ALU.add, ALU.max).then_inc(*n)
                n = step()
                dve.tensor_tensor(rB[:, :], rB[:, :], rP[:, :], ALU.add).then_inc(*n)

            def rows_starts():
                n = step()
                dve.memset(mstart[:, :], 0.0).then_inc(*n)
                for z in range(2):
                    rows = slice(32 * z, 32 * z + 32)
                    end = P - 1 if z == 0 else 0
                    for z_i in range(1, TILES):
                        i, before = ORDER[z][z_i], ORDER[z][z_i - 1]
                        n = step()
                        dve.tensor_copy(mstart[rows, i:i + 1], rB[rows, P * before + end:P * before + end + 1]).then_inc(*n)
                    n = step()
                    dve.tensor_copy(pend[rows, :], rP[rows, end::P]).then_inc(*n)

            def rows_weights():
                by_tile = lambda t: t.rearrange("p (i t) -> p i t", t=P)
                wide = lambda t: t.unsqueeze(2).to_broadcast([64, TILES, P])
                n = step()
                dve.tensor_tensor(by_tile(rI[:, :]), wide(mstart[:, :]), by_tile(rP[:, :]), ALU.subtract).then_inc(*n)
                n = step()
                dve.tensor_tensor(by_tile(tmp[0:64, :]), by_tile(rA[:, :]), wide(pend[:, :]), ALU.subtract).then_inc(*n)
                dve.wait_ge(*own.last())
                dve.tensor_scalar(rP[:, :], rP[:, :], -1.0, None, ALU.mult).then_inc(*own.one(row_args))

            cm = lambda z, neg: cmask[:, 2 * neg + z, :]

            def scores_masked(un):
                z, b = UNITS[un][1], un % 2
                dve.wait_ge(ga_done.sem, un + 1)
                dve.wait_ge(*own.last())
                if un >= 2:
                    dve.wait_ge(gi_done.sem, 2 * (un - 1))
                dve.tensor_tensor(gsc[:, b, :, :, :], ps[:, 0:2, 0:2 * P].rearrange("q b (p c) -> q b p c", p=2),
                                  cm(z, 0).unsqueeze(1).unsqueeze(1).to_broadcast([P, 2, GLA_PAIRS, P]), ALU.mult)\
                   .then_inc(*own.one(gsc_ready))

            rows_stages = (rows_sums, rows_gains, rows_maxima, rows_starts, rows_weights)
            scores_masked(0)
            for un, (n, z, i) in enumerate(UNITS):
                if un + 1 < len(UNITS):
                    scores_masked(un + 1)
                for c in range(2):
                    dve.wait_ge(gkv_done.sem, 2 * un + c + 1)
                    dve.wait_ge(gS_ready.sem, 2 * un + c + 1)
                    dve.wait_ge(*own.last())
                    for hh in range(2):
                        rows = slice(64 * hh, 64 * hh + 64)
                        dve.tensor_tensor(gT[rows, z, :, hh, :], gS[rows, z, c, :, hh, :],
                                          ps[rows, kv_bank(un, c), :].rearrange("q (p b c) -> q p b c", p=2, b=2)[:, :, hh, :],
                                          ALU.add).then_inc(*own.one(gT_ready if hh else dve_own))
                dve.wait_ge(gi_done.sem, 2 * un + 2)
                dve.wait_ge(*own.last())
                src = ps[:, 5 + un % 2, :].rearrange("p (a t) -> p a t", a=HEADS)
                dst = gla_o[:, :, tile(i)]
                if FRESH[un]:
                    dve.tensor_copy(dst, src).then_inc(*own.one(go_taken))
                else:
                    dve.tensor_tensor(dst, src, dst, ALU.add).then_inc(*own.one(go_taken))
                if un < len(rows_stages):
                    rows_stages[un]()

            dve.wait_ge(*own.last())
            dve.memset(mC[:, :, :, :], 0.0).then_inc(*own.one(mC_zero))
            four = lambda t: t.rearrange("p (a b) -> p a b", a=HEADS)

            def weigh(un):
                (n, z, i), b = UNITS[un], un % 2
                dve.wait_ge(ml_lw.sem, un + 1)
                dve.wait_ge(*own.last())
                dve.tensor_tensor(mD[:, b, :, :], four(ps[:, 0, :]),
                                  cm(z, 1).unsqueeze(1).to_broadcast([P, HEADS, P]), ALU.add)\
                   .then_inc(*own.one(lw_ready))
                dve.wait_ge(ml_iw.sem, un + 1)
                if un >= 2:
                    dve.wait_ge(mh_done.sem, un - 1)
                dve.tensor_tensor(mqs[:, b, :, :], mqk[:, 0:HEADS, tile(i)], four(ps[:, 2, :]), ALU.mult)\
                   .then_inc(*own.one(mqs_ready))
                dve.wait_ge(*own.last())
                end = P - 1 if z == 0 else 0
                dve.tensor_copy(mdec[:, b, :], ps[:, 2, end::P]).then_inc(*own.one(iw_taken))
                dve.wait_ge(mD_ready.sem, un + 1)
                dve.wait_ge(ml_sc.sem, un + 1)
                dve.tensor_tensor(msc[:, b, :, :], four(ps[:, 1, :]), mD[:, b, :, :], ALU.mult)\
                   .then_inc(*own.one(msc_ready))

            weigh(0)
            for un, (n, z, i) in enumerate(UNITS):
                if un + 1 < len(UNITS):
                    weigh(un + 1)
                b = un % 2
                dve.wait_ge(mh_done.sem, un + 1)
                if un == 0:
                    dve.wait_ge(wend_ready.sem, 1)
                    dve.wait_ge(ktok_ready.sem, 1)
                dve.wait_ge(*own.last())
                out = ps[:, 3:5, 0:2 * (ML_DH + 1)].rearrange("p a (b c) -> p a b c", b=2)
                r0 = 32 * z
                dve.scalar_tensor_tensor(out=mden[:, :, :], in0=out[:, :, :, ML_DH], scalar=-1.0,
                                         in1=guard[:, i, r0:r0 + HEADS].rearrange("p (a b) -> p a b", a=2),
                                         op0=ALU.mult, op1=ALU.max).then_inc(*own.one(dve_own))
                dve.wait_ge(*own.last())
                dve.tensor_tensor(mden[:, :, :], out[:, :, :, ML_DH], mden[:, :, :], ALU.max).then_inc(*own.one(dve_own))
                dve.wait_ge(*own.last())
                dve.reciprocal(mden[:, :, :], mden[:, :, :]).then_inc(*own.one(dve_own))
                dve.wait_ge(*own.last())
                for hd in range(HEADS):
                    dst, src, w = ml_t[:, i, hd, :], out[:, hd // 2, hd % 2, 0:ML_DH], mden[:, hd // 2, hd % 2:hd % 2 + 1]
                    last = own.one(mh_taken if hd == HEADS - 1 else dve_own)
                    if FRESH[un]:
                        dve.tensor_scalar(dst, src, w, None, ALU.mult).then_inc(*last)
                    else:
                        dve.scalar_tensor_tensor(out=dst, in0=src, scalar=w, in1=dst, op0=ALU.mult, op1=ALU.add)\
                           .then_inc(*last)
                dve.wait_ge(mkv_done.sem, un + 1)
                dve.wait_ge(*own.last())
                for hd in range(HEADS):
                    c0 = (ML_DH + 1) * (hd % 2)
                    dve.scalar_tensor_tensor(out=mC[:, z, hd, :], in0=mC[:, z, hd, :], scalar=mdec[:, b, hd:hd + 1],
                                             in1=ps[:, 5 + hd // 2, c0:c0 + ML_DH + 1], op0=ALU.mult, op1=ALU.add)\
                       .then_inc(*own.one(mC_ready if hd == HEADS - 1 else dve_own))

            dve.wait_ge(g_root.sem, 1)
            dve.wait_ge(*own.last())
            dve.reciprocal(grt[:, :, :], grt[:, :, :]).then_inc(*own.one(g_rt))
            for f in range(KT + 1):
                if f < KT:
                    o = gla_o[:, f, :] if f < 4 else ml_o[:, f - 4, :]
                    w = V_GLAN if f < 4 else V_MLN
                    dve.wait_ge(g_spread.sem, f + 1)
                    dve.wait_ge(*own.last())
                    for t, bank, n in ((CTX, 4, N_CTX), (LAT, 3, N_LAT)):
                        dve.scalar_tensor_tensor(out=gy[:, f % 2, t], in0=o[:, t], scalar=vec[:, w:w + 1],
                                                 in1=ps[:, bank + 2 * (f % 2), 0:n], op0=ALU.mult, op1=ALU.mult)\
                           .then_inc(*own.one(g_scaled if t == LAT else dve_own))
                    dve.wait_ge(*own.last())
                    dve.tensor_tensor(gy[:, f % 2, :], gy[:, f % 2, :], gates[:, f, :], ALU.mult).then_inc(*own.one(g_y))
                if f >= 1:
                    e = f - 1
                    dve.wait_ge(g_hi.sem, e + 1)
                    dve.wait_ge(*own.last())
                    dve.tensor_tensor(u[:, e, 1, :], gy[:, e % 2, :], u[:, e, 0, :].bitcast(F32), ALU.subtract)\
                       .then_inc(*own.one(g_lo))

            def gate_of(layer, part, m, r):
                c = (layer * MOD_PARTS + part) * KT + m
                return modm[:, c, r:r + 1]

            def add_out(q, s0, layer, toks):
                if layer == 0:
                    dve.wait_ge(c_ready.sem, 2)
                for m in range(N_OUT):
                    if layer == 0:
                        modulate(MOD_FIRST + S_OUT0 + m, 0, early=False)
                    dve.wait_ge(block_used.sem, s0 + m + 1)
                    dve.wait_ge(*own.last())
                    if layer == 0:
                        dve.scalar_tensor_tensor(out=h[:, m, CTX], in0=cx_bank(m),
                                                 scalar=gate_of(layer, 2, m, 1), in1=h[:, m, CTX],
                                                 op0=ALU.mult, op1=ALU.add).then_inc(*own.one(dve_own))
                    dve.scalar_tensor_tensor(out=h[:, m, LAT], in0=ps[:, m % 2, :], scalar=gate_of(layer, 2, m, 0),
                                             in1=h[:, m, LAT], op0=ALU.mult, op1=ALU.add)\
                       .then_inc(*own.one(q.out_updated))
                    if m >= 2:
                        add_squares(norm[2 * layer + 1], m - 1, toks)

            def feed_forward(q, layer, s_up, s_down, toks):
                lo, w = (0, CW) if layer == 0 else (L0C, N_LAT)
                cv = V_CONV + layer * FT * 4
                dve.wait_ge(*own.last())
                for c0 in (0, N_CTX + 1, L0C):
                    dve.memset(apad[:, :, c0:c0 + 1], 0.0).then_inc(*own.one(dve_own))
                dve.memset(apad[:, :, PADW - 1:PADW], 0.0).then_inc(*own.one(q.pad_zero))

                def modulations(j, i, cols):
                    for s in range(s_up + 2 * j, s_up + 2 * j + 2):
                        if s < S_MIX:
                            modulate(MOD_FIRST + s, i, early=False, cols=cols)

                def up(j, i):
                    par = j % 2
                    c = at_(vec, cv + 4 * j, 8 * i)
                    dve.wait_ge(q.c_ready.sem, j + 1 + 2 * i)
                    dve.wait_ge(*own.last())
                    dve.scalar_tensor_tensor(out=conv[:, par, lo:lo + w], in0=apad[:, par, lo:lo + w], scalar=c(0),
                                             in1=conv[:, par, lo:lo + w], op0=ALU.mult, op1=ALU.add)\
                       .then_inc(*own.one(dve_own))
                    dve.wait_ge(*own.last())
                    dve.scalar_tensor_tensor(out=conv[:, par, lo:lo + w], in0=apad[:, par, lo + 2:lo + 2 + w],
                                             scalar=c(2), in1=conv[:, par, lo:lo + w], op0=ALU.mult, op1=ALU.add)\
                       .then_inc(*own.one(q.conv_done))
                    dve.wait_ge(q.gel_ready.sem, j + 1 + 2 * i)
                    dve.wait_ge(block_used.sem, s_up + 2 * j + 2 + 4 * i)
                    if layer == 0:
                        dve.tensor_tensor(hid_at(j, i, CTX, 2), gel[:, par, 0:N_CTX], cx_bank(1), ALU.mult)\
                           .then_inc(*own.one(dve_own))
                    dve.tensor_tensor(hid_at(j, i, LAT, 2), gel[:, par, L0C:L0C + N_LAT], ps[:, 1, :], ALU.mult)\
                       .then_inc(*own.one(q.g_taken))

                given = {q.conv_done: 2, q.g_taken: 2, dve_own: 4 if layer == 0 else 2}
                if layer == 1:
                    for j in range(2):
                        up(j, 0)
                    with own.loop((FT - 2) // 2, given) as i:
                        for j in range(2, 4):
                            up(j, i)
                else:
                    both = 6
                    for j in range(2):
                        modulations(j, 0, 2)
                        up(j, 0)
                    with own.loop((both - 2) // 2, {**given, mod_done: 4, pre_ready: 4}) as i:
                        for j in range(2, 4):
                            modulations(j, i, 2)
                            up(j, i)
                    with own.loop((FT - 2 - both) // 2, {**given, mod_done: 4}) as i:
                        for j in range(both, both + 2):
                            modulations(j, i, 1)
                            up(j, i)
                    for j in range(FT - 2, FT):
                        modulations(j, 0, 1)
                        up(j, 0)
                    take_mod(6 * KT, MOD_TILES)
                    norm_scale(2)
                    norm_scale(3)

                def hidden_low(k, kx, i=0):
                    dve.wait_ge(q.hh_ready.sem, k + 1 + 8 * i)
                    dve.wait_ge(*own.last())
                    dve.tensor_tensor(hsp[:, k % 2, 1, toks], hid_at(kx, i, toks),
                                      hsp[:, k % 2, 0, toks].bitcast(F32), ALU.subtract)\
                       .then_inc(*own.one(q.hl_ready))

                def update(m, mm):
                    dve.wait_ge(*own.last())
                    if layer == 0:
                        dve.scalar_tensor_tensor(out=h[:, m, CTX],
                                                 in0=ps[:, 4 + mm // 2, 256 * (mm % 2):256 * (mm % 2) + 256],
                                                 scalar=gate_of(layer, 5, m, 1), in1=h[:, m, CTX],
                                                 op0=ALU.mult, op1=ALU.add).then_inc(*own.one(dve_own))
                    dve.scalar_tensor_tensor(out=h[:, m, LAT], in0=ps[:, mm, :], scalar=gate_of(layer, 5, m, 0),
                                             in1=h[:, m, LAT], op0=ALU.mult, op1=ALU.add)\
                       .then_inc(*own.one(q.h_updated))

                for g in range(2):
                    k0 = FT * g
                    for kx in range(2 * g, 6):
                        hidden_low(k0 + kx, kx)
                        if g and kx >= 3:
                            add_squares(q.norm, kx - 2, toks)
                    with own.loop((FT - 6) // 8, {q.hl_ready: 8}) as i:
                        for kx in range(6, 14):
                            hidden_low(k0 + kx, kx, i)
                    dve.wait_ge(block_used.sem, s_down + FT // 2 * (g + 1))
                    for mm in range(M_GROUP):
                        update(M_GROUP * g + mm, mm)
                        if g == 0 and mm % 2 == 1:
                            hidden_low(FT + mm // 2, mm // 2)

            dve.wait_ge(x_again.sem, 16)
            add_out(ffn[0], S_OUT0, 0, slice(0, N_TOK))
            take_mod(5 * KT, 6 * KT)
            normalise(norm[1], 1, shift(0, 3), slice(0, N_TOK))
            feed_forward(ffn[0], 0, S_UP0, S_DOWN0, slice(0, N_TOK))
            normalise(norm[2], 2, shift(1, 0), slice(0, N_TOK), permute=True)

            for cg in range(2):
                dve.wait_ge(block_used.sem, S_V1 + 4 * cg + 4)
                for i in range(1, TILES, 2):
                    dve.wait_ge(*own.last())
                    dve.tensor_copy(nav[:, i, 512 * cg:512 * cg + 512], ps[:, i, :]).then_inc(*own.one(nav_dve))

            N_NA = NA_HEADS * NA_TILES
            for un in range(N_NA + 4):
                if un < N_NA:
                    hd, j = un // NA_TILES, un % NA_TILES
                    if j == 0:
                        dve.wait_ge(bias_loaded[hd % 2].sem, 16 * (hd // 2 + 1))
                    dve.wait_ge(s_done.sem, un + 1)
                    if un >= 4:
                        dve.wait_ge(p_turned.sem, un - 3)
                    dve.wait_ge(*own.last())
                    dve.tensor_tensor(nas[:, un % 4, 0:256], ps[:, un % 2, 0:256], nab[:, hd % 2, j, :], ALU.add)\
                       .then_inc(*own.one(bias_used if j == NA_TILES - 1 else s_lat))
                if 2 <= un <= N_NA + 1:
                    x = (un - 2) % 4
                    dve.wait_ge(p_exp.sem, un - 1)
                    dve.wait_ge(*own.last())
                    dve.reciprocal(nast[:, x, 2:3], nast[:, x, 1:2]).then_inc(*own.one(dve_own))
                    dve.wait_ge(*own.last())
                    dve.tensor_scalar(nas[:, x, :], nas[:, x, :], nast[:, x, 2:3], None, ALU.mult)\
                       .then_inc(*own.one(p_ready))
                if un < N_NA:
                    dve.wait_ge(s_ctx.sem, un + 1)
                    dve.wait_ge(*own.last())
                    dve.tensor_reduce(nast[:, un % 4, 0:1], nas[:, un % 4, :], AX_X, ALU.max, negate=True)\
                       .then_inc(*own.one(neg_max))
                if un >= 4 and (un - 4) % 8 == 7:
                    m = (un - 4) // 8
                    dve.wait_ge(o_done.sem, un - 3)
                    dve.wait_ge(*own.last())
                    out = ps[:, 4 + m % 2, :].rearrange("p (g r c) -> p r g c", g=8, c=8)
                    dst = nay[:, m % 2, :].rearrange("p (r g c) -> p r g c", g=8, c=8)
                    dve.tensor_copy(dst[:, :, 1:8, :], out[:, :, 0:7, :]).then_inc(*own.one(dve_own))
                    dve.tensor_copy(dst[:, :, 0:1, :], out[:, :, 7:8, :]).then_inc(*own.one(y_taken))
                    dve.wait_ge(y_hi.sem, m + 1)
                    dve.wait_ge(*own.last())
                    dve.tensor_tensor(u[:, m, 1, LAT], nay[:, m % 2, :], u[:, m, 0, LAT].bitcast(F32),
                                      ALU.subtract).then_inc(*own.one(y_lo))

            add_out(ffn[1], S_OUT1, 1, LAT)
            normalise(norm[3], 3, shift(1, 3), LAT)
            feed_forward(ffn[1], 1, S_UP1, S_DOWN1, LAT)
            normalise(norm[4], None, None, LAT)

        @block.tensor
        def _(pe):
            own = Own(pe)

            def normalise(q, toks):
                first = toks.start // P
                pe.wait_ge(ones_ready.sem, 2)
                for k in range(q.direct - 1, KT):
                    pe.wait_ge(q.sq_ready.sem, k + 1)
                    if k == q.direct - 1:
                        src = q.acc
                        if k:
                            pe.wait_ge(q.acc_added.sem, k)
                    else:
                        src = q.sq[:, k % 2, :]
                    for i in range(first, TILES):
                        mm = pe.matmul(ps[:, q.cx_bank, 2 * i:2 * i + 2], src[:, tile(i)], ones[:, 0:2],
                                       start=(k == q.direct - 1 and i == first), stop=(k == KT - 1),
                                       skip_group_check=True)
                    mm.then_inc(*own.one(q.sq_summed))
                pe.wait_ge(norm_rt.sem, q.turn)
                for i in range(first, TILES):
                    out = ps[:, q.cx_bank, tile(i)] if i < N_CTX // P else ps[:, 6, tile(i - N_CTX // P)]
                    mm = pe.matmul(out, rt[:, i:i + 1].to_broadcast([P, P]), ident[:, :], start=True, stop=True)
                mm.then_inc(*own.one(norm_spread))

            PASSES = ((0, 0), (0, 1), (1, 0))

            def features(s, i, lat, cx, x, ready=None):
                pe.wait_ge(lo_ready.sem, s_count(s, i))
                for k in range(KT):
                    if ready is not None:
                        pe.wait_ge(ready.sem, k + 1)
                    for a, (wp, xp) in enumerate(PASSES):
                        w = wsp[:, s % 2, wp, tile(k)]
                        first, last = k == 0 and a == 0, k == KT - 1 and a == 2
                        if cx is not None:
                            pe.matmul(cx, w, x[:, k, xp, CTX], start=first, stop=last)
                        mm = pe.matmul(lat, w, x[:, k, xp, LAT], start=first, stop=last)
                mm.then_inc(*own.one(block_used))

            def tokens(s, b, taken):
                pe.wait_ge(lo_ready.sem, s + 1)
                for kk in range(2):
                    k = 2 * b + kk
                    for i in range(TILES):
                        if k == 0:
                            for q, n in taken:
                                pe.wait_ge(q.sem, n)
                        for a, (wp, xp) in enumerate(PASSES):
                            mm = pe.matmul(ps[:, i, :], u[:, k, xp, tile(i)], wsp[:, s % 2, wp, 512 * kk:512 * kk + 512],
                                           start=(k == 0 and a == 0), stop=(k == KT - 1 and a == 2),
                                           skip_group_check=True)
                mm.then_inc(*own.one(block_used))

            pe.wait_ge(ident_loaded.sem, 16)
            normalise(norm[0], slice(0, N_TOK))

            def projection(n, i=0):
                if n >= 2:
                    pe.wait_ge(in_act_took.sem, n - 1 + 4 * i)
                if 3 <= n <= 14:
                    pe.wait_ge(in_dve_took.sem, n - 2 + 4 * i)
                features(S_IN + n, i, ps[:, n % 2, :], cx_bank(n), u, norm[0].lo_ready if n == 0 else None)

            def decay_inputs(zp):
                b = 3 + 2 * (zp % 2)
                if zp >= 2:
                    pe.wait_ge(apre_taken.sem, 2 * (zp - 1))
                for t, bank, w in ((LAT, b, N_LAT), (CTX, b + 1, N_CTX)):
                    mm = pe.matmul(ps[:, bank, 0:w], aup[:, zp // 2, tile(zp % 2)], small[:, t], start=True, stop=True)
                mm.then_inc(*own.one(apre_done))

            for n in range(3):
                projection(n)
            pe.wait_ge(const_loaded.sem, 16 * 5)
            for zp in range(2):
                decay_inputs(zp)
            with own.loop(2, {block_used: 4}) as i:
                for n in range(3, 7):
                    projection(n, i)
            for zp in range(2, 4):
                decay_inputs(zp)
            for n in range(11, 15):
                projection(n)
            for n in range(15, N_IN):
                projection(n)

            for cg in range(2):
                taken = [(in_act_took, N_IN), (apre_taken, 8)] if cg == 0 else [(v_act, 3), (v_dve, 3)]
                for b in range(4):
                    tokens(S_V + 4 * cg + b, b, taken)

            pe.wait_ge(v_act.sem, 6)
            pe.wait_ge(v_dve.sem, 6)
            for c, b in ((0, 3), (1, 5)):
                for t, bank, w in ((LAT, b, N_LAT), (CTX, b + 1, N_CTX)):
                    mm = pe.matmul(ps[0:64, bank, 0:w], sel[:, c, :], small[:, t], start=True, stop=True)
                mm.then_inc(*own.one(rows_done))

            pe.wait_ge(dec_ready.sem, 4)
            pe.wait_ge(rows_taken.sem, 4)
            def gla_scores(un):
                n, z, i = UNITS[un]
                if un >= 1:
                    pe.wait_ge(gsc_ready.sem, un)
                    pe.wait_ge(gktok_ready.sem, un)
                for p in range(GLA_PAIRS):
                    zp = 2 * z + p
                    for hh in range(2):
                        rows = slice(64 * hh, 64 * hh + 64)
                        pe.matmul(ps[:, hh, P * p:P * p + P], kd[rows, zp, tile(i)], qd[rows, zp, tile(i)],
                                  start=True, stop=True)
                    mm = pe.transpose(ps[:, 2, P * p:P * p + P], kd[:, zp, tile(i)], ident[:, :])
                mm.then_inc(*own.one(ga_done))

            def gla_keys_values(un):
                n, z, i = UNITS[un]
                pe.wait_ge(gktok_ready.sem, un + 1)
                for c in range(2):
                    if 2 * un + c >= 3:
                        pe.wait_ge(gT_ready.sem, 2 * un + c - 2)
                    cc = c if z == 0 else 1 - c
                    rows = slice(64 * cc, 64 * cc + 64)
                    for p in range(GLA_PAIRS):
                        mm = pe.matmul(ps[:, kv_bank(un, c), 256 * p:256 * p + 256], gktok[rows, un % 2, tile(p)],
                                       gv[rows, i, 256 * p:256 * p + 256], start=True, stop=True)
                    mm.then_inc(*own.one(gkv_done))

            gla_scores(0)
            gla_keys_values(0)
            for un, (n, z, i) in enumerate(UNITS):
                if un + 1 < len(UNITS):
                    gla_scores(un + 1)
                pe.wait_ge(gsc_ready.sem, un + 1)
                if un >= 2:
                    pe.wait_ge(go_taken.sem, un - 1)
                for hd in range(HEADS):
                    pe.matmul(ps[:, 5 + un % 2, tile(hd)], gv[:, i, tile(hd)], gsc[:, un % 2, hd % 2, hd // 2, :],
                              start=(hd == 0), stop=False, skip_group_check=True)
                if un + 1 < len(UNITS):
                    gla_keys_values(un + 1)
                for c in range(2):
                    cc = c if z == 0 else 1 - c
                    pe.wait_ge(gS_ready.sem, 2 * un + c + 1)
                    for hd in range(HEADS):
                        t0 = 64 * cc
                        mm = pe.matmul(ps[:, 5 + un % 2, P * hd + t0:P * hd + t0 + 64], gS[:, z, c, hd // 2, hd % 2, :],
                                       qd[:, 2 * z + hd // 2, P * i + t0:P * i + t0 + 64],
                                       start=False, stop=(c == 1), skip_group_check=True)
                    mm.then_inc(*own.one(gi_done))

            pe.wait_ge(row_exp.sem, 3)
            pe.wait_ge(go_taken.sem, len(UNITS))
            for i in range(TILES):
                pe.transpose(ps[:, 6, 64 * i:64 * i + 64], rB[:, tile(i)], ident[0:64, 0:64])
                mm = pe.transpose(ps[:, 5, 64 * i:64 * i + 64], tmp[0:64, tile(i)], ident[0:64, 0:64])
            mm.then_inc(*own.one(wend_turned))
            for i in range(TILES):
                if i >= 2:
                    pe.wait_ge(ktok_ready.sem, i - 1)
                for hd in range(HEADS):
                    mm = pe.transpose(ps[:, i % 2, tile(hd)], mqk[:, HEADS + hd, tile(i)], ident[:, :])
                mm.then_inc(*own.one(ktok_turned))
            pe.wait_ge(mC_zero.sem, 1)
            pe.wait_ge(ktok_ready.sem, TILES)
            pe.wait_ge(wend_ready.sem, 1)
            def row(z, hd):
                return ident[0:64, 32 * z + hd:32 * z + hd + 1].to_broadcast([64, P])

            def ml_weights(un):
                n, z, i = UNITS[un]
                if un >= 1:
                    pe.wait_ge(lw_ready.sem, un)
                    pe.wait_ge(iw_taken.sem, un)
                for hd in range(HEADS):
                    pe.matmul(ps[:, 0, tile(hd)], row(z, hd), rP[:, tile(i)], start=True, stop=False)
                    mm = pe.matmul(ps[:, 0, tile(hd)], rA[:, tile(i)], row(z, hd), start=False, stop=True)
                mm.then_inc(*own.one(ml_lw))
                for hd in range(HEADS):
                    mm = pe.matmul(ps[:, 2, tile(hd)], row(z, hd), rI[:, tile(i)], start=True, stop=True)
                mm.then_inc(*own.one(ml_iw))
                if un >= 1:
                    pe.wait_ge(msc_ready.sem, un)
                for hd in range(HEADS):
                    mm = pe.matmul(ps[:, 1, tile(hd)], mqk[:, HEADS + hd, tile(i)], mqk[:, hd, tile(i)],
                                   start=True, stop=True)
                mm.then_inc(*own.one(ml_sc))
            ml_weights(0)
            for un, (n, z, i) in enumerate(UNITS):
                b = un % 2
                if un + 1 < len(UNITS):
                    ml_weights(un + 1)
                pe.wait_ge(mks_ready.sem, un + 1)
                if un >= 1:
                    pe.wait_ge(mC_ready.sem, un)
                for hd in range(HEADS):
                    c0 = (ML_DH + 1) * (hd % 2)
                    mm = pe.matmul(ps[:, 5 + hd // 2, c0:c0 + ML_DH + 1], mks[:, b, hd, :], mv[:, i, hd, :],
                                   start=True, stop=True)
                mm.then_inc(*own.one(mkv_done))
                pe.wait_ge(mqs_ready.sem, un + 1)
                pe.wait_ge(msc_ready.sem, un + 1)
                if un >= 1:
                    pe.wait_ge(mh_taken.sem, un)
                for hd in range(HEADS):
                    c0 = (ML_DH + 1) * (hd % 2)
                    out = ps[:, 3 + hd // 2, c0:c0 + ML_DH + 1]
                    pe.matmul(out, msc[:, b, hd, :], mv[:, i, hd, :], start=True, stop=False)
                    mm = pe.matmul(out, mqs[:, b, hd, :], mC[:, z, hd, :], start=False, stop=True)
                mm.then_inc(*own.one(mh_done))

            pe.wait_ge(mh_taken.sem, len(UNITS))
            for i in range(TILES):
                if i >= 2:
                    pe.wait_ge(out_ready.sem, i - 1)
                for hd in range(HEADS):
                    mm = pe.transpose(ps[:, i % 2, tile(hd)], ml_t[:, i, hd, :], ident[:, :])
                mm.then_inc(*own.one(out_turned))

            for f in range(KT):
                pe.wait_ge(g_sq.sem, f + 1)
                for i in range(TILES):
                    c0 = 2 * (TILES * f + i)
                    mm = pe.matmul(ps[:, 2, c0:c0 + 2], gsq[:, f % 2, tile(i)], ones[:, 0:2], start=True, stop=True)
                mm.then_inc(*own.one(g_sum))
            pe.wait_ge(g_rt.sem, 1)
            for f in range(KT):
                if f >= 2:
                    pe.wait_ge(g_scaled.sem, f - 1)
                for i in range(TILES):
                    bank = 2 * (f % 2) + (4 if i < N_CTX // P else 3)
                    out = ps[:, bank, tile(i if i < N_CTX // P else i - N_CTX // P)]
                    mm = pe.matmul(out, grt[:, f, i:i + 1].to_broadcast([P, P]), ident[:, :], start=True, stop=True)
                mm.then_inc(*own.one(g_spread))

            def out_projection(q, s0, layer, ready):
                pe.wait_ge(ready.sem, KT)
                for m in range(N_OUT):
                    if m >= 2:
                        pe.wait_ge(q.out_updated.sem, m - 1)
                    features(s0 + m, 0, ps[:, m % 2, :], cx_bank(m) if layer == 0 else None, u)

            def feed_forward(q, n, layer, s_up, s_down, toks):
                def up(b, i):
                    if b >= 2:
                        pe.wait_ge((q.g_taken if b % 2 else q.a_taken).sem, b // 2 + 2 * i)
                    features(s_up + b, i, ps[:, b % 2, :], cx_bank(b) if layer == 0 else None, u,
                             n.lo_ready if b == 0 else None)

                blocks(own.loop, {block_used: 4}, N_UP, up)

                def down(b, i):
                    g, first = b // (FT // 2), b % (FT // 2) == 0
                    end = b % (FT // 2) == FT // 2 - 1
                    pe.wait_ge(lo_ready.sem, s_count(s_down + b, i))
                    for kk in range(2):
                        pe.wait_ge(q.hl_ready.sem, 2 * b + kk + 1 + 8 * i)
                        for mm_ in range(M_GROUP):
                            if first and kk == 0 and g == 1 and mm_ % 2 == 0:
                                pe.wait_ge(q.h_updated.sem, mm_ + 2)
                            if first and kk == 0 and g == 0 and mm_ == 0:
                                pe.wait_ge(q.g_taken.sem, FT)
                            lat = ps[:, mm_, :]
                            cx = ps[:, 4 + mm_ // 2, 256 * (mm_ % 2):256 * (mm_ % 2) + 256]
                            for a, (wp, xp) in enumerate(PASSES):
                                w = wsp[:, (s_down + b) % 2, wp, 512 * kk + P * mm_:512 * kk + P * mm_ + P]
                                one, last = first and kk == 0 and a == 0, end and kk == 1 and a == 2
                                if layer == 0:
                                    pe.matmul(cx, w, hsp[:, kk, xp, CTX], start=(one and mm_ % 2 == 0), stop=last,
                                              skip_group_check=True)
                                mm = pe.matmul(lat, w, hsp[:, kk, xp, LAT], start=one, stop=last,
                                               skip_group_check=True)
                        if kk == 0:
                            mm.then_inc(*own.one(q.hid_used))
                        else:
                            mm.then_inc(*own.one(block_used))

                half = FT // 2
                for g0 in (0, half):
                    down(g0, 0)
                    with own.loop(2, {block_used: 4, q.hid_used: 4}) as i:
                        for b in range(g0 + 1, g0 + 5):
                            down(b, i)
                    for b in range(g0 + 9, g0 + half):
                        down(b, 0)

            out_projection(ffn[0], S_OUT0, 0, g_lo)
            normalise(norm[1], slice(0, N_TOK))
            feed_forward(ffn[0], norm[1], 0, S_UP0, S_DOWN0, slice(0, N_TOK))
            normalise(norm[2], slice(0, N_TOK))

            for n in range(N_QK):
                if n >= 2:
                    pe.wait_ge(qk_taken.sem, n - 1)
                features(S_QK + n, 0, ps[:, n % 2, :], cx_bank(n) if n >= KT else None, u,
                         norm[2].lo_ready if n == 0 else None)
            for cg in range(2):
                taken = [(qk_taken, N_QK)] if cg == 0 else [(nav_act, 3), (nav_dve, 3)]
                for b in range(4):
                    tokens(S_V1 + 4 * cg + b, b, taken)

            pe.wait_ge(nav_act.sem, 6)
            pe.wait_ge(nav_dve.sem, 6)
            N_NA = NA_HEADS * NA_TILES
            for un in range(N_NA + 4):
                if un < N_NA:
                    hd, j = un // NA_TILES, un % NA_TILES
                    rows, m, x = slice(64 * (hd % 2), 64 * (hd % 2) + 64), hd // 2, un % 2
                    if un >= 2:
                        pe.wait_ge(s_ctx.sem, un - 1)
                        pe.wait_ge(neg_max.sem, un - 1)
                    if j < NA_TILES - 1:
                        keys = nak[rows, m, N_CTX + P * j:N_CTX + P * j + 256]
                        parts = [(slice(0, P), slice(64 * (2 * j + 1), 64 * (2 * j + 3)))]
                    else:
                        keys = nak[rows, m, LAT].rearrange("p (i t) -> p i t", t=P)[:, 0::3, :]
                        parts = [(slice(0, 64), slice(448, 512)), (slice(64, P), slice(0, 64))]
                    for out_rows, cols in parts:
                        pe.matmul(ps[out_rows, x, 0:256], naq[rows, m, cols], keys, start=True, stop=True)
                        mm = pe.matmul(ps[out_rows, 6 + x, 0:256], naq[rows, m, cols], nak[rows, m, CTX],
                                       start=True, stop=True)
                    mm.then_inc(*own.one(s_done))
                if 3 <= un <= N_NA + 2:
                    e = un - 3
                    pe.wait_ge(p_ready.sem, e + 1)
                    if e >= 2:
                        pe.wait_ge(pt_ready.sem, e - 1)
                    for c in range(4):
                        mm = pe.transpose(ps[:, 2 + e % 2, tile(c)], nas[:, e % 4, tile(c)], ident[:, :])
                    mm.then_inc(*own.one(p_turned))
                if un >= 4:
                    e = un - 4
                    hd, j = e // NA_TILES, e % NA_TILES
                    m = hd // 2
                    pe.wait_ge(pt_ready.sem, e + 1)
                    if m >= 2 and hd % 2 == 0 and j == 0:
                        pe.wait_ge(y_taken.sem, m - 1)
                    keys = (2 + j, 3 + j, 0, 1) if j < NA_TILES - 1 else (2, 5, 0, 1)
                    for c, t in enumerate(keys):
                        mm = pe.matmul(ps[64 * (hd % 2):64 * (hd % 2) + 64, 4 + m % 2, tile(j)],
                                       nav[:, t, NA_DH * hd:NA_DH * hd + NA_DH], nap[:, e % 2, c, :],
                                       start=(c == 0), stop=(c == 3))
                    mm.then_inc(*own.one(o_done))

            out_projection(ffn[1], S_OUT1, 1, y_lo)
            normalise(norm[3], LAT)
            feed_forward(ffn[1], norm[3], 1, S_UP1, S_DOWN1, LAT)
            normalise(norm[4], LAT)


def rope_table():
    pos = np.arange(N_LAT)
    row, col = (pos // GRID_W).astype(np.float32), (pos % GRID_W).astype(np.float32)
    out = np.zeros((P, 4, N_LAT), np.float32)
    for a, dh in enumerate((GLA_DK, ML_DH)):
        n = dh // 4
        inv = (np.float32(10000.0) ** (-np.arange(n, dtype=np.float32) / np.float32(n))).astype(np.float32)
        ang = np.concatenate([row[:, None] * inv, col[:, None] * inv], axis=-1).astype(np.float32)
        d = np.arange(P) % dh
        sign = np.where(d < dh // 2, -1.0, 1.0).astype(np.float32)
        out[:, 2 * a] = np.cos(ang).T[d % (dh // 2)]
        out[:, 2 * a + 1] = sign[:, None] * np.sin(ang).T[d % (dh // 2)]
    return out


def reset_table():
    t = np.arange(N_TOK + 1)
    out = np.stack([(t % GLA_CHUNK != 0), (t % P != 0)]).astype(np.float32)
    return np.broadcast_to(out, (P, 2, N_TOK + 1)).copy()


def packed_constants():
    out = np.zeros((P, 6 * P), np.float32)
    out[:, 0:P] = np.eye(P)
    for z in range(2):
        for hd in range(HEADS):
            out[64 + 4 * z + hd, P + 32 * z + hd] = 1.0
            out[96 + 4 * z + hd, P + 64 + 32 * z + hd] = 1.0
    s, t = np.arange(P)[:, None], np.arange(P)[None, :]
    for z in range(2):
        order = (s <= t) if z == 0 else (s >= t)
        out[:, (2 + z) * P:(3 + z) * P] = order & (s // GLA_CHUNK == t // GLA_CHUNK)
        out[:, (4 + z) * P:(5 + z) * P] = np.where(order, 0.0, NEG)
    return out


def bias_places():
    g8 = lambda g: [(r, 8 * g + c) for r in range(GRID_H) for c in range(8)]
    out = np.zeros((NA_TILES, P, 256), np.int64)
    pad = (2 * 8 - 1) * (2 * NA_WIN_W - 1)
    for j in range(NA_TILES):
        qs = [(2 * j + 1) % 8, (2 * j + 2) % 8]
        ks = range(2 * j, 2 * j + 4) if j < NA_TILES - 1 else (0, 1, 6, 7)
        q = np.array([x for g in qs for x in g8(g)])
        k = np.array([x for g in ks for x in g8(g)])
        start = np.clip(q[:, 1] - NA_WIN_W // 2, 0, GRID_W - NA_WIN_W)
        dr = k[None, :, 0] - q[:, None, 0] + 7
        dc = k[None, :, 1] - q[:, None, 1] + NA_WIN_W - 1
        inside = (k[None, :, 1] >= start[:, None]) & (k[None, :, 1] < start[:, None] + NA_WIN_W)
        out[j] = np.where(inside, dr * (2 * NA_WIN_W - 1) + np.clip(dc, 0, 2 * NA_WIN_W - 2), pad)
    return out


def column_blocks(w):
    m = w.shape[1] // P
    return w.reshape(KT, P, m, P).transpose(2, 1, 0, 3).reshape(m, P, BLOCK)


def row_blocks(w):
    k = w.shape[0] // P
    return w.reshape(k // 2, 2, P, 2, 512).transpose(3, 0, 2, 1, 4).reshape(k, P, BLOCK)


def kernel(**inputs):
    import concourse.bacc as bacc
    from concourse.bass_utils import run_bass_kernel_spmd

    g = {k: np.asarray(v) for k, v in inputs.items()}
    tokens = np.concatenate([g["ctx"][0], g["x"][0]], axis=0)
    xT = tokens.T.reshape(KT, P, N_TOK).transpose(1, 0, 2)

    win = g["ev_w_in"][0]
    sizes = (256, 256, 512, 512, 32, 512, 512, 512, 512, 16)
    at = np.concatenate([[0], np.cumsum(sizes)])
    gq, gk, gv, gg, ga, mq, mk, mv, mo, mg = (win[:, a:b] for a, b in zip(at[:-1], at[1:]))
    mg = mg.reshape(D, 2, 2, HEADS)
    gate_cols = np.zeros((D, P), win.dtype)
    for z in range(2):
        gate_cols[:, 32 * z:32 * z + 16] = ga[:, 16 * z:16 * z + 16]
        gate_cols[:, 64 + 4 * z:68 + 4 * z] = mg[:, z, 0]
        gate_cols[:, 96 + 4 * z:100 + 4 * z] = mg[:, z, 1]
    stream = [column_blocks(x) for x in (gate_cols, gq, gk, mq, mk, gg, mo)]
    stream += [row_blocks(np.concatenate([gv, mv], axis=1)), column_blocks(g["ev_w_out"][0])]

    def up(w):
        a, b = column_blocks(w[:, :D_FF]), column_blocks(w[:, D_FF:])
        return np.stack([a, b], axis=1).reshape(2 * FT, P, BLOCK)

    qkv = g["na_w_qkv"][0]
    stream += [up(g["ffn_w_up"][0]), row_blocks(g["ffn_w_down"][0])]
    stream += [column_blocks(qkv[:, :2 * D]), row_blocks(qkv[:, 2 * D:]), column_blocks(g["na_w_out"][0])]
    stream += [up(g["ffn_w_up"][1]), row_blocks(g["ffn_w_down"][1])]
    stream = np.concatenate(stream, axis=0)
    mods = np.concatenate([g["mod_w"][l].T.reshape(-1, P, D) for l in range(2)], axis=0)
    mixed = np.stack([stream[:S_MIX], mods[MOD_FIRST:]], axis=1).reshape(-1, P, BLOCK)
    weights = np.concatenate([mods[:MOD_FIRST], mixed, stream[S_MIX:]], axis=0)

    by_part = lambda v: v.reshape(-1, P).T
    vecs = np.zeros((P, V_N), np.float32)
    for l in range(2):
        vecs[:, V_NMIX + KT * l:V_NMIX + KT * l + KT] = by_part(g["norm_mix_w"][l])
        vecs[:, V_NFFN + KT * l:V_NFFN + KT * l + KT] = by_part(g["norm_ffn_w"][l])
        vecs[:, V_MODB + 48 * l:V_MODB + 48 * l + 48] = by_part(g["mod_b"][l])
        cv = np.stack([by_part(g["ffn_conv_w"][l, t]) for t in range(3)] + [by_part(g["ffn_conv_b"][l])], axis=2)
        vecs[:, V_CONV + 4 * FT * l:V_CONV + 4 * FT * l + 4 * FT] = cv.reshape(P, 4 * FT)
    vecs[:, V_NFIN:V_NFIN + KT] = by_part(g["final_norm_w"])
    vecs[:, V_GLAN] = g["gla_norm_w"][0]
    vecs[:, V_MLN] = g["ml_norm_w"][0]
    vecs[:, V_ABIAS:V_ABIAS + 4] = by_part(g["gla_a_bias"][0].reshape(-1))
    for z in range(2):
        vecs[32 * z:32 * z + HEADS, V_GATEB:V_GATEB + 2] = g["ml_gate_bias"][0, z].T
    c_rows = np.broadcast_to(np.stack([g["c"][0], g["c_ctx"]]), (P, 2, D))
    a_up = np.zeros((P, 2, 256), np.float32)
    for z in range(2):
        a_up[32 * z:32 * z + 16, z] = g["gla_a_up"][0, z]
    rpb = g["na_rpb"][0].reshape(NA_HEADS, -1)
    rpb = np.concatenate([rpb, np.full((NA_HEADS, 1), NEG, rpb.dtype)], axis=1)
    na_bias = rpb[:, bias_places()].transpose(0, 2, 1, 3)

    arrays = {"in_x": xT, "in_vecs": vecs, "in_consts": packed_constants(), "in_rope": rope_table(),
              "in_reset": reset_table(), "in_aup": a_up, "in_nabias": na_bias, "in_crows": c_rows, "in_weights": weights}
    arrays = {k: np.ascontiguousarray(v) for k, v in arrays.items()}
    nc = bacc.Bacc("TRN2", target_bir_lowering=False, num_devices=1)
    aps = [nc.dram_tensor(k, a.shape, mybir.dt.from_np(a.dtype), kind="ExternalInput").ap() for k, a in arrays.items()]
    out = nc.dram_tensor("out_0", (P, KT, N_LAT), F32, kind="ExternalOutput").ap()
    build(nc, *aps, out)
    r = run_bass_kernel_spmd(nc, [arrays], core_ids=[0])
    y = r.results[0]["out_0"]
    return y.transpose(1, 0, 2).reshape(D, N_LAT).T.reshape(1, N_LAT, D)
```
